# Optimizing a Trainium2 kernel written in Bass

```python
import jax, jax.numpy as jnp
from jax import lax
import numpy as np
import math

D_MODEL = 1024
BATCH = 1
SEQ = 256
DEPTH = 2

GRID_W = 64
NA_HEADS = 8
NA_HEAD_DIM = 64
NA_WIN_R = 8
NA_WIN_C = 16
NA_W = NA_HEADS * NA_HEAD_DIM
MLA_HEADS = 4
MLA_Q_RANK = 384
MLA_KV_RANK = 256
MLA_NOPE = 128
MLA_ROPE = 64
MLA_V = 128
MLA_QK = MLA_NOPE + MLA_ROPE
MLA_W = MLA_HEADS * MLA_V
GQA_HEADS = 8
GQA_KV_HEADS = 2
GQA_HEAD_DIM = 64
GQA_WINDOW = 128
GQA_Q_W = GQA_HEADS * GQA_HEAD_DIM
GQA_KV_W = GQA_KV_HEADS * GQA_HEAD_DIM
BLOCK = 128
N_BRANCH = 3
D_FF = 2816
CONV_W = 3
ROPE_THETA = 10000.0
EPS = 1e-6
NEG_INF = -1e30
IN_SPLITS = (3 * NA_W, MLA_Q_RANK, MLA_KV_RANK, MLA_ROPE, GQA_Q_W, 2 * GQA_KV_W, N_BRANCH * D_MODEL)
IN_W = 3 * NA_W + MLA_Q_RANK + MLA_KV_RANK + MLA_ROPE + GQA_Q_W + 2 * GQA_KV_W + N_BRANCH * D_MODEL


def rmsnorm(x, g):
    xf = x.astype(jnp.float32)
    y = xf * lax.rsqrt(jnp.mean(xf * xf, axis=-1, keepdims=True) + EPS)
    return (y * g.astype(jnp.float32)).astype(x.dtype)

def rope_tables(seq, dim):
    inv = 1.0 / (ROPE_THETA ** (jnp.arange(0, dim, 2, dtype=jnp.float32) / dim))
    ang = jnp.arange(seq, dtype=jnp.float32)[:, None] * inv[None, :]
    return jnp.cos(ang), jnp.sin(ang)

def apply_rope(x, cos, sin):
    x1, x2 = jnp.split(x, 2, axis=-1)
    c = cos[None, :, None, :].astype(x.dtype)
    s = sin[None, :, None, :].astype(x.dtype)
    return jnp.concatenate([x1 * c - x2 * s, x1 * s + x2 * c], axis=-1)

def neighbourhood_attention(q, k, v, rpb):
    B, S, H, hd = q.shape
    rows = S // GRID_W
    win_r = min(NA_WIN_R, rows)
    qg = q.reshape(B, rows, GRID_W, H, hd)
    kg = k.reshape(B, rows, GRID_W, H, hd)
    vg = v.reshape(B, rows, GRID_W, H, hd)
    col_q = jnp.arange(GRID_W)
    col_start = jnp.clip(col_q - NA_WIN_C // 2, 0, GRID_W - NA_WIN_C)
    col_idx = col_start[:, None] + jnp.arange(NA_WIN_C)[None, :]
    col_bias_idx = col_idx - col_q[:, None] + (NA_WIN_C - 1)
    scale = hd ** -0.5

    def one_row(r):
        r_start = jnp.clip(r - NA_WIN_R // 2, 0, rows - win_r)
        q_r = lax.dynamic_index_in_dim(qg, r, axis=1, keepdims=False)
        k_rows = lax.dynamic_slice_in_dim(kg, r_start, win_r, axis=1)
        v_rows = lax.dynamic_slice_in_dim(vg, r_start, win_r, axis=1)
        k_win = k_rows[:, :, col_idx]
        v_win = v_rows[:, :, col_idx]
        s = jnp.einsum('bqhd,brqchd->bhqrc', q_r, k_win,
                       preferred_element_type=jnp.float32) * scale
        row_bias_idx = r_start + jnp.arange(win_r) - r + (NA_WIN_R - 1)
        bias = rpb[:, row_bias_idx[None, :, None], col_bias_idx[:, None, :]]
        s = s + bias[None].astype(jnp.float32)
        p = jax.nn.softmax(s.reshape(B, H, GRID_W, win_r * NA_WIN_C), axis=-1)
        p = p.reshape(B, H, GRID_W, win_r, NA_WIN_C).astype(v.dtype)
        return jnp.einsum('bhqrc,brqchd->bqhd', p, v_win)

    out = lax.map(one_row, jnp.arange(rows))
    return out.transpose(1, 0, 2, 3, 4).reshape(B, S, H * hd)

def mla_attention(c_q, c_kv, k_rope, g_qa, g_kva, w_uq, w_ukv, cos, sin):
    B, S, _ = c_q.shape
    H = MLA_HEADS
    q = (rmsnorm(c_q, g_qa) @ w_uq).reshape(B, S, H, MLA_QK)
    q_nope = q[..., :MLA_NOPE]
    q_pe = apply_rope(q[..., MLA_NOPE:], cos, sin)
    kv = (rmsnorm(c_kv, g_kva) @ w_ukv).reshape(B, S, H, MLA_NOPE + MLA_V)
    k_nope = kv[..., :MLA_NOPE]
    v = kv[..., MLA_NOPE:]
    k_pe = apply_rope(k_rope[:, :, None, :], cos, sin)[:, :, 0, :]
    scale = MLA_QK ** -0.5
    nb = S // BLOCK
    qn_b = q_nope.reshape(B, nb, BLOCK, H, MLA_NOPE).transpose(1, 0, 2, 3, 4)
    qp_b = q_pe.reshape(B, nb, BLOCK, H, MLA_ROPE).transpose(1, 0, 2, 3, 4)

    def one_block(args):
        qn, qp = args
        s = (jnp.einsum('bqhd,bkhd->bhqk', qn, k_nope, preferred_element_type=jnp.float32)
             + jnp.einsum('bqhr,bkr->bhqk', qp, k_pe, preferred_element_type=jnp.float32)) * scale
        p = jax.nn.softmax(s, axis=-1).astype(v.dtype)
        return jnp.einsum('bhqk,bkhd->bqhd', p, v)

    o = lax.map(one_block, (qn_b, qp_b))
    return o.transpose(1, 0, 2, 3, 4).reshape(B, S, H * MLA_V)

def window_gqa_sink(q, k, v, sink, cos, sin):
    B, S, H, hd = q.shape
    KVH = k.shape[2]
    G = H // KVH
    q = apply_rope(q, cos, sin)
    k = apply_rope(k, cos, sin)
    nb = S // BLOCK
    qb = q.reshape(B, nb, BLOCK, KVH, G, hd)
    pad = ((0, 0), (BLOCK, BLOCK), (0, 0), (0, 0))
    kp = jnp.pad(k, pad).reshape(B, nb + 2, BLOCK, KVH, hd)
    vp = jnp.pad(v, pad).reshape(B, nb + 2, BLOCK, KVH, hd)
    kw = jnp.concatenate([kp[:, :-2], kp[:, 1:-1], kp[:, 2:]], axis=2)
    vw = jnp.concatenate([vp[:, :-2], vp[:, 1:-1], vp[:, 2:]], axis=2)
    scale = hd ** -0.5
    s = jnp.einsum('bnqkgd,bnjkd->bnkgqj', qb, kw,
                   preferred_element_type=jnp.float32) * scale
    blk = jnp.arange(nb)
    qpos = blk[:, None] * BLOCK + jnp.arange(BLOCK)[None, :]
    kpos = (blk[:, None] - 1) * BLOCK + jnp.arange(3 * BLOCK)[None, :]
    valid = ((kpos[:, None, :] >= 0) & (kpos[:, None, :] < S)
             & (jnp.abs(qpos[:, :, None] - kpos[:, None, :]) <= GQA_WINDOW))
    s = jnp.where(valid[None, :, None, None], s, NEG_INF)
    sink_b = jnp.broadcast_to(sink.astype(jnp.float32).reshape(KVH, G)[None, None, :, :, None, None],
                              s.shape[:-1] + (1,))
    p = jax.nn.softmax(jnp.concatenate([s, sink_b], axis=-1), axis=-1)[..., :-1]
    o = jnp.einsum('bnkgqj,bnjkd->bnqkgd', p.astype(v.dtype), vw)
    return o.reshape(B, S, H * hd)

def gated_parallel_mixer(h, w_in, b_gate, na_rpb, mla_qa_g, mla_kva_g, mla_w_uq, mla_w_ukv,
                         gqa_sink, w_br_na, w_br_mla, w_br_gqa, w_out, cos_mla, sin_mla, cos_gqa, sin_gqa):
    B, S, _ = h.shape
    z = h @ w_in
    offs = np.cumsum(IN_SPLITS)[:-1].tolist()
    z_na, c_q, c_kv, k_rope, z_gq, z_gkv, z_gate = jnp.split(z, offs, axis=-1)
    na_qkv = z_na.reshape(B, S, 3, NA_HEADS, NA_HEAD_DIM)
    y_na = neighbourhood_attention(na_qkv[:, :, 0], na_qkv[:, :, 1], na_qkv[:, :, 2], na_rpb)
    y_mla = mla_attention(c_q, c_kv, k_rope, mla_qa_g, mla_kva_g, mla_w_uq, mla_w_ukv, cos_mla, sin_mla)
    gkv = z_gkv.reshape(B, S, 2, GQA_KV_HEADS, GQA_HEAD_DIM)
    y_gqa = window_gqa_sink(z_gq.reshape(B, S, GQA_HEADS, GQA_HEAD_DIM), gkv[:, :, 0], gkv[:, :, 1],
                            gqa_sink, cos_gqa, sin_gqa)
    gates = jax.nn.sigmoid(z_gate + b_gate).reshape(B, S, N_BRANCH, D_MODEL)
    merged = (gates[:, :, 0] * (y_na @ w_br_na)
              + gates[:, :, 1] * (y_mla @ w_br_mla)
              + gates[:, :, 2] * (y_gqa @ w_br_gqa))
    return merged @ w_out

def conv_ffn(h, w_up, conv_w, conv_b, w_down):
    u = h @ w_up
    C = u.shape[-1]
    u = lax.conv_general_dilated(u, conv_w[:, None, :].astype(u.dtype), window_strides=(1,),
                                 padding=((CONV_W // 2, CONV_W // 2),),
                                 dimension_numbers=('NWC', 'WIO', 'NWC'),
                                 feature_group_count=C) + conv_b
    a, g = jnp.split(u, 2, axis=-1)
    return (jax.nn.gelu(g) * a) @ w_down

def first_inputs(seed: int = 0) -> dict:
    key = jax.random.key(seed)
    ks = jax.random.split(key, 24)
    f32 = jnp.float32

    def nrm(k, shape, scale):
        return jax.random.normal(k, shape, f32) * scale

    L = DEPTH
    return {
        "x": nrm(ks[0], (BATCH, SEQ, D_MODEL), 1.0),
        "norm1_g": 1.0 + nrm(ks[1], (L, D_MODEL), 0.05),
        "w_in": nrm(ks[2], (L, D_MODEL, IN_W), D_MODEL ** -0.5),
        "b_gate": nrm(ks[3], (L, N_BRANCH * D_MODEL), 0.02),
        "na_rpb": nrm(ks[4], (L, NA_HEADS, 2 * NA_WIN_R - 1, 2 * NA_WIN_C - 1), 0.1),
        "mla_qa_g": 1.0 + nrm(ks[5], (L, MLA_Q_RANK), 0.05),
        "mla_kva_g": 1.0 + nrm(ks[6], (L, MLA_KV_RANK), 0.05),
        "mla_w_uq": nrm(ks[7], (L, MLA_Q_RANK, MLA_HEADS * MLA_QK), MLA_Q_RANK ** -0.5),
        "mla_w_ukv": nrm(ks[8], (L, MLA_KV_RANK, MLA_HEADS * (MLA_NOPE + MLA_V)), MLA_KV_RANK ** -0.5),
        "gqa_sink": nrm(ks[9], (L, GQA_HEADS), 0.5),
        "w_br_na": nrm(ks[10], (L, NA_W, D_MODEL), NA_W ** -0.5),
        "w_br_mla": nrm(ks[11], (L, MLA_W, D_MODEL), MLA_W ** -0.5),
        "w_br_gqa": nrm(ks[12], (L, GQA_Q_W, D_MODEL), GQA_Q_W ** -0.5),
        "w_out": nrm(ks[13], (L, D_MODEL, D_MODEL), D_MODEL ** -0.5),
        "norm2_g": 1.0 + nrm(ks[14], (L, D_MODEL), 0.05),
        "w_up": nrm(ks[15], (L, D_MODEL, 2 * D_FF), D_MODEL ** -0.5),
        "conv_w": nrm(ks[16], (L, CONV_W, 2 * D_FF), CONV_W ** -0.5),
        "conv_b": nrm(ks[17], (L, 2 * D_FF), 0.02),
        "w_down": nrm(ks[18], (L, D_FF, D_MODEL), D_FF ** -0.5),
        "final_g": 1.0 + nrm(ks[19], (D_MODEL,), 0.05),
    }

def first_block(x, norm1_g, w_in, b_gate, na_rpb, mla_qa_g, mla_kva_g, mla_w_uq, mla_w_ukv,
              gqa_sink, w_br_na, w_br_mla, w_br_gqa, w_out, norm2_g, w_up, conv_w, conv_b,
              w_down, final_g):
    S = x.shape[1]
    cos_mla, sin_mla = rope_tables(S, MLA_ROPE)
    cos_gqa, sin_gqa = rope_tables(S, GQA_HEAD_DIM)
    for l in range(DEPTH):
        h = rmsnorm(x, norm1_g[l])
        x = x + gated_parallel_mixer(h, w_in[l], b_gate[l], na_rpb[l], mla_qa_g[l], mla_kva_g[l],
                                     mla_w_uq[l], mla_w_ukv[l], gqa_sink[l], w_br_na[l], w_br_mla[l],
                                     w_br_gqa[l], w_out[l], cos_mla, sin_mla, cos_gqa, sin_gqa)
        h = rmsnorm(x, norm2_g[l])
        x = x + conv_ffn(h, w_up[l], conv_w[l], conv_b[l], w_down[l])
    return rmsnorm(x, final_g)


DEEPNORM_ALPHA = (2 * DEPTH) ** 0.25
DEEPNORM_BETA = (8 * DEPTH) ** -0.25
LN_EPS = 1e-5
ROPE_THETA_2 = 500000.0
ROPE_FRACTION = 4
RWKV_HEAD_DIM = 64
RWKV_DIM = D_MODEL // 2
RWKV_HEADS = RWKV_DIM // RWKV_HEAD_DIM
DECAY_LORA = max(32, int(round(1.8 * D_MODEL ** 0.5 / 32)) * 32)
ICLR_LORA = max(32, int(round(1.8 * D_MODEL ** 0.5 / 32)) * 32)
GATE_LORA = max(32, int(round(0.6 * D_MODEL ** 0.8 / 32)) * 32)
RWKV_GN_EPS = 64e-5
RWKV_PROJ_COLS = 3 * RWKV_DIM + DECAY_LORA + ICLR_LORA + GATE_LORA
MOBA_HEAD_DIM = 128
MOBA_WIDTH = D_MODEL - RWKV_DIM
MOBA_HEADS = MOBA_WIDTH // MOBA_HEAD_DIM
MOBA_BLOCK = 256
MOBA_TOPK = 3
MOBA_Q_CHUNK = 16
AB_IN_COLS = RWKV_PROJ_COLS + 3 * MOBA_WIDTH
AB_OUT_COLS = RWKV_DIM + MOBA_WIDTH
DIL_PAIRS = ((128, 1), (512, 4), (2048, 16))
DIL_GROUPS = len(DIL_PAIRS)
DIL_HEAD_DIM = 128
DIL_HEADS = D_MODEL // DIL_HEAD_DIM
C_WIDTH = DIL_HEADS * DIL_HEAD_DIM
C_IN_COLS = DIL_GROUPS * C_WIDTH + 2 * C_WIDTH
MLP_HIDDEN = 4 * D_MODEL
NEG_INF_2 = -1e30


def _layer_norm(x, g, b):
    xf = x.astype(jnp.float32)
    mu = jnp.mean(xf, -1, keepdims=True)
    var = jnp.mean(jnp.square(xf - mu), -1, keepdims=True)
    return ((xf - mu) * lax.rsqrt(var + LN_EPS) * g + b).astype(x.dtype)

def _partial_rotary(x, pos):
    rot = x.shape[-1] // ROPE_FRACTION
    half = rot // 2
    inv_freq = ROPE_THETA_2 ** (-jnp.arange(half, dtype=jnp.float32) / half)
    ang = pos.astype(jnp.float32)[:, None] * inv_freq[None, :]
    cos = jnp.cos(ang).astype(x.dtype)
    sin = jnp.sin(ang).astype(x.dtype)
    x1, x2, rest = x[..., :half], x[..., half:rot], x[..., rot:]
    return jnp.concatenate([x1 * cos - x2 * sin, x2 * cos + x1 * sin, rest], axis=-1)

def _token_shift(z):
    return jnp.pad(z, ((0, 0), (1, 0), (0, 0)))[:, :-1]

def _rwkv7_time_mix(z, shift_mix, w0, w_up, a0, a_up, g_up, k_k, k_a, r_k, lnx_g, lnx_b):
    B, T, _ = z.shape
    H, N = RWKV_HEADS, RWKV_HEAD_DIM
    f32 = jnp.float32
    z = z + (_token_shift(z) - z) * shift_mix
    o1, o2, o3 = RWKV_DIM, 2 * RWKV_DIM, 3 * RWKV_DIM
    o4 = o3 + DECAY_LORA
    o5 = o4 + ICLR_LORA
    r, k, v = z[..., :o1], z[..., o1:o2], z[..., o2:o3]
    w_d, a_d, g_d = z[..., o3:o4], z[..., o4:o5], z[..., o5:]
    w = -jax.nn.softplus(-(w0 + jnp.tanh(w_d) @ w_up)) - 0.5
    decay = jnp.exp(-jnp.exp(w.astype(f32)))
    a = jax.nn.sigmoid(a0 + a_d @ a_up).astype(f32)
    g = jax.nn.sigmoid(g_d) @ g_up
    heads = lambda t: t.astype(f32).reshape(B, T, H, N)
    kk = heads(k * k_k)
    kk = kk / jnp.maximum(jnp.linalg.norm(kk, axis=-1, keepdims=True), 1e-12)
    k = k.astype(f32) * (1.0 + (a - 1.0) * k_a)
    r, k, v, a, decay = heads(r), heads(k), heads(v), heads(a), heads(decay)

    def step(S, inp):
        r_t, w_t, k_t, v_t, a_t, b_t = inp
        sa = jnp.einsum('bhvk,bhk->bhv', S, a_t)
        S = S * w_t[:, :, None, :] + sa[..., None] * b_t[:, :, None, :] + v_t[..., None] * k_t[:, :, None, :]
        return S, jnp.einsum('bhvk,bhk->bhv', S, r_t)

    seq_first = lambda t: jnp.moveaxis(t, 1, 0)
    xs = (seq_first(r), seq_first(decay), seq_first(k), seq_first(v), seq_first(-kk), seq_first(kk * a))
    _, y = lax.scan(step, jnp.zeros((B, H, N, N), f32), xs)
    y = jnp.moveaxis(y, 0, 1)
    mu = jnp.mean(y, -1, keepdims=True)
    var = jnp.mean(jnp.square(y - mu), -1, keepdims=True)
    y = ((y - mu) * lax.rsqrt(var + RWKV_GN_EPS)).reshape(B, T, RWKV_DIM) * lnx_g + lnx_b
    bonus = jnp.sum(r * k * r_k, -1, keepdims=True) * v
    y = y + bonus.reshape(B, T, RWKV_DIM)
    return y * g

def _moba_attention(q, k, v):
    B, H, T, Dh = q.shape
    f32 = jnp.float32
    nb = -(-T // MOBA_BLOCK)
    Tp = nb * MOBA_BLOCK
    pad = ((0, 0), (0, 0), (0, Tp - T), (0, 0))
    q, k, v = jnp.pad(q, pad), jnp.pad(k, pad), jnp.pad(v, pad)
    scale = Dh ** -0.5
    kb = k.reshape(B, H, nb, MOBA_BLOCK, Dh)
    vb = v.reshape(B, H, nb, MOBA_BLOCK, Dh)
    n_sel = min(MOBA_TOPK, nb - 1)
    sel = None
    if n_sel > 0:
        k_mean = jnp.mean(kb.astype(f32), axis=3)
        gate = jnp.einsum('bhtd,bhnd->bhtn', q.astype(f32), k_mean)
        q_blk = jnp.arange(Tp) // MOBA_BLOCK
        past = jnp.arange(nb)[None, :] < q_blk[:, None]
        gate = jnp.where(past, gate, NEG_INF_2)
        _, sel = lax.top_k(gate, n_sel)
    bi = jnp.arange(B)[:, None, None, None]
    hi = jnp.arange(H)[None, :, None, None]

    def chunk(c):
        t0 = c * MOBA_Q_CHUNK
        i = t0 // MOBA_BLOCK
        qc = lax.dynamic_slice_in_dim(q, t0, MOBA_Q_CHUNK, axis=2)
        k_own = lax.dynamic_slice_in_dim(k, i * MOBA_BLOCK, MOBA_BLOCK, axis=2)
        v_own = lax.dynamic_slice_in_dim(v, i * MOBA_BLOCK, MOBA_BLOCK, axis=2)
        s_own = jnp.einsum('bhqd,bhkd->bhqk', qc, k_own).astype(f32) * scale
        causal = (i * MOBA_BLOCK + jnp.arange(MOBA_BLOCK))[None, :] <= (t0 + jnp.arange(MOBA_Q_CHUNK))[:, None]
        s_own = jnp.where(causal, s_own, NEG_INF_2)
        if n_sel == 0:
            p = jax.nn.softmax(s_own, axis=-1).astype(v.dtype)
            return jnp.einsum('bhqk,bhkd->bhqd', p, v_own)
        idx = lax.dynamic_slice_in_dim(sel, t0, MOBA_Q_CHUNK, axis=2)
        k_sel = kb[bi, hi, idx]
        v_sel = vb[bi, hi, idx]
        s_sel = jnp.einsum('bhqd,bhqskd->bhqsk', qc, k_sel).astype(f32) * scale
        valid = jnp.arange(n_sel) < i
        s_sel = jnp.where(valid[:, None], s_sel, NEG_INF_2)
        n_k = n_sel * MOBA_BLOCK
        s_all = jnp.concatenate([s_sel.reshape(B, H, MOBA_Q_CHUNK, n_k), s_own], axis=-1)
        p = jax.nn.softmax(s_all, axis=-1).astype(v.dtype)
        p_sel = p[..., :n_k].reshape(B, H, MOBA_Q_CHUNK, n_sel, MOBA_BLOCK)
        return (jnp.einsum('bhqsk,bhqskd->bhqd', p_sel, v_sel)
                + jnp.einsum('bhqk,bhkd->bhqd', p[..., n_k:], v_own))

    out = lax.map(chunk, jnp.arange(Tp // MOBA_Q_CHUNK))
    out = jnp.moveaxis(out, 0, 2).reshape(B, H, Tp, Dh)
    return out[:, :, :T]

def _dilated_window_branch(q, k, v, span, dilation):
    B, H, T, Dh = q.shape
    f32 = jnp.float32
    L = T // dilation
    W = span // dilation
    nblk = -(-L // W)
    Lp = nblk * W

    def strided(t):
        t = t.reshape(B, H, L, dilation, Dh).transpose(0, 1, 3, 2, 4)
        return jnp.pad(t, ((0, 0), (0, 0), (0, 0), (0, Lp - L), (0, 0)))

    qb = strided(q).reshape(B, H, dilation, nblk, W, Dh)
    kb = strided(k).reshape(B, H, dilation, nblk, W, Dh)
    vb = strided(v).reshape(B, H, dilation, nblk, W, Dh)
    prev = lambda t: jnp.pad(t, ((0, 0), (0, 0), (0, 0), (1, 0), (0, 0), (0, 0)))[:, :, :, :-1]
    k_band = jnp.concatenate([prev(kb), kb], axis=4)
    v_band = jnp.concatenate([prev(vb), vb], axis=4)
    s = jnp.einsum('bhrnqd,bhrnkd->bhrnqk', qb, k_band).astype(f32) * (Dh ** -0.5)
    qi = jnp.arange(W)[:, None]
    kj = jnp.arange(2 * W)[None, :]
    dist = W + qi - kj
    blk = jnp.arange(nblk)[:, None, None]
    mask = (dist >= 0) & (dist <= W) & ((blk > 0) | (kj >= W))
    s = jnp.where(mask, s, NEG_INF_2)
    lse = jax.nn.logsumexp(s, axis=-1)
    p = jnp.exp(s - lse[..., None]).astype(v.dtype)
    o = jnp.einsum('bhrnqk,bhrnkd->bhrnqd', p, v_band)
    o = o.reshape(B, H, dilation, Lp, Dh)[:, :, :, :L].transpose(0, 1, 3, 2, 4).reshape(B, H, T, Dh)
    lse = lse.reshape(B, H, dilation, Lp)[..., :L].transpose(0, 1, 3, 2).reshape(B, H, T)
    return o, lse

def _rwkv_moba_mixer(x, w_in, shift_mix, w0, w_up, a0, a_up, g_up, k_k, k_a, r_k, lnx_g, lnx_b, w_out, pos):
    B, T, _ = x.shape
    z = x @ w_in
    y_a = _rwkv7_time_mix(z[..., :RWKV_PROJ_COLS], shift_mix, w0, w_up, a0, a_up, g_up,
                          k_k, k_a, r_k, lnx_g, lnx_b)
    qkv = z[..., RWKV_PROJ_COLS:].reshape(B, T, 3, MOBA_HEADS, MOBA_HEAD_DIM).transpose(2, 0, 3, 1, 4)
    q = _partial_rotary(qkv[0], pos)
    k = _partial_rotary(qkv[1], pos)
    y_b = _moba_attention(q, k, qkv[2]).transpose(0, 2, 1, 3).reshape(B, T, MOBA_WIDTH)
    y = jnp.concatenate([y_a.astype(x.dtype), y_b.astype(x.dtype)], axis=-1)
    return (y @ w_out).astype(x.dtype)

def _dilated_mixer(x, w_in, w_out, pos):
    B, T, _ = x.shape
    z = x @ w_in
    nq = DIL_GROUPS * C_WIDTH
    q = z[..., :nq].reshape(B, T, DIL_GROUPS, DIL_HEADS, DIL_HEAD_DIM).transpose(0, 2, 3, 1, 4)
    kv = z[..., nq:].reshape(B, T, 2, DIL_HEADS, DIL_HEAD_DIM).transpose(2, 0, 3, 1, 4)
    q = _partial_rotary(q, pos)
    k = _partial_rotary(kv[0], pos)
    v = kv[1]
    outs, lses = [], []
    for g, (span, dilation) in enumerate(DIL_PAIRS):
        o, l = _dilated_window_branch(q[:, g], k, v, span, dilation)
        outs.append(o)
        lses.append(l)
    wts = jax.nn.softmax(jnp.stack(lses, axis=0), axis=0).astype(v.dtype)
    o = jnp.einsum('gbht,gbhtd->bhtd', wts, jnp.stack(outs, axis=0))
    o = o.transpose(0, 2, 1, 3).reshape(B, T, C_WIDTH)
    return (o @ w_out).astype(x.dtype)

def _sq_relu_mlp(x, w1, w2):
    return jnp.square(jax.nn.relu(x @ w1)) @ w2

def second_inputs(seed: int = 0) -> dict:
    key = jax.random.key(seed)
    ks = iter(jax.random.split(key, 24))
    f32 = jnp.float32
    nrm = lambda shape, scale: jax.random.normal(next(ks), shape, f32) * scale
    D = D_MODEL
    NE = (DEPTH + 1) // 2
    NO = DEPTH // 2
    x = nrm((BATCH, SEQ, D), 1.0)
    ab_w_in = nrm((NE, D, AB_IN_COLS), D ** -0.5)
    ab_shift_mix = jax.random.uniform(next(ks), (NE, RWKV_PROJ_COLS), f32)
    ab_w0 = jax.random.uniform(next(ks), (NE, RWKV_DIM), f32, minval=-6.0, maxval=0.0)
    ab_w_up = nrm((NE, DECAY_LORA, RWKV_DIM), 0.5 * DECAY_LORA ** -0.5)
    ab_a0 = nrm((NE, RWKV_DIM), 0.1)
    ab_a_up = nrm((NE, ICLR_LORA, RWKV_DIM), 0.5 * ICLR_LORA ** -0.5)
    ab_g_up = nrm((NE, GATE_LORA, RWKV_DIM), GATE_LORA ** -0.5)
    ab_k_k = 0.85 + nrm((NE, RWKV_DIM), 0.02)
    ab_k_a = 1.0 + nrm((NE, RWKV_DIM), 0.02)
    ab_r_k = nrm((NE, RWKV_HEADS, RWKV_HEAD_DIM), 0.1)
    ab_lnx_g = 1.0 + nrm((NE, RWKV_DIM), 0.02)
    ab_lnx_b = nrm((NE, RWKV_DIM), 0.02)
    ab_w_out = nrm((NE, AB_OUT_COLS, D), DEEPNORM_BETA * AB_OUT_COLS ** -0.5)
    c_w_in = nrm((NO, D, C_IN_COLS), D ** -0.5)
    c_w_out = nrm((NO, C_WIDTH, D), DEEPNORM_BETA * C_WIDTH ** -0.5)
    ln1_g = 1.0 + nrm((DEPTH, D), 0.02)
    ln1_b = nrm((DEPTH, D), 0.02)
    mlp_w1 = nrm((DEPTH, D, MLP_HIDDEN), D ** -0.5)
    mlp_w2 = nrm((DEPTH, MLP_HIDDEN, D), DEEPNORM_BETA * MLP_HIDDEN ** -0.5)
    ln2_g = 1.0 + nrm((DEPTH, D), 0.02)
    ln2_b = nrm((DEPTH, D), 0.02)
    return {'x': x, 'ab_w_in': ab_w_in, 'ab_shift_mix': ab_shift_mix, 'ab_w0': ab_w0,
            'ab_w_up': ab_w_up, 'ab_a0': ab_a0, 'ab_a_up': ab_a_up, 'ab_g_up': ab_g_up,
            'ab_k_k': ab_k_k, 'ab_k_a': ab_k_a, 'ab_r_k': ab_r_k, 'ab_lnx_g': ab_lnx_g,
            'ab_lnx_b': ab_lnx_b, 'ab_w_out': ab_w_out, 'c_w_in': c_w_in, 'c_w_out': c_w_out,
            'ln1_g': ln1_g, 'ln1_b': ln1_b, 'mlp_w1': mlp_w1, 'mlp_w2': mlp_w2,
            'ln2_g': ln2_g, 'ln2_b': ln2_b}

def second_block(x, ab_w_in, ab_shift_mix, ab_w0, ab_w_up, ab_a0, ab_a_up, ab_g_up, ab_k_k, ab_k_a,
              ab_r_k, ab_lnx_g, ab_lnx_b, ab_w_out, c_w_in, c_w_out, ln1_g, ln1_b, mlp_w1, mlp_w2,
              ln2_g, ln2_b):
    T = x.shape[1]
    pos = jnp.arange(T)
    for layer in range(DEPTH):
        j = layer // 2
        if layer % 2 == 0:
            h = _rwkv_moba_mixer(x, ab_w_in[j], ab_shift_mix[j], ab_w0[j], ab_w_up[j], ab_a0[j],
                                 ab_a_up[j], ab_g_up[j], ab_k_k[j], ab_k_a[j], ab_r_k[j],
                                 ab_lnx_g[j], ab_lnx_b[j], ab_w_out[j], pos)
        else:
            h = _dilated_mixer(x, c_w_in[j], c_w_out[j], pos)
        x = _layer_norm(DEEPNORM_ALPHA * x + h, ln1_g[layer], ln1_b[layer])
        x = _layer_norm(DEEPNORM_ALPHA * x + _sq_relu_mlp(x, mlp_w1[layer], mlp_w2[layer]),
                        ln2_g[layer], ln2_b[layer])
    return x


def setup_inputs(seed=0):
    out = dict(first_inputs(seed))
    for name, value in second_inputs(seed + 1).items():
        if name != "x":
            out[name + "_2"] = value
    return out


def reference(
    x, norm1_g, w_in, b_gate, na_rpb, mla_qa_g, mla_kva_g, mla_w_uq, mla_w_ukv, gqa_sink,
    w_br_na, w_br_mla, w_br_gqa, w_out, norm2_g, w_up, conv_w, conv_b, w_down, final_g,
    ab_w_in_2, ab_shift_mix_2, ab_w0_2, ab_w_up_2, ab_a0_2, ab_a_up_2, ab_g_up_2, ab_k_k_2,
    ab_k_a_2, ab_r_k_2, ab_lnx_g_2, ab_lnx_b_2, ab_w_out_2, c_w_in_2, c_w_out_2, ln1_g_2,
    ln1_b_2, mlp_w1_2, mlp_w2_2, ln2_g_2, ln2_b_2,
):
    x = first_block(
        x, norm1_g, w_in, b_gate, na_rpb, mla_qa_g, mla_kva_g, mla_w_uq, mla_w_ukv, gqa_sink,
        w_br_na, w_br_mla, w_br_gqa, w_out, norm2_g, w_up, conv_w, conv_b, w_down, final_g,
    )
    return second_block(
        x, ab_w_in_2, ab_shift_mix_2, ab_w0_2, ab_w_up_2, ab_a0_2, ab_a_up_2, ab_g_up_2,
        ab_k_k_2, ab_k_a_2, ab_r_k_2, ab_lnx_g_2, ab_lnx_b_2, ab_w_out_2, c_w_in_2, c_w_out_2,
        ln1_g_2, ln1_b_2, mlp_w1_2, mlp_w2_2, ln2_g_2, ln2_b_2,
    )


_drawn_inputs = setup_inputs


def setup_inputs(seed=0):
    import zlib

    import numpy as np

    out = dict(_drawn_inputs(seed))
    spreads = {}
    factors = {'b_gate': 8.0,
     'na_rpb': 3.345,
     'mla_qa_g': 8.0,
     'mla_kva_g': 6.646,
     'gqa_sink': 8.0,
     'ab_w_up_2': 8.0,
     'ab_a0_2': 8.0,
     'ab_k_k_2': 59.435,
     'ab_k_a_2': 23.604,
     'ab_lnx_g_2': 28.43,
     'ab_lnx_b_2': 26.437}
    for name, (base, spread) in spreads.items():
        noise = np.random.default_rng([zlib.crc32(name.encode()), seed]).standard_normal(out[name].shape)
        drawn = base * np.exp(spread * noise) if base else spread * noise
        out[name] = __import__('jax').numpy.asarray(drawn.astype(out[name].dtype))
    for name, factor in factors.items():
        out[name] = (out[name] * factor).astype(out[name].dtype)
    return out
```

```python
from contextlib import ExitStack

import numpy as np
import concourse.bass as bass
from concourse import mybir

F32 = mybir.dt.float32
F32R = mybir.dt.float32r
ALU = mybir.AluOpType
ACT = mybir.ActivationFunctionType
AX = mybir.AxisListType

P = 128
T = 256
D = 1024
DFF = 2816
BIG = 1e30
KAPPA = float(np.exp(np.float32(-0.5)))
ALPHA = float(4.0 ** 0.25)
UNIT = 2048
NRAW, NSPL, AHEAD = 3, 3, 2


def shape_constants():
    i = np.arange(P)
    tok = np.arange(T)
    c = {}
    c["ident"] = np.eye(P)
    c["ones"] = np.ones((P, P))
    c["half"] = (i[:, None] // 64 == i[None, :] // 64) * 1.0

    def rope(dim, rot, theta, width):
        half = rot // 2
        f = i % width
        if dim == rot:
            inv = 1.0 / (np.float32(theta) ** (np.arange(0, dim, 2, dtype=np.float32) / np.float32(dim)))
        else:
            inv = np.float32(theta) ** (-np.arange(half, dtype=np.float32) / np.float32(half))
        ang = tok.astype(np.float32)[None, :] * inv.astype(np.float32)[f % half][:, None]
        cs = np.where((f < rot)[:, None], np.cos(ang), 1.0)
        sn = np.where((f < rot)[:, None], np.sin(ang), 0.0)
        perm = np.zeros((P, P))
        for m in range(P):
            if f[m] < half:
                perm[m + half, m] = -1.0
            elif f[m] < rot:
                perm[m - half, m] = 1.0
        return cs, sn, perm

    c["cos1"], c["sin1"], c["perm1"] = rope(64, 64, 10000.0, 64)
    c["cos2"], c["sin2"], c["perm2"] = rope(128, 32, 500000.0, 128)
    cq = np.arange(64)
    start = np.clip(cq - 8, 0, 48)
    inside = (cq[None, :] >= start[:, None]) & (cq[None, :] < start[:, None] + 16)
    c["namask"] = np.tile(np.where(inside, 0.0, BIG), (2, 1))

    def both(ok):
        m = np.where(ok, 0.0, BIG)
        return np.concatenate([m[0:P], m[P:T]], axis=1)

    q, k = tok[:, None], tok[None, :]
    c["gmask"] = both(np.abs(q - k) <= 128)
    c["causal"] = both(k <= q)
    c["dil0"] = both((k <= q) & (q - k <= 128))
    c["dil1"] = both((k <= q) & ((q - k) % 4 == 0))
    c["dil2"] = both((k <= q) & ((q - k) % 16 == 0))
    a = i % 64
    j = np.arange(64)
    for n in range(6):
        m = 1 << n
        t, s = j[None, :], a[:, None]
        c[f"lev{n}"] = ((t // (2 * m) == s // (2 * m)) & (t % (2 * m) >= m) & (s % (2 * m) < m)) * 1.0
    c["strict"] = (j[None, :] > a[:, None]) * 1.0
    c["incl"] = (j[None, :] >= a[:, None]) * 1.0
    c["id64"] = (j[None, :] == a[:, None]) * 1.0
    c["eps"] = np.tile(np.array([[1e-6, 1e-5, 64e-5, 0.0]]), (P, 1))
    return c


CONST1 = ["ident", "ones", "half", "eps"]
CONST_A = ["cos1", "sin1", "perm1", "namask", "gmask"]
CONST_M = ["cos2", "sin2", "perm2", "causal"]
CONST_W = ["lev0", "lev1", "lev2", "lev3", "lev4", "lev5", "strict", "incl", "id64"]
CONST_D = ["cos2", "sin2", "perm2", "dil0", "dil1", "dil2"]


def pack(names, c):
    at, cols, n = {}, [], 0
    for name in names:
        at[name] = (n, c[name].shape[1])
        cols.append(c[name])
        n += c[name].shape[1]
    return at, np.ascontiguousarray(np.concatenate(cols, axis=1).astype(np.float32))


def param_list():
    out = []
    for l in range(2):
        for name in ("norm1_g", "b_gate", "mla_qa_g", "mla_kva_g", "norm2_g", "conv_b"):
            out.append((f"{name}{l}", name, (l,)))
        for t in range(3):
            out.append((f"conv{t}_{l}", "conv_w", (l, t)))
        for name in ("ln1_g_2", "ln1_b_2", "ln2_g_2", "ln2_b_2"):
            out.append((f"{name}{l}", name, (l,)))
    out.append(("final_g", "final_g", ()))
    for name in ("ab_shift_mix_2", "ab_w0_2", "ab_a0_2", "ab_k_k_2", "ab_k_a_2", "ab_r_k_2", "ab_lnx_g_2", "ab_lnx_b_2"):
        out.append((name, name, (0,)))
    return out


PARAM_LEN = {"norm1_g": 1024, "b_gate": 3072, "mla_qa_g": 384, "mla_kva_g": 256, "norm2_g": 1024, "conv_b": 5632,
             "conv_w": 5632, "ln1_g_2": 1024, "ln1_b_2": 1024, "ln2_g_2": 1024, "ln2_b_2": 1024, "final_g": 1024,
             "ab_shift_mix_2": 1824, "ab_w0_2": 512, "ab_a0_2": 512, "ab_k_k_2": 512, "ab_k_a_2": 512,
             "ab_r_k_2": 512, "ab_lnx_g_2": 512, "ab_lnx_b_2": 512}


def param_places():
    at, n = {}, 0
    for key, name, _ in param_list():
        w = -(-PARAM_LEN[name] // P)
        at[key] = n
        n += w
    at["sink0"] = n
    at["sink1"] = n + 8
    return at, n + 16


class Prog:

    ENGINES = ("pe", "dve", "act", "pool", "sp")

    def __init__(self):
        self.q = {e: [] for e in self.ENGINES}
        self.count = {}
        self.seen = {e: {} for e in self.ENGINES}
        self.extra = {e: [] for e in self.ENGINES}

    def waits(self, e, deps):
        need = {}
        stack = [deps, self.extra[e]]
        while stack:
            x = stack.pop()
            if x is None:
                continue
            if isinstance(x, list):
                stack.extend(x)
            else:
                need[x[0]] = max(need.get(x[0], 0), x[1])
        self.extra[e] = []
        out = []
        for s, v in need.items():
            if self.seen[e].get(s, 0) < v:
                self.seen[e][s] = v
                out.append((s, v))
        return out

    def op(self, e, fn, deps=None, sig=True, sem=None, step=1):
        w = self.waits(e, [deps])
        s = sem or e
        self.q[e].append((w, fn, s if sig else None, step))
        if sig:
            self.count[s] = self.count.get(s, 0) + step
            return (s, self.count[s])
        return None

    def last(self, e):
        return (e, self.count[e]) if self.count.get(e) else None

    def fence(self, engines, after=("pe", "dve", "act", "pool")):
        tokens = [self.last(x) for x in after]
        for e in engines:
            self.extra[e] = self.extra[e] + tokens


class Banks:

    def __init__(self, tiles):
        self.tiles = tiles
        self.free = [[] for _ in tiles]
        self.open = [False] * len(tiles)
        self.n = 0

    def get(self):
        b = self.n % len(self.tiles)
        self.n += 1
        assert not self.open[b], "PSUM bank still in use"
        self.open[b] = True
        return b

    def done(self, b, tokens):
        self.free[b] = tokens
        self.open[b] = False


class Weights:

    def __init__(self, pr, specs):
        self.pr, self.specs, self.known = pr, [], specs
        self.n = self.split_to = self.loaded = 0
        self.pe_done, self.parts_done, self.raw_done = {}, {}, {}

    def start(self, dram, raw, hi, lo, offsets):
        self.dram, self.raw, self.hi, self.lo, self.offsets = dram, raw, hi, lo, offsets
        for _ in range(min(NRAW, len(self.known or []))):
            self.load()

    def width(self, u):
        name, layer, rows, cols = self.known[u]
        return len(rows) * len(cols)

    def load(self):
        u = self.loaded
        if u >= len(self.known):
            return
        self.loaded += 1
        n = self.width(u)
        src = self.dram[self.offsets[u]:self.offsets[u] + P * n].rearrange("(p n) -> p n", p=P)
        dst = self.raw[u % NRAW][:, 0:n]
        self.raw_done[u] = self.pr.op("sp", lambda e: e.dma_start(dst, src),
                                      [self.parts_done.get(u - NRAW)], sem=f"w{u % NRAW}", step=16)

    def split(self, u):
        n = self.width(u)
        raw, hi, lo = self.raw[u % NRAW][:, 0:n], self.hi[u % NSPL][:, 0:n], self.lo[u % NSPL][:, 0:n]
        free = self.pe_done.get(u - NSPL)
        t1 = self.pr.op("act", lambda e: e.activation(hi, raw, ACT.Copy), [self.raw_done[u], free])
        t2 = self.pr.op("dve", lambda e: e.tensor_tensor(lo, raw, hi.bitcast(F32), ALU.subtract), [t1, self.raw_done[u], free])
        self.parts_done[u] = [t1, t2]
        self.load()

    def use(self, name, layer, rows, cols):
        u = self.n
        self.n += 1
        self.specs.append((name, layer, tuple(rows), tuple(int(c) for c in cols)))
        if self.known:
            while self.split_to < min(u + AHEAD + 1, len(self.known)):
                self.split(self.split_to)
                self.split_to += 1
        else:
            self.parts_done[u] = []
        return u

    def part(self, u, k, c0, c1, low):
        nc = len(self.specs[u][3])
        t = (self.lo if low else self.hi)[u % NSPL]
        return t[:, k * nc + c0:k * nc + c1]

    def done(self, u, token):
        self.pe_done[u] = token


def program(nc, dram, places, specs, offsets):
    tag = "a" if specs is None else "b"
    pr = Prog()
    W = Weights(pr, specs)
    names = [0]
    at1, atA, atM, atW, atD, atP = places
    top = ExitStack()

    def sb(ctx, shape, dt=F32):
        names[0] += 1
        return ctx.enter_context(nc.sbuf_tensor(f"{tag}{names[0]}", shape, dt))

    def op(e, fn, *deps):
        return pr.op(e, fn, list(deps))

    def dve(fn, *deps):
        return pr.op("dve", fn, list(deps))

    def act(fn, *deps):
        return pr.op("act", fn, list(deps))

    def pool(fn, *deps):
        return pr.op("pool", fn, list(deps))

    def mm(out, lhsT, rhs, start, stop, deps=None, sig=False):
        return pr.op("pe", lambda e: e.matmul(out, lhsT, rhs, start=start, stop=stop), deps, sig=sig)

    banks = Banks([top.enter_context(nc.psum_tensor(f"{tag}ps{b}", [P, 512], F32)) for b in range(8)])
    raw = [sb(top, [P, UNIT]) for _ in range(NRAW)]
    whi = [sb(top, [P, UNIT], F32R) for _ in range(NSPL)]
    wlo = [sb(top, [P, UNIT], F32R) for _ in range(NSPL)]
    X = sb(top, [P, 8, T])
    Hh = sb(top, [P, 8, T], F32R)
    Hl = sb(top, [P, 8, T], F32R)
    c1 = sb(top, [P, sum(w for _, w in at1.values())])
    par = sb(top, [P, atP[1]])
    rs = sb(top, [P, T])
    mu = sb(top, [P, T])

    def C(name, a=0, b=None):
        o, w = at1[name]
        return c1[:, o + a:o + (w if b is None else b)]

    def par_col(key, j=0):
        o = atP[0][key] + j
        return par[:, o:o + 1]

    ident, ones, half = C("ident"), C("ones"), C("half")
    eps_rms, eps_ln, eps_gn = C("eps", 0, 1), C("eps", 1, 2), C("eps", 2, 3)

    t_x = pr.op("sp", lambda e: e.dma_start(X[:, :, :], dram["x"]), sem="ld_x", step=16)
    t_c1 = pr.op("sp", lambda e: e.dma_start(c1[:, :], dram["c1"]), sem="ld_c", step=16)
    t_par = pr.op("sp", lambda e: e.dma_start(par[:, :], dram["par"]), sem="ld_p", step=16)
    W.start(dram["w"], raw, whi, wlo, offsets)
    for e in ("pe", "act", "dve", "pool"):
        pr.extra[e] = [t_c1, t_par]

    class Act2:

        def __init__(self, hi, lo, tokens):
            self.hi, self.lo, self.tokens = hi, lo, tokens

    def split_act(src, hi, lo, *deps, eng="dve"):
        t1 = act(lambda e: e.activation(hi, src, ACT.Copy), *deps)
        t2 = op(eng, lambda e: e.tensor_tensor(lo, src, hi.bitcast(F32), ALU.subtract), t1, *deps)
        return [t1, t2]

    def feature_tiles(name, layer, kchunks, tile_cols, x, per_unit=None, kpart=None):
        nk = len(kchunks)
        kpart = kpart or nk
        per_unit = per_unit or max(1, UNIT // (kpart * P))
        n = len(tile_cols)
        j = 0
        b = None
        while j < n:
            g = list(range(j, min(j + per_unit, n)))
            cols = np.concatenate([tile_cols[i] for i in g])
            parts = [list(range(a, min(a + kpart, nk))) for a in range(0, nk, kpart)]
            assert len(parts) == 1 or len(g) == 1
            for pi, ks in enumerate(parts):
                u = W.use(name, layer, [kchunks[k] for k in ks], cols)
                for gi, i in enumerate(g):
                    if pi == 0:
                        b = banks.get()
                    out = banks.tiles[b][:, 0:T]
                    deps = [W.parts_done[u], x.tokens, banks.free[b]]
                    for q, k in enumerate(ks):
                        first, last = k == 0, k == nk - 1
                        wh = W.part(u, q, gi * P, gi * P + P, False)
                        wl = W.part(u, q, gi * P, gi * P + P, True)
                        mm(out, wh, x.hi[:, k, :], first, False, deps if q == 0 else None)
                        mm(out, wh, x.lo[:, k, :], False, False)
                        tok = mm(out, wl, x.hi[:, k, :], False, last, sig=(q == len(ks) - 1))
                    if pi == len(parts) - 1 and gi < len(g) - 1:
                        yield i, out, b, tok, i == n - 1
                W.done(u, tok)
                if pi == len(parts) - 1:
                    yield g[-1], out, b, tok, g[-1] == n - 1
            j += per_unit

    def token_tiles(name, layer, kchunks, cols, x, width):
        nk = len(kchunks)
        for c0 in range(0, len(cols), width):
            cc = cols[c0:c0 + width]
            w = len(cc)
            u = W.use(name, layer, kchunks, cc)
            b = banks.get()
            for tb in range(2):
                out = banks.tiles[b][:, tb * w:tb * w + w]
                deps = [W.parts_done[u], x.tokens, banks.free[b]]
                for k in range(nk):
                    xh, xl = x.hi[:, k, tb * P:tb * P + P], x.lo[:, k, tb * P:tb * P + P]
                    mm(out, xh, W.part(u, k, 0, w, False), k == 0, False, deps if k == 0 else None)
                    mm(out, xl, W.part(u, k, 0, w, False), False, False)
                    tok = mm(out, xh, W.part(u, k, 0, w, True), False, k == nk - 1, sig=(k == nk - 1))
            W.done(u, tok)
            yield c0, b, tok

    def pieces(a, b):
        return [np.arange(c, c + P) for c in range(a, b, P)]

    def inverse_root(src, bank, scale, eps, dep):
        t = act(lambda e: e.activation(rs[:, :], src, ACT.Sqrt, bias=eps, scale=scale), dep, rs_free[0])
        banks.done(bank, [t])
        return dve(lambda e: e.reciprocal(rs[:, :], rs[:, :]), t)

    rs_free = [None]

    def column_sums(sq, n, deps):
        b = banks.get()
        out = banks.tiles[b][:, 0:T]
        for k in range(n):
            tok = mm(out, ones, sq[:, k, :], k == 0, k == n - 1, [deps, banks.free[b]] if k == 0 else None, sig=(k == n - 1))
        return b, out, tok

    def rmsnorm(src, n, gkey, sq, *deps):
        t = act(lambda e: e.activation(sq[:, 0:n, :], src[:, 0:n, :], ACT.Square), *deps)
        b, out, tok = column_sums(sq, n, [t])
        t = inverse_root(out, b, 1.0 / (n * P), eps_rms, tok)
        res = []
        for k in range(n):
            res.append(dve(lambda e, k=k: e.scalar_tensor_tensor(sq[:, k, :], src[:, k, :], par_col(gkey, k), rs[:, :],
                                                                ALU.mult, ALU.mult), t, tok))
        rs_free[0] = res[-1]
        return res

    def split_chunks(src, n, hi, lo, toks, *deps):
        res = []
        for k in range(0, n, 2):
            m = min(n, k + 2)
            res += split_act(src[:, k:m, :], hi[:, k:m, :], lo[:, k:m, :], toks[k:m], *deps, eng="dve" if k % 4 else "pool")
        return res

    def layernorm(key_g, key_b, out, sq, *deps):
        b, s, tok = column_sums(X, 8, list(deps))
        t = act(lambda e: e.mul(mu[:, :], s, 1.0 / D), tok)
        banks.done(b, [t])
        mub = mu[:, :].unsqueeze(1).broadcast_to([P, 8, T])
        t = dve(lambda e: e.tensor_tensor(X[:, :, :], X[:, :, :], mub, ALU.subtract), t, *deps)
        t2 = act(lambda e: e.activation(sq[:, :, :], X[:, :, :], ACT.Square), t)
        b, s2, tok = column_sums(sq, 8, [t2])
        t = inverse_root(s2, b, 1.0 / D, eps_ln, tok)
        rsb = rs[:, :].unsqueeze(1).broadcast_to([P, 8, T])
        t = dve(lambda e: e.tensor_tensor(X[:, :, :], X[:, :, :], rsb, ALU.mult), t)
        rs_free[0] = t
        res = []
        for k in range(8):
            g, bb = par_col(key_g, k), par_col(key_b, k)
            res.append(act(lambda e, k=k, g=g, bb=bb: e.activation(out[:, k, :], X[:, k, :], ACT.Identity, bias=bb, scale=g), t))
        return res

    def rope(dst, src, cos, sin, perm, tmp, tmp_free, scale, t_src, *deps):
        b = banks.get()
        out = banks.tiles[b][:, 0:T]
        tok = mm(out, perm, src, True, True, [t_src, list(deps), banks.free[b]], sig=True)
        t1 = dve(lambda e: e.scalar_tensor_tensor(tmp, out, scale, sin, ALU.mult, ALU.mult), tok, tmp_free, *deps)
        banks.done(b, [t1])
        t2 = dve(lambda e: e.scalar_tensor_tensor(src, src, scale, cos, ALU.mult, ALU.mult), tok, *deps)
        res = []
        for (d, r0, r1) in dst:
            res.append(dve(lambda e, d=d, r0=r0, r1=r1: e.tensor_tensor(d, src[r0:r1, :], tmp[r0:r1, :], ALU.add), t1, t2, *deps))
        return res

    class Ring:
        def __init__(self, tiles):
            self.tiles, self.free, self.n = tiles, [None] * len(tiles), 0

        def get(self):
            i = self.n % len(self.tiles)
            self.n += 1
            return i

    def attention(heads, rS, rT, small):
        lag = {"s": 0, "t": 2, "v": 3}
        n = len(heads)

        def scores(h):
            h["col"] = col = small["n"] % small["size"]
            small["n"] += 1
            w = h["widths"]
            st = small["tile"]
            mn, l, r = st[:, col, 0:2], st[:, col, 2:4], st[:, col, 4:6]
            ng = len(h["qk"])
            h["bufs"] = []
            prev = [[small["free"][col]], [small["free"][col]]]
            toks_min = [None, None]
            for g in range(ng):
                b = banks.get()
                tok = h["qk"][g](banks.tiles[b], banks.free[b])
                i = rS.get()
                S = rS.tiles[i]
                h["bufs"].append(i)
                if h["masks"][g] is None:
                    t = dve(lambda e, b=b: e.tensor_reduce(mn, banks.tiles[b][:, :].rearrange("p (a k) -> p a k", a=2),
                                                           AX.X, ALU.min), tok, prev[0])
                    toks_min = [t, t]
                    h["src"] = banks.tiles[b]
                    h["bank"] = b
                else:
                    ts = []
                    o = 0
                    for qb in range(2):
                        init = 3.0e38 if g == 0 else mn[:, qb:qb + 1]
                        if h.get("sink") is not None:
                            init = h["sink"]
                        dst, ps, mk = S[:, o:o + w[qb]], banks.tiles[b][:, o:o + w[qb]], h["masks"][g][qb]
                        t = dve(lambda e, dst=dst, ps=ps, mk=mk, init=init, qb=qb: e.tensor_tensor_reduce(
                            dst, ps, mk, 1.0, init, ALU.add, ALU.min, mn[:, qb:qb + 1]), tok, rS.free[i], prev[qb], h["deps"])
                        toks_min[qb] = t
                        prev[qb] = [t]
                        ts.append(t)
                        o += w[qb]
                    banks.done(b, ts)
            te = []
            for g in range(ng):
                S = rS.tiles[h["bufs"][g]]
                o = 0
                for qb in range(2):
                    src = S if h["masks"][g] is not None else h["src"]
                    acc = l[:, qb:qb + 1] if ng == 1 else st[:, col, 6 + 2 * g + qb:7 + 2 * g + qb]
                    t = act(lambda e, S=S, src=src, o=o, qb=qb, acc=acc: e.activation(
                        S[:, o:o + w[qb]], src[:, o:o + w[qb]], ACT.Exp, bias=mn[:, qb:qb + 1], scale=-1.0, accum_out=acc),
                        toks_min, rS.free[h["bufs"][g]] if h["masks"][g] is None else None)
                    te.append(t)
                    o += w[qb]
                if h["masks"][g] is None:
                    banks.done(h["bank"], te)
            tot = sum(w)
            S0 = rS.tiles[h["bufs"][0]]
            if ng == 1 and h.get("sink") is not None:
                for qb in range(2):
                    te.append(act(lambda e, qb=qb: e.activation(st[:, col, 6 + qb:7 + qb], h["sink"], ACT.Exp,
                                                                bias=mn[:, qb:qb + 1], scale=-1.0), toks_min))
                t = dve(lambda e: e.tensor_tensor(l, l, st[:, col, 6:8], ALU.add), te)
            elif ng == 3:
                t = dve(lambda e: e.tensor_tensor(l, st[:, col, 6:8], st[:, col, 8:10], ALU.add), te)
                t = dve(lambda e: e.tensor_tensor(l, l, st[:, col, 10:12], ALU.add), t)
                S1, S2 = rS.tiles[h["bufs"][1]], rS.tiles[h["bufs"][2]]
                t2 = pool(lambda e: e.tensor_tensor(S0[:, 0:tot], S0[:, 0:tot], S1[:, 0:tot], ALU.add), te)
                t3 = dve(lambda e: e.tensor_tensor(S0[:, 0:tot], S0[:, 0:tot], S2[:, 0:tot], ALU.add), t2)
                rS.free[h["bufs"][1]] = t2
                rS.free[h["bufs"][2]] = t3
                t = [t, t3]
            else:
                t = te
            t = dve(lambda e: e.reciprocal(r, l), t, te)
            o = 0
            h["p"] = []
            for qb in range(2):
                h["p"].append(dve(lambda e, o=o, qb=qb: e.tensor_scalar(S0[:, o:o + w[qb]], S0[:, o:o + w[qb]], r[:, qb:qb + 1],
                                                                       None, ALU.mult), t))
                o += w[qb]
            small["free"][col] = h["p"]

        def turn(h):
            w = h["widths"]
            i = h["bufs"][0]
            S = rS.tiles[i]
            b = banks.get()
            h["pt"] = []
            o = 0
            first = [banks.free[b], h["p"]]
            for qb in range(2):
                for kb in range(w[qb] // P):
                    slot = len(h["pt"])
                    h["pt"].append((kb, qb))
                    out, src = banks.tiles[b][:, slot * P:slot * P + P], S[:, o + kb * P:o + kb * P + P]
                    tok = pr.op("pe", lambda e, out=out, src=src: e.transpose(out, src, ident), first, sig=True)
                    first = None
                o += w[qb]
            rS.free[i] = tok
            j = rT.get()
            h["T"] = j
            n_ = len(h["pt"]) * P
            dst, src = rT.tiles[j][:, 0:n_], banks.tiles[b][:, 0:n_]
            t = act(lambda e: e.activation(dst, src, ACT.Copy), tok, rT.free[j])
            banks.done(b, [t])
            h["tt"] = t

        pair = {}

        def values(h):
            d = h["d"]
            TT = rT.tiles[h["T"]]
            base = h["base"]
            if base == 0:
                pair["b"] = banks.get()
            b = pair["b"]
            first = [banks.free[b], h["tt"], h["vdeps"]]
            w = h["widths"]
            for qb in range(2):
                kbs = [kb for kb, q in h["pt"] if q == qb]
                out = banks.tiles[b][base:base + d, qb * P:qb * P + P]
                for x, kb in enumerate(kbs):
                    slot = h["pt"].index((kb, qb))
                    tok = mm(out, h["v"](kb), TT[:, slot * P:slot * P + P], x == 0, x == len(kbs) - 1, first, sig=(x == len(kbs) - 1))
                    first = None
            rT.free[h["T"]] = tok
            if base + d == P:
                src = banks.tiles[b][:, 0:T]
                hi, lo, sink_list = h["out"]
                t1 = act(lambda e: e.activation(hi, src, ACT.Copy), tok, h["odeps"])
                t2 = dve(lambda e: e.tensor_tensor(lo, src, hi.bitcast(F32), ALU.subtract), t1)
                banks.done(b, [t1, t2])
                sink_list += [t1, t2]

        for i in range(n + 3):
            if i < n:
                scores(heads[i])
            if 0 <= i - lag["t"] < n:
                turn(heads[i - lag["t"]])
            if 0 <= i - lag["v"] < n:
                values(heads[i - lag["v"]])
            yield

    def run(gen):
        for _ in gen:
            pass

    def mk_small(ctx):
        return {"tile": sb(ctx, [P, 6, 12]), "n": 0, "size": 6, "free": [None] * 6}

    def residual_add(name, layer, nk, x, scale, kpart=None):
        toks = []
        for j, out, b, tok, last in feature_tiles(name, layer, list(range(nk)), pieces(0, D), x, kpart=kpart):
            if scale == 1.0:
                t = dve(lambda e, j=j, out=out: e.tensor_tensor(X[:, j, :], X[:, j, :], out, ALU.add), tok)
            else:
                t = dve(lambda e, j=j, out=out: e.scalar_tensor_tensor(X[:, j, :], X[:, j, :], scale, out, ALU.mult, ALU.add), tok)
            toks.append(t)
            banks.done(b, toks[-1:])
        return toks

    def mixer1(l, x_toks):
        with ExitStack() as s1:
            cA = sb(s1, [P, sum(w for _, w in atA.values())])
            pr.fence(["sp"])
            t_cA = pr.op("sp", lambda e: e.dma_start(cA[:, :], dram["cA"]), sem="ld_A", step=16)

            def CA(name):
                o, w = atA[name]
                return cA[:, o:o + w]

            cos, sin, perm = CA("cos1"), CA("sin1"), CA("perm1")
            yh = [sb(s1, [P, 4, T], F32R) for _ in range(3)]
            yl = [sb(s1, [P, 4, T], F32R) for _ in range(3)]
            ytok = [[], [], []]
            early = s1.enter_context(ExitStack())
            S_ring = Ring([sb(early, [P, 512]) for _ in range(3)])
            T_ring = Ring([sb(early, [P, 512]) for _ in range(2)])
            small = mk_small(early)
            nsink = sb(early, [P, 8])
            cqn_h, cqn_l = sb(early, [P, 3, T], F32R), sb(early, [P, 3, T], F32R)
            ckn_h, ckn_l = sb(early, [P, 2, T], F32R), sb(early, [P, 2, T], F32R)
            pr.fence(["act", "dve", "pool"])
            with ExitStack() as s2:
                hs = sb(s2, [P, 8, T])
                t = rmsnorm(X, 8, f"norm1_g{l}", hs, x_toks)
                H = Act2(Hh, Hl, split_chunks(hs, 8, Hh, Hl, t))
            o_s = atP[0][f"sink{l}"]
            t_sink = pool(lambda e: e.tensor_scalar(nsink[:, :], par[:, o_s:o_s + 8], -1.0, None, ALU.mult))

            with ExitStack() as s2:
                pr.fence(["sp", "act", "dve", "pool"])
                bias = sb(s2, [P, 8, 2, T])
                tb = []
                for qb in range(2):
                    for r2 in range(2):
                        rq = 2 * qb + r2
                        src = dram["rpb"][l, :, :, 3 - rq:7 - rq, :].rearrange("p h r c -> p h (r c)")
                        dst = bias[64 * r2:64 * r2 + 64, :, qb, :]
                        tb.append(pr.op("act", lambda e, src=src, dst=dst: e.dma_start(dst, src), None, sem=f"ld_b{rq}", step=16))
                Q = sb(s2, [P, 4, T])
                K = sb(s2, [P, 8, T])
                V = sb(s2, [P, 2, 512])
                t_z = pool(lambda e: e.memset(K[:, :, :], 0.0))
                nm = CA("namask").unsqueeze(1).broadcast_to([P, 64, 64])
                t_bias = pool(lambda e: e.tensor_tensor(bias[:, :, :, :].rearrange("p h q (r c) -> p (h q r) c", c=64), nm,
                                                        bias[:, :, :, :].rearrange("p h q (r c) -> p (h q r) c", c=64),
                                                        ALU.subtract), tb, t_cA)
                tq, tk, tv = [], [], []
                for j, out, b, tok, last in feature_tiles("w_in", l, range(8), pieces(0, 512), H):
                    tq.append(act(lambda e, j=j, out=out: e.mul(Q[:, j, :], out, -0.125), tok))
                    banks.done(b, tq[-1:])
                for j, out, b, tok, last in feature_tiles("w_in", l, range(8), pieces(512, 1024), H):
                    tk.append(dve(lambda e, j=j, out=out: e.tensor_copy(K[0:64, 2 * j, :], out[0:64, :]), tok, t_z))
                    tk.append(act(lambda e, j=j, out=out: e.activation(K[64:128, 2 * j + 1, :], out[64:128, :], ACT.Copy), tok, t_z))
                    banks.done(b, tk[-2:])
                for c0, b, tok in token_tiles("w_in", l, range(8), np.arange(1024, 1536), H, T):
                    tv.append(act(lambda e, c0=c0, b=b: e.activation(V[:, :, c0:c0 + T], banks.tiles[b][:, :].rearrange("p (a c) -> p a c", a=2), ACT.Copy), tok))
                    banks.done(b, tv[-1:])

                with ExitStack() as s3:
                    cq = sb(s3, [P, 3, T])
                    ck = sb(s3, [P, 2, T])
                    sq = sb(s3, [P, 3, T])
                    tc = []
                    for j, out, b, tok, last in feature_tiles("w_in", l, range(8), pieces(1536, 2176), H):
                        dst = cq[:, j, :] if j < 3 else ck[:, j - 3, :]
                        tc.append(act(lambda e, dst=dst, out=out: e.activation(dst, out, ACT.Copy), tok))
                        banks.done(b, tc[-1:])
                    t = rmsnorm(cq, 3, f"mla_qa_g{l}", sq, tc)
                    CQ = Act2(cqn_h, cqn_l, split_chunks(sq, 3, cqn_h, cqn_l, t))
                    t = rmsnorm(ck, 2, f"mla_kva_g{l}", sq, tc, CQ.tokens)
                    CK = Act2(ckn_h, ckn_l, split_chunks(sq, 2, ckn_h, ckn_l, t))

                heads = []
                for h in range(8):
                    def qk(ps, free, h=h):
                        for qb in range(2):
                            tok = mm(ps[:, qb * T:qb * T + T], Q[:, h // 2, qb * P:qb * P + P], K[:, h, :], True, True,
                                     [free, tq, tk] if qb == 0 else None, sig=True)
                        return tok
                    heads.append(dict(qk=[qk], masks=[[bias[:, h, 0, :], bias[:, h, 1, :]]], widths=[T, T], deps=[t_bias], d=64,
                                      base=64 * (h % 2), v=lambda kb, h=h: V[:, kb, 64 * h:64 * h + 64], vdeps=tv,
                                      out=(yh[0][:, h // 2, :], yl[0][:, h // 2, :], ytok[0]), odeps=None))
                run(attention(heads, S_ring, T_ring, small))

            with ExitStack() as s2:
                pr.fence(["act", "dve", "pool"])
                qn = sb(s2, [P, 4, T])
                qp = sb(s2, [P, 2, T])
                kn = sb(s2, [P, 4, T])
                kp = sb(s2, [P, 2, T])
                vm = sb(s2, [P, 2, 512])
                gq = sb(s2, [P, 4, T])
                gk = sb(s2, [P, 4, T])
                gv = sb(s2, [P, 2, P])
                raw_ring = Ring([sb(s2, [P, T]) for _ in range(3)])
                tmp_ring = Ring([sb(s2, [P, T]) for _ in range(2)])
                tz1 = pool(lambda e: e.memset(kp[:, :, :], 0.0))
                tz2 = pool(lambda e: e.memset(gk[:, :, :], 0.0))

                def rotated(out, b, tok, freeing, dst, scale, deps):
                    i, j = raw_ring.get(), tmp_ring.get()
                    t = act(lambda e: e.activation(raw_ring.tiles[i][:, :], out, ACT.Copy), tok, raw_ring.free[i])
                    res = rope(dst, raw_ring.tiles[i][:, :], cos, sin, perm, tmp_ring.tiles[j][:, :], tmp_ring.free[j], scale, t, t_cA, *deps)
                    raw_ring.free[i] = tmp_ring.free[j] = res
                    return t, res

                kr = np.arange(2176, 2240)
                tiles = [np.concatenate([kr, kr])] + pieces(2240, 2752)
                for g in range(2):
                    k0 = np.arange(2752 + 64 * g, 2816 + 64 * g)
                    tiles.append(np.concatenate([k0, k0]))
                tkp, tgq, tgk, prevt = [], [], [], []
                for j, out, b, tok, last in feature_tiles("w_in", l, range(8), tiles, H):
                    if j == 0:
                        dst, scale, deps = [(kp[0:64, 0, :], 0, 64), (kp[64:128, 1, :], 64, 128)], 1.0, [tz1]
                    elif j < 5:
                        dst, scale, deps = [(gq[:, j - 1, :], 0, 128)], -0.125, []
                    else:
                        g = j - 5
                        dst, scale, deps = [(gk[0:64, 2 * g, :], 0, 64), (gk[64:128, 2 * g + 1, :], 64, 128)], 1.0, [tz2]
                    t, res = rotated(out, b, tok, None, dst, scale, deps)
                    prevt.append(t)
                    (tkp if j == 0 else tgq if j < 5 else tgk).extend(res)
                    banks.done(b, prevt[-1:])
                tgv = []
                for c0, b, tok in token_tiles("w_in", l, range(8), np.arange(2880, 3008), H, P):
                    tgv.append(act(lambda e, b=b: e.activation(gv[:, :, :], banks.tiles[b][:, 0:T].rearrange("p (a c) -> p a c", a=2), ACT.Copy), tok))
                    banks.done(b, tgv[-1:])
                sc = -(192.0 ** -0.5)
                tiles = [np.arange(192 * h, 192 * h + P) for h in range(4)]
                tiles += [np.concatenate([np.arange(192 * h + P, 192 * h + 192) for h in (2 * c, 2 * c + 1)]) for c in range(2)]
                tqn, tqp, prevt = [], [], []
                for j, out, b, tok, last in feature_tiles("mla_w_uq", l, range(3), tiles, CQ, per_unit=3):
                    if j < 4:
                        t = act(lambda e, j=j, out=out: e.mul(qn[:, j, :], out, sc), tok)
                        tqn.append(t)
                    else:
                        t, res = rotated(out, b, tok, None, [(qp[:, j - 4, :], 0, 128)], sc, [])
                        tqp += res
                    prevt.append(t)
                    banks.done(b, prevt[-1:])
                tkn, tvm = [], []
                for j, out, b, tok, last in feature_tiles("mla_w_ukv", l, range(2), [np.arange(256 * h, 256 * h + P) for h in range(4)], CK, per_unit=4):
                    tkn.append(act(lambda e, j=j, out=out: e.activation(kn[:, j, :], out, ACT.Copy), tok))
                    banks.done(b, tkn[-1:])
                vc = np.concatenate([np.arange(256 * h + P, 256 * h + 256) for h in range(4)])
                for c0, b, tok in token_tiles("mla_w_ukv", l, range(2), vc, CK, T):
                    tvm.append(act(lambda e, c0=c0, b=b: e.activation(vm[:, :, c0:c0 + T], banks.tiles[b][:, :].rearrange("p (a c) -> p a c", a=2), ACT.Copy), tok))
                    banks.done(b, tvm[-1:])

                heads = []
                for h in range(4):
                    def qk(ps, free, h=h):
                        for qb in range(2):
                            mm(ps[:, qb * T:qb * T + T], qn[:, h, qb * P:qb * P + P], kn[:, h, :], True, False,
                               [free, tqn, tqp, tkn, tkp] if qb == 0 else None)
                            tok = mm(ps[:, qb * T:qb * T + T], qp[:, h // 2, qb * P:qb * P + P], kp[:, h % 2, :], False, True, sig=True)
                        return tok
                    heads.append(dict(qk=[qk], masks=[None], widths=[T, T], deps=None, d=P, base=0,
                                      v=lambda kb, h=h: vm[:, kb, P * h:P * h + P], vdeps=tvm,
                                      out=(yh[1][:, h, :], yl[1][:, h, :], ytok[1]), odeps=None))
                gm = CA("gmask")
                for h in range(8):
                    def qk(ps, free, h=h):
                        for qb in range(2):
                            tok = mm(ps[:, qb * T:qb * T + T], gq[:, h // 2, qb * P:qb * P + P], gk[:, 2 * (h // 4) + h % 2, :], True, True,
                                     [free, tgq, tgk] if qb == 0 else None, sig=True)
                        return tok
                    heads.append(dict(qk=[qk], masks=[[gm[:, 0:T], gm[:, T:2 * T]]], widths=[T, T], deps=[t_cA, t_sink], d=64,
                                      base=64 * (h % 2), sink=nsink[:, h:h + 1], v=lambda kb, h=h: gv[:, kb, 64 * (h // 4):64 * (h // 4) + 64],
                                      vdeps=tgv, out=(yh[2][:, h // 2, :], yl[2][:, h // 2, :], ytok[2]), odeps=None))
                run(attention(heads, S_ring, T_ring, small))
            early.close()

            with ExitStack() as s2:
                pr.fence(["act", "dve", "pool"])
                gt = [sb(s2, [P, 6, T]) for _ in range(2)]
                pt = [sb(s2, [P, 3, T]) for _ in range(2)]
                mh, ml = sb(s2, [P, 8, T], F32R), sb(s2, [P, 8, T], F32R)
                Y = [Act2(yh[i], yl[i], ytok[i]) for i in range(3)]
                gfree, pfree = [None, None], [None, None]
                mt = []
                for mp in range(4):
                    tg = []
                    G = gt[mp % 2]
                    tiles = [np.arange(3008 + D * br + P * m, 3008 + D * br + P * m + P) for m in (2 * mp, 2 * mp + 1) for br in range(3)]
                    for j, out, b, tok, last in feature_tiles("w_in", l, range(8), tiles, H):
                        bg = par_col(f"b_gate{l}", 8 * (j % 3) + 2 * mp + j // 3)
                        tg.append(act(lambda e, j=j, out=out, bg=bg, G=G: e.activation(G[:, j, :], out, ACT.Sigmoid, bias=bg), tok, gfree[mp % 2]))
                        banks.done(b, tg[-1:])
                    gr = []
                    for m2 in range(2):
                        m = 2 * mp + m2
                        Q_ = pt[m % 2]
                        tp = []
                        for br in range(3):
                            u = W.use(["w_br_na", "w_br_mla", "w_br_gqa"][br], l, range(4), np.arange(P * m, P * m + P))
                            b = banks.get()
                            out = banks.tiles[b][:, 0:T]
                            deps = [W.parts_done[u], Y[br].tokens, banks.free[b]]
                            for k in range(4):
                                wh, wl = W.part(u, k, 0, P, False), W.part(u, k, 0, P, True)
                                mm(out, wh, Y[br].hi[:, k, :], k == 0, False, deps if k == 0 else None)
                                mm(out, wh, Y[br].lo[:, k, :], False, False)
                                tok = mm(out, wl, Y[br].hi[:, k, :], False, k == 3, sig=(k == 3))
                            W.done(u, tok)
                            tp.append(dve(lambda e, br=br, out=out, G=G, Q_=Q_, m2=m2: e.tensor_tensor(
                                Q_[:, br, :], out, G[:, 3 * m2 + br, :], ALU.mult), tok, tg, pfree[m % 2]))
                            banks.done(b, tp[-1:])
                        gr += tp
                        t = pool(lambda e, Q_=Q_: e.tensor_tensor(Q_[:, 0, :], Q_[:, 0, :], Q_[:, 1, :], ALU.add), tp)
                        t = pool(lambda e, Q_=Q_: e.tensor_tensor(Q_[:, 0, :], Q_[:, 0, :], Q_[:, 2, :], ALU.add), t)
                        tt = split_act(Q_[:, 0, :], mh[:, m, :], ml[:, m, :], t, eng="pool")
                        pfree[m % 2] = tt
                        mt += tt
                    gfree[mp % 2] = gr
                return residual_add("w_out", l, 8, Act2(mh, ml, mt), 1.0)

    def ffn1(l, x_toks):
        with ExitStack() as s1:
            pr.fence(["act", "dve", "pool"])
            fh, fl = sb(s1, [P, 22, T], F32R), sb(s1, [P, 22, T], F32R)
            hs = sb(s1, [P, 8, T])
            t = rmsnorm(X, 8, f"norm2_g{l}", hs, x_toks)
            H = Act2(Hh, Hl, split_chunks(hs, 8, Hh, Hl, t))
            ab = Ring([sb(s1, [P, 2, T]) for _ in range(3)])
            ft = []
            tiles = []
            for m in range(22):
                tiles += [np.arange(P * m, P * m + P), np.arange(DFF + P * m, DFF + P * m + P)]
            tt = []
            for j, out, b, tok, last in feature_tiles("w_up", l, range(8), tiles, H):
                m, g = j // 2, j % 2
                f = 22 * g + m
                if g == 0:
                    i = ab.get()
                    A = ab.tiles[i]
                    tt = []
                t = act(lambda e, A=A, g=g, out=out, f=f: e.activation(A[:, g, :], out, ACT.Identity, bias=par_col(f"conv_b{l}", f),
                                                                  scale=par_col(f"conv1_{l}", f)), tok, ab.free[i])
                t = dve(lambda e, A=A, g=g, out=out, f=f: e.scalar_tensor_tensor(
                    A[:, g, 1:T], out[:, 0:T - 1], par_col(f"conv0_{l}", f), A[:, g, 1:T], ALU.mult, ALU.add), t)
                t = dve(lambda e, A=A, g=g, out=out, f=f: e.scalar_tensor_tensor(
                    A[:, g, 0:T - 1], out[:, 1:T], par_col(f"conv2_{l}", f), A[:, g, 0:T - 1], ALU.mult, ALU.add), t)
                tt.append(t)
                banks.done(b, [t])
                if g:
                    t = act(lambda e, A=A: e.activation(A[:, 1, :], A[:, 1, :], ACT.Gelu_apprx_tanh), tt)
                    t = dve(lambda e, A=A: e.tensor_tensor(A[:, 0, :], A[:, 0, :], A[:, 1, :], ALU.mult), t)
                    s = split_act(A[:, 0, :], fh[:, m, :], fl[:, m, :], t, eng="pool")
                    ab.free[i] = s
                    ft += s
            return residual_add("w_down", l, 22, Act2(fh, fl, ft), 1.0, kpart=11)

    def split_x(x_toks):
        return Act2(Hh, Hl, split_chunks(X, 8, Hh, Hl, x_toks))

    def mlp2(l, x_toks):
        with ExitStack() as s1:
            pr.fence(["act", "dve", "pool"])
            H = split_x(x_toks)
            fh, fl = sb(s1, [P, 32, T], F32R), sb(s1, [P, 32, T], F32R)
            ring = Ring([sb(s1, [P, T]) for _ in range(4)])
            ft, pend = [], []
            for j, out, b, tok, last in feature_tiles("mlp_w1_2", l, range(8), pieces(0, 4096), H):
                i = ring.get()
                R = ring.tiles[i]
                t = dve(lambda e, R=R, out=out: e.tensor_scalar(R[:, :], out, 0.0, None, ALU.max), tok, ring.free[i])
                pend.append(t)
                banks.done(b, pend[-1:])
                t = act(lambda e, R=R: e.activation(R[:, :], R[:, :], ACT.Square), t)
                s = split_act(R[:, :], fh[:, j, :], fl[:, j, :], t, eng="pool")
                ring.free[i] = s
                ft += s
            return residual_add("mlp_w2_2", l, 32, Act2(fh, fl, ft), ALPHA, kpart=16)

    def ln2(which, l, x_toks):
        with ExitStack() as s1:
            pr.fence(["act", "dve", "pool"])
            sq = sb(s1, [P, 8, T])
            return layernorm(f"ln{which}_g_2{l}", f"ln{which}_b_2{l}", X, sq, x_toks)

    def rwkv_moba(x_toks):
        with ExitStack() as s1:
            pr.fence(["act", "dve", "pool"])
            H = split_x(x_toks)
            yh, yl = sb(s1, [P, 8, T], F32R), sb(s1, [P, 8, T], F32R)
            ytok = []
            with ExitStack() as s2:
                cM = sb(s2, [P, sum(w for _, w in atM.values())])
                pr.fence(["sp"])
                t_cM = pr.op("sp", lambda e: e.dma_start(cM[:, :], dram["cM"]), sem="ld_M", step=16)

                def CM(name):
                    o, w = atM[name]
                    return cM[:, o:o + w]

                S_ring = Ring([sb(s2, [P, 512]) for _ in range(3)])
                T_ring = Ring([sb(s2, [P, 512]) for _ in range(2)])
                small = mk_small(s2)
                Q, K, V = sb(s2, [P, 4, T]), sb(s2, [P, 4, T]), sb(s2, [P, 2, 512])
                raw_ring = Ring([sb(s2, [P, T]) for _ in range(3)])
                tmp_ring = Ring([sb(s2, [P, T]) for _ in range(2)])
                qk_toks, prevt, tv = [], [], []
                for j, out, b, tok, last in feature_tiles("ab_w_in_2", 0, range(8), pieces(1824, 2848), H):
                    i, k = raw_ring.get(), tmp_ring.get()
                    t = act(lambda e, i=i, out=out: e.activation(raw_ring.tiles[i][:, :], out, ACT.Copy), tok, raw_ring.free[i])
                    dst = Q[:, j, :] if j < 4 else K[:, j - 4, :]
                    res = rope([(dst, 0, P)], raw_ring.tiles[i][:, :], CM("cos2"), CM("sin2"), CM("perm2"), tmp_ring.tiles[k][:, :],
                               tmp_ring.free[k], -(128.0 ** -0.5) if j < 4 else 1.0, t, t_cM)
                    raw_ring.free[i] = tmp_ring.free[k] = res
                    qk_toks += res
                    prevt.append(t)
                    banks.done(b, prevt[-1:])
                for c0, b, tok in token_tiles("ab_w_in_2", 0, range(8), np.arange(2848, 3360), H, T):
                    tv.append(act(lambda e, c0=c0, b=b: e.activation(V[:, :, c0:c0 + T], banks.tiles[b][:, :].rearrange("p (a c) -> p a c", a=2), ACT.Copy), tok))
                    banks.done(b, tv[-1:])
                cz = CM("causal")
                heads = []
                for h in range(4):
                    def qk(ps, free, h=h):
                        mm(ps[:, 0:P], Q[:, h, 0:P], K[:, h, 0:P], True, True, [free, qk_toks])
                        return mm(ps[:, P:P + T], Q[:, h, P:T], K[:, h, :], True, True, sig=True)
                    heads.append(dict(qk=[qk], masks=[[cz[:, 0:P], cz[:, T:2 * T]]], widths=[P, T], deps=[t_cM], d=P, base=0,
                                      v=lambda kb, h=h: V[:, kb, P * h:P * h + P], vdeps=tv,
                                      out=(yh[:, 4 + h, :], yl[:, 4 + h, :], ytok), odeps=None))
                run(attention(heads, S_ring, T_ring, small))
            rwkv(H, yh, yl, ytok)
            return residual_add("ab_w_out_2", 0, 8, Act2(yh, yl, ytok), ALPHA)

    def rwkv(H, yh, yl, ytok):
        with ExitStack() as s1:
            pr.fence(["act", "dve", "pool", "sp"])
            bonus = sb(s1, [P, 4, T])
            gate = sb(s1, [P, 4, T])
            AR = sb(s1, [P, 4, 4, 2, 64])
            KH = sb(s1, [P, 4, T])
            BH = sb(s1, [P, 4, T])
            Vt = sb(s1, [P, 2, 512])
            FC = sb(s1, [P, 4, 4])
            v4 = lambda t: t.rearrange("p c (k i) -> p c k i", i=64)
            with ExitStack() as s2:
                Z = sb(s2, [P, 15, T + 1])
                Dz = sb(s2, [P, 15, T])
                lora = sb(s2, [P, 3, 512])
                t_l = pr.op("sp", lambda e: e.dma_start(lora[:, :, :], dram["lora"]), sem="ld_l", step=16)
                t_z0 = pool(lambda e: e.memset(Z[:, :, 0:1], 0.0))
                gcol = np.concatenate([np.arange(1792, 1824), np.full(96, -1)])
                tz = []
                for j, out, b, tok, last in feature_tiles("ab_w_in_2", 0, range(8), pieces(0, 1792) + [gcol], H):
                    if j % 2:
                        tz.append(act(lambda e, j=j, out=out: e.activation(Z[:, j, 1:T + 1], out, ACT.Copy), tok))
                    else:
                        tz.append(dve(lambda e, j=j, out=out: e.tensor_copy(Z[:, j, 1:T + 1], out), tok))
                    banks.done(b, tz[-1:])
                td = []
                for j in range(15):
                    t = dve(lambda e, j=j: e.tensor_tensor(Dz[:, j, :], Z[:, j, 0:T], Z[:, j, 1:T + 1], ALU.subtract), tz[j], t_z0)
                    td.append(dve(lambda e, j=j: e.scalar_tensor_tensor(Z[:, j, 1:T + 1], Dz[:, j, :], par_col("ab_shift_mix_2", j),
                                                                       Z[:, j, 1:T + 1], ALU.mult, ALU.add), t))
                R, K, V = Z[:, 0:4, 1:T + 1], Z[:, 4:8, 1:T + 1], Z[:, 8:12, 1:T + 1]
                sig, aa, cs = Dz[:, 0:4, :], Dz[:, 4:8, :], Dz[:, 8:12, :]
                with ExitStack() as s3:
                    kk = sb(s3, [P, 4, T])
                    ex = sb(s3, [P, 4, T])
                    tw = sb(s3, [P, 3, T])
                    t_w = act(lambda e: e.activation(tw[0:64, 0, :], Z[0:64, 12, 1:T + 1], ACT.Tanh), td)
                    t_g1 = act(lambda e: e.activation(tw[:, 1, :], Z[:, 13, 1:T + 1], ACT.Sigmoid), td)
                    t_g2 = act(lambda e: e.activation(tw[0:32, 2, :], Z[0:32, 14, 1:T + 1], ACT.Sigmoid), td)
                    ts, ta, tg = [], [], []
                    for c in range(4):
                        cc = slice(P * c, P * c + P)
                        b = banks.get()
                        o1, o2 = banks.tiles[b][:, 0:T], banks.tiles[b][:, T:2 * T]
                        t1 = mm(o1, lora[0:64, 0, cc], tw[0:64, 0, :], True, True, [t_w, t_l, banks.free[b]], sig=True)
                        ts.append(act(lambda e, c=c, o1=o1: e.activation(sig[:, c, :], o1, ACT.Sigmoid, bias=par_col("ab_w0_2", c)), t1, td))
                        b2 = banks.get()
                        o2 = banks.tiles[b2][:, 0:T]
                        t2 = mm(o2, lora[64:128, 0, cc], Z[64:128, 12, 1:T + 1], True, True, [td, banks.free[b2]], sig=True)
                        ta.append(act(lambda e, c=c, o2=o2: e.activation(aa[:, c, :], o2, ACT.Sigmoid, bias=par_col("ab_a0_2", c)), t2, td))
                        b3 = banks.get()
                        o3 = banks.tiles[b3][:, 0:T]
                        mm(o3, lora[:, 1, cc], tw[:, 1, :], True, False, [t_g1, t_g2, banks.free[b3]])
                        t3 = mm(o3, lora[0:32, 2, cc], tw[0:32, 2, :], False, True, sig=True)
                        tg.append(dve(lambda e, c=c, o3=o3: e.tensor_copy(gate[:, c, :], o3), t3))
                        banks.done(b, ts[-1:])
                        banks.done(b2, ta[-1:])
                        banks.done(b3, tg[-1:])
                    t_one = pool(lambda e: e.memset(ex[:, :, :], 1.0))
                    t_one = pool(lambda e: e.memset(v4(ex[:, :, :])[:, :, :, 0:1], 0.0), t_one)
                    fl2 = lambda t: t.rearrange("p c t -> p (c t)")
                    t_cs = dve(lambda e: e.tensor_tensor_scan(fl2(cs), fl2(ex[:, :, :]), fl2(sig), 0.0, ALU.mult, ALU.add), t_one, ts, td)
                    cs4, sg4 = v4(cs), v4(sig)
                    mid = sb(s3, [P, 4, 4])
                    end = sb(s3, [P, 4, 4])
                    t_m = dve(lambda e: e.tensor_copy(mid[:, :, :], cs4[:, :, :, 31]), t_cs)
                    for c in range(4):
                        mb = mid[:, c, :].unsqueeze(2).broadcast_to([P, 4, 64])
                        t_c = dve(lambda e, c=c, mb=mb: e.tensor_tensor(cs4[:, c], cs4[:, c], mb, ALU.subtract), t_m)
                    t_e = dve(lambda e: e.tensor_copy(end[:, :, 0:3], cs4[:, :, 0:3, 63]), t_c)
                    t_e = dve(lambda e: e.tensor_tensor(end[:, :, 0:3], end[:, :, 0:3], mid[:, :, 1:4], ALU.add), t_e)
                    t_F = act(lambda e: e.activation(FC[:, :, 0:3], end[:, :, 0:3], ACT.Exp, scale=-KAPPA), t_e)
                    t = act(lambda e: e.activation(ex[:, :, :], cs, ACT.Exp, scale=-KAPPA), t_c, t_cs)
                    ex4 = v4(ex[:, :, :])
                    t_r = []
                    for c in range(4):
                        t_r.append(dve(lambda e, c=c: e.tensor_tensor(AR[:, c, :, 1, :], v4(R)[:, c], ex4[:, c], ALU.mult), t, td))
                    t = dve(lambda e: e.tensor_tensor(sig, cs, sig, ALU.subtract), t_c)
                    t_xa = act(lambda e: e.activation(sig, sig, ACT.Exp, scale=-KAPPA), t)
                    tk = []
                    for c in range(4):
                        tk.append(dve(lambda e, c=c: e.tensor_scalar(kk[:, c, :], K[:, c, :], par_col("ab_k_k_2", c), None, ALU.mult), td))
                    t_sq = act(lambda e: e.activation(ex[:, :, :], kk[:, :, :], ACT.Square), tk, t_r)
                    tn = []
                    for c2 in range(2):
                        b = banks.get()
                        for c in range(2):
                            tok = mm(banks.tiles[b][:, c * T:c * T + T], half, ex[:, 2 * c2 + c, :], True, True, [t_sq, banks.free[b]], sig=True)
                        e2 = ex[:, 2 * c2:2 * c2 + 2, :]
                        t = dve(lambda e, e2=e2, b=b: e.tensor_scalar(e2, banks.tiles[b][:, :].rearrange("p (c t) -> p c t", c=2),
                                                                     1e-24, None, ALU.max), tok)
                        banks.done(b, [t])
                        t = act(lambda e, e2=e2: e.activation(e2, e2, ACT.Sqrt), t)
                        t = dve(lambda e, e2=e2: e.reciprocal(e2, e2), t)
                        tn.append(dve(lambda e, e2=e2, c2=c2: e.tensor_tensor(kk[:, 2 * c2:2 * c2 + 2, :], kk[:, 2 * c2:2 * c2 + 2, :], e2, ALU.mult), t))
                    for c in range(4):
                        t_a = dve(lambda e, c=c: e.scalar_tensor_tensor(AR[:, c, :, 0, :], v4(kk[:, :, :])[:, c], -1.0, sg4[:, c],
                                                                       ALU.mult, ALU.mult), tn, t_xa)
                    t_xk = act(lambda e: e.activation(cs, cs, ACT.Exp, scale=KAPPA), t_e, t_r, t_xa)
                    t = dve(lambda e: e.tensor_tensor(kk[:, :, :], kk[:, :, :], aa, ALU.mult), t_a, ta)
                    t_b = dve(lambda e: e.tensor_tensor(BH[:, :, :], kk[:, :, :], cs, ALU.mult), t, t_xk)
                    tk2 = []
                    for c in range(4):
                        t = dve(lambda e, c=c: e.tensor_scalar(aa[:, c, :], aa[:, c, :], -1.0, par_col("ab_k_a_2", c), ALU.add, ALU.mult), t_b)
                        tk2.append(dve(lambda e, c=c: e.scalar_tensor_tensor(K[:, c, :], aa[:, c, :], 1.0, K[:, c, :], ALU.add, ALU.mult), t, tk))
                    t_k = dve(lambda e: e.tensor_tensor(KH[:, :, :], K, cs, ALU.mult), tk2, t_xk)
                    tb = []
                    for c in range(4):
                        tb.append(dve(lambda e, c=c: e.scalar_tensor_tensor(ex[:, c, :], R[:, c, :], par_col("ab_r_k_2", c), K[:, c, :],
                                                                           ALU.mult, ALU.mult), tk2, tn))
                    t_bon = []
                    for c2 in range(2):
                        b = banks.get()
                        for c in range(2):
                            tok = mm(banks.tiles[b][:, c * T:c * T + T], half, ex[:, 2 * c2 + c, :], True, True, [tb, banks.free[b]], sig=True)
                        t_bon.append(dve(lambda e, c2=c2, b=b: e.tensor_tensor(
                            bonus[:, 2 * c2:2 * c2 + 2, :], banks.tiles[b][:, :].rearrange("p (c t) -> p c t", c=2),
                            V[:, 2 * c2:2 * c2 + 2, :], ALU.mult), tok))
                        banks.done(b, t_bon[-1:])
                    t_vt = turn_tokens(V, Vt, td)
            with ExitStack() as s2:
                pr.fence(["act", "dve", "pool", "sp"])
                cW = sb(s2, [P, sum(w for _, w in atW.values())])
                t_cW = pr.op("sp", lambda e: e.dma_start(cW[:, :], dram["cW"]), sem="ld_W", step=16)

                def CW(name):
                    o, w = atW[name]
                    return cW[:, o:o + w]

                Bt, Kt = sb(s2, [P, 2, 512]), sb(s2, [P, 2, 512])
                NT, RB, AK, RK = (sb(s2, [P, 8, 2, 64]) for _ in range(4))
                XX, XT, YY, ET = (sb(s2, [P, 8, 2, 64]) for _ in range(4))
                SZ = sb(s2, [P, 8, 64])
                Gs = sb(s2, [P, 512])
                Us = sb(s2, [P, 512])
                Yo = sb(s2, [P, 4, T])
                sq = YY[:, :, :, :].rearrange("p (c a) b i -> p c (a b i)", c=4)
                t_bt = turn_tokens(BH[:, :, :], Bt, t_b)
                t_kt = turn_tokens(KH[:, :, :], Kt, t_k)
                strict, incl = CW("strict"), CW("incl")
                tsc = []
                for L, dst, dep in ((BH, (NT, RB), t_b), (KH, (AK, RK), t_k)):
                    for c in range(4):
                        p0, tbk = 64 * (c % 2), c // 2
                        for par2 in range(2):
                            b = banks.get()
                            r0 = 64 * par2
                            for f in range(4):
                                tok = mm(banks.tiles[b][p0:p0 + 64, f * P:f * P + P], L[r0:r0 + 64, f, 64 * c:64 * c + 64],
                                         AR[r0:r0 + 64, f, c, :, :].rearrange("p a i -> p (a i)"), True, True,
                                         [dep, t_a, t_r, banks.free[b]] if f == 0 else None, sig=(f == 3))
                            src = banks.tiles[b][p0:p0 + 64, :].rearrange("p (f a i) -> p f a i", f=4, a=2)
                            ts2 = []
                            for a2, m in ((0, strict), (1, incl)):
                                mk = m[p0:p0 + 64, :].unsqueeze(1).broadcast_to([64, 4, 64])
                                o = dst[a2][p0:p0 + 64, par2:8:2, tbk, :]
                                ts2.append(dve(lambda e, o=o, a2=a2, mk=mk, src=src: e.tensor_tensor(o, src[:, :, a2, :], mk, ALU.mult), tok, t_cW))
                            banks.done(b, ts2)
                            tsc += ts2
                idb = CW("id64").unsqueeze(1).broadcast_to([P, 16, 64])
                flat = lambda t: t[:, :, :, :].rearrange("p h b i -> p (h b) i")

                def products(lhs, rhs, deps):
                    res = []
                    for c in range(4):
                        p0, tbk = 64 * (c % 2), c // 2
                        b = banks.get()
                        for h in range(8):
                            tok = mm(banks.tiles[b][p0:p0 + 64, 64 * h:64 * h + 64], lhs(p0, h, tbk), rhs(p0, h, tbk), True, True,
                                     [deps, banks.free[b]] if h == 0 else None, sig=(h == 7))
                        res.append((c, b, tok, banks.tiles[b][p0:p0 + 64, :].rearrange("p (h i) -> p h i", h=8)))
                    return res

                at = lambda t: (lambda p0, h, tbk: t[p0:p0 + 64, h, tbk, :])
                view = lambda t, c: t[64 * (c % 2):64 * (c % 2) + 64, :, c // 2, :]
                lev = lambda n: CW(f"lev{n}").unsqueeze(1).broadcast_to([P, 16, 64])
                t_e = pool(lambda e: e.tensor_tensor(flat(ET), flat(NT), lev(0), ALU.mult), tsc, t_cW)
                ident64 = CW("id64")
                t_xt = dve(lambda e: e.tensor_tensor(flat(XT), flat(ET), idb, ALU.add), t_e)
                t_x = []
                for c, b, tok, ps in products(at(ET), lambda p0, h, tbk: ident64[p0:p0 + 64, :], [t_e]):
                    p0 = 64 * (c % 2)
                    ib = ident64[p0:p0 + 64, :].unsqueeze(1).broadcast_to([64, 8, 64])
                    t = dve(lambda e, c=c, ps=ps, ib=ib: e.tensor_tensor(view(XX, c), ps, ib, ALU.add), tok)
                    t_x.append(t)
                    banks.done(b, [t])
                t_x = [t_x, t_xt]
                for n in range(1, 6):
                    t_e = pool(lambda e, n=n: e.tensor_tensor(flat(ET), flat(NT), lev(n), ALU.mult), pr.last("pe"), t_xt)
                    ty = []
                    for c, b, tok, ps in products(at(ET), at(XX), [t_e, t_x]):
                        t = act(lambda e, c=c, ps=ps: e.activation(view(YY, c), ps, ACT.Copy), tok)
                        ty.append(t)
                        banks.done(b, [t])
                    r1 = products(at(XT), at(YY), [ty])
                    r2 = products(at(YY), at(XT), [])
                    pe_all = pr.last("pe")
                    t_x = []
                    for dst, rr in ((XX, r1), (XT, r2)):
                        for c, b, tok, ps in rr:
                            t = dve(lambda e, c=c, ps=ps, dst=dst: e.tensor_tensor(view(dst, c), view(dst, c), ps, ALU.add), pe_all)
                            t_x.append(t)
                            banks.done(b, [t])
                t_s = pool(lambda e: e.memset(SZ[:, :, :], 0.0))
                t_yo = []
                free_g = None
                for c in range(4):
                    p0, tbk = 64 * (c % 2), c // 2
                    rows = slice(p0, p0 + 64)
                    b = banks.get()
                    for h in range(8):
                        o = banks.tiles[b][rows, 64 * h:64 * h + 64]
                        mm(o, AR[:, h // 2, c, 0, :], SZ[:, h, :], True, False, [t_s, t_vt, banks.free[b]])
                        tok = mm(o, AK[rows, h, tbk, :], Vt[rows, tbk, 64 * h:64 * h + 64], False, True, sig=True)
                    t_g = act(lambda e, b=b, rows=rows: e.activation(Gs[rows, :], banks.tiles[b][rows, :], ACT.Copy), tok)
                    banks.done(b, [t_g])
                    b = banks.get()
                    for h in range(8):
                        tok = mm(banks.tiles[b][rows, 64 * h:64 * h + 64], XT[rows, h, tbk, :], Gs[rows, 64 * h:64 * h + 64], True, True,
                                 [t_g, t_x, banks.free[b]], sig=True)
                    t_u = act(lambda e, b=b, rows=rows: e.activation(Us[rows, :], banks.tiles[b][rows, :], ACT.Copy), tok)
                    banks.done(b, [t_u])
                    if c < 3:
                        b = banks.get()
                        for h in range(8):
                            o = banks.tiles[b][64 * (h % 2):64 * (h % 2) + 64, 64 * (h // 2):64 * (h // 2) + 64]
                            mm(o, Bt[rows, tbk, 64 * h:64 * h + 64], Us[rows, 64 * h:64 * h + 64], True, False, [t_u, t_bt, t_kt, banks.free[b]])
                            tok = mm(o, Kt[rows, tbk, 64 * h:64 * h + 64], Vt[rows, tbk, 64 * h:64 * h + 64], False, True, sig=True)
                        bs, tok_s = b, tok
                    b = banks.get()
                    for h in range(8):
                        o = banks.tiles[b][64 * (h % 2):64 * (h % 2) + 64, 64 * (h // 2):64 * (h // 2) + 64]
                        mm(o, SZ[:, h, :], AR[:, h // 2, c, 1, :], True, False, [t_u, banks.free[b]])
                        mm(o, Us[rows, 64 * h:64 * h + 64], RB[rows, h, tbk, :], False, False)
                        tok = mm(o, Vt[rows, tbk, 64 * h:64 * h + 64], RK[rows, h, tbk, :], False, True, sig=True)
                    t = act(lambda e, b=b, c=c: e.activation(Yo[:, :, 64 * c:64 * c + 64], banks.tiles[b][:, 0:T].rearrange("p (f i) -> p f i", f=4), ACT.Copy), tok)
                    banks.done(b, [t])
                    t_yo.append(t)
                    if c < 3:
                        t_s = []
                        for par2 in range(2):
                            r = slice(64 * par2, 64 * par2 + 64)
                            st = SZ[r, par2:8:2, :]
                            ps = banks.tiles[bs][r, 0:T].rearrange("p (f i) -> p f i", f=4)
                            t1 = dve(lambda e, st=st, ps=ps: e.tensor_tensor(st, st, ps, ALU.add), tok_s, tok)
                            fb = FC[r, :, c:c + 1].broadcast_to([64, 4, 64])
                            t_s.append(dve(lambda e, st=st, fb=fb: e.tensor_tensor(st, st, fb, ALU.mult), t1, t_F))
                            if par2:
                                banks.done(bs, [t1, t_s[0]])
                mus = Gs[:, :].rearrange("p (c t) -> p c t", c=2)
                for c2 in range(2):
                    yv = Yo[:, 2 * c2:2 * c2 + 2, :]
                    b = banks.get()
                    for c in range(2):
                        tok = mm(banks.tiles[b][:, c * T:c * T + T], half, Yo[:, 2 * c2 + c, :], True, True, [t_yo, banks.free[b]], sig=True)
                    ps = banks.tiles[b][:, :].rearrange("p (c t) -> p c t", c=2)
                    t = dve(lambda e, yv=yv, ps=ps: e.scalar_tensor_tensor(yv, ps, -1.0 / 64, yv, ALU.mult, ALU.add), tok)
                    banks.done(b, [t])
                    t2 = act(lambda e, yv=yv, c2=c2: e.activation(sq[:, 2 * c2:2 * c2 + 2, :], yv, ACT.Square), t)
                    b = banks.get()
                    for c in range(2):
                        tok = mm(banks.tiles[b][:, c * T:c * T + T], half, sq[:, 2 * c2 + c, :], True, True, [t2, banks.free[b]], sig=True)
                    ps = banks.tiles[b][:, :].rearrange("p (c t) -> p c t", c=2)
                    t3 = act(lambda e, ps=ps, c2=c2: e.activation(sq[:, 2 * c2:2 * c2 + 2, :], ps, ACT.Sqrt, bias=eps_gn, scale=1.0 / 64), tok)
                    banks.done(b, [t3])
                    t3 = dve(lambda e, c2=c2: e.reciprocal(sq[:, 2 * c2:2 * c2 + 2, :], sq[:, 2 * c2:2 * c2 + 2, :]), t3)
                    t3 = dve(lambda e, c2=c2, yv=yv: e.tensor_tensor(yv, yv, sq[:, 2 * c2:2 * c2 + 2, :], ALU.mult), t3)
                    for c in range(2):
                        f = 2 * c2 + c
                        y1 = Yo[:, f, :]
                        t4 = dve(lambda e, y1=y1, f=f: e.tensor_scalar(y1, y1, par_col("ab_lnx_g_2", f), par_col("ab_lnx_b_2", f), ALU.mult, ALU.add), t3)
                        t4 = dve(lambda e, y1=y1, f=f: e.tensor_tensor(y1, y1, bonus[:, f, :], ALU.add), t4, t_bon)
                        t4 = dve(lambda e, y1=y1, f=f: e.tensor_tensor(y1, y1, gate[:, f, :], ALU.mult), t4, tg)
                        ytok += split_act(y1, yh[:, f, :], yl[:, f, :], t4)

    def turn_tokens(src, dst, dep):
        res = []
        for tb in range(2):
            b = banks.get()
            first = [dep, banks.free[b]]
            for c in range(4):
                o, s = banks.tiles[b][:, c * P:c * P + P], src[:, c, tb * P:tb * P + P]
                tok = pr.op("pe", lambda e, o=o, s=s: e.transpose(o, s, ident), first, sig=True)
                first = None
            t = act(lambda e, tb=tb, b=b: e.activation(dst[:, tb, :], banks.tiles[b][:, :], ACT.Copy), tok)
            banks.done(b, [t])
            res.append(t)
        return res

    def dilated(x_toks):
        with ExitStack() as s1:
            pr.fence(["act", "dve", "pool", "sp"])
            H = split_x(x_toks)
            cD = sb(s1, [P, sum(w for _, w in atD.values())])
            t_cD = pr.op("sp", lambda e: e.dma_start(cD[:, :], dram["cD"]), sem="ld_D", step=16)

            def CD(name):
                o, w = atD[name]
                return cD[:, o:o + w]

            yh, yl = sb(s1, [P, 8, T], F32R), sb(s1, [P, 8, T], F32R)
            ytok = []
            S_ring = Ring([sb(s1, [P, 384]) for _ in range(9)])
            T_ring = Ring([sb(s1, [P, 384]) for _ in range(2)])
            small = mk_small(s1)
            raw_ring = Ring([sb(s1, [P, T]) for _ in range(3)])
            tmp_ring = Ring([sb(s1, [P, T]) for _ in range(2)])
            Q, K, V = sb(s1, [P, 12, T]), sb(s1, [P, 4, T]), sb(s1, [P, 2, 512])
            free = None
            for hg in range(2):
                tiles = []
                for h in range(4 * hg, 4 * hg + 4):
                    for g in range(4):
                        tiles.append(np.arange(D * g + P * h, D * g + P * h + P))
                tq, prevt, tv = [], [], []
                for j, out, b, tok, last in feature_tiles("c_w_in_2", 0, range(8), tiles, H):
                    i, k = raw_ring.get(), tmp_ring.get()
                    t = act(lambda e, i=i, out=out: e.activation(raw_ring.tiles[i][:, :], out, ACT.Copy), tok, raw_ring.free[i])
                    h, g = j // 4, j % 4
                    dst = Q[:, 3 * h + g, :] if g < 3 else K[:, h, :]
                    res = rope([(dst, 0, P)], raw_ring.tiles[i][:, :], CD("cos2"), CD("sin2"), CD("perm2"), tmp_ring.tiles[k][:, :],
                               tmp_ring.free[k], -(128.0 ** -0.5) if g < 3 else 1.0, t, t_cD, free)
                    raw_ring.free[i] = tmp_ring.free[k] = res
                    tq += res
                    prevt.append(t)
                    banks.done(b, prevt[-1:])
                for c0, b, tok in token_tiles("c_w_in_2", 0, range(8), np.arange(4 * D + 512 * hg, 4 * D + 512 * hg + 512), H, T):
                    tv.append(act(lambda e, c0=c0, b=b: e.activation(V[:, :, c0:c0 + T], banks.tiles[b][:, :].rearrange("p (a c) -> p a c", a=2), ACT.Copy), tok, free))
                    banks.done(b, tv[-1:])
                heads = []
                for h in range(4):
                    def qk(ps, fr, h, g):
                        mm(ps[:, 0:P], Q[:, 3 * h + g, 0:P], K[:, h, 0:P], True, True, [fr, tq])
                        return mm(ps[:, P:P + T], Q[:, 3 * h + g, P:T], K[:, h, :], True, True, sig=True)
                    heads.append(dict(qk=[lambda ps, fr, h=h, g=g: qk(ps, fr, h, g) for g in range(3)],
                                      masks=[[CD(f"dil{g}")[:, 0:P], CD(f"dil{g}")[:, T:2 * T]] for g in range(3)], widths=[P, T],
                                      deps=[t_cD], d=P, base=0, v=lambda kb, h=h: V[:, kb, P * h:P * h + P], vdeps=tv,
                                      out=(yh[:, 4 * hg + h, :], yl[:, 4 * hg + h, :], ytok), odeps=None))
                run(attention(heads, S_ring, T_ring, small))
                free = [pr.last("pe")]
            return residual_add("c_w_out_2", 0, 8, Act2(yh, yl, ytok), ALPHA)

    with top:
        xt = [t_x]
        for l in range(2):
            xt = mixer1(l, xt)
            xt = ffn1(l, xt)
        with ExitStack() as s1:
            pr.fence(["act", "dve", "pool"])
            fin = sb(s1, [P, 8, T])
            t = rmsnorm(X, 8, "final_g", fin, xt)
            xt = [dve(lambda e: e.tensor_copy(X[:, :, :], fin[:, :, :]), t)]
        for l in range(2):
            xt = rwkv_moba(xt) if l == 0 else dilated(xt)
            xt = ln2(1, l, xt)
            xt = mlp2(l, xt)
            xt = ln2(2, l, xt)
        t_out = pr.op("sp", lambda e: e.dma_start(dram["out"], X[:, :, :]), [xt], sem="st", step=16)
        pr.op("sp", None, [t_out], sig=False)

        if specs is not None:
            assert W.specs == specs
            sems = {s: top.enter_context(nc.semaphore(f"s_{s}")) for s in sorted(pr.count)}
            block = top.enter_context(nc.Block())

            def play(e, name):
                for waits, fn, s, step in pr.q[name]:
                    for ws, wv in waits:
                        e.wait_ge(sems[ws], wv)
                    if fn is not None:
                        ins = fn(e)
                        if s is not None:
                            ins.then_inc(sems[s], step)

            block.sync(lambda e: play(e, "sp"))
            block.tensor(lambda e: play(e, "pe"))
            block.vector(lambda e: play(e, "dve"))
            block.scalar(lambda e: play(e, "act"))
            block.gpsimd(lambda e: play(e, "pool"))
    return W.specs


def lay_unit(inputs, spec):
    name, layer, rows, cols = spec
    a = inputs[name][layer]
    cols = np.array(cols)
    parts = []
    for k in rows:
        block = np.zeros((P, len(cols)), a.dtype)
        block[:, cols >= 0] = a[k * P:(k + 1) * P, cols[cols >= 0]]
        parts.append(block)
    return np.concatenate(parts, axis=1).reshape(-1)


def lay_params(inputs):
    cols = []
    for key, name, idx in param_list():
        v = inputs[name][idx].reshape(-1)
        w = -(-v.size // P)
        pad = np.zeros(w * P, v.dtype)
        pad[:v.size] = v
        cols.append(pad.reshape(w, P).T)
    for l in range(2):
        cols.append(np.broadcast_to(inputs["gqa_sink"][l][None, :], (P, 8)))
    return np.ascontiguousarray(np.concatenate(cols, axis=1))


def lay_bias(rpb):
    out = np.zeros((2, 64, 8, 7, 64), rpb.dtype)
    for c in range(64):
        k = np.arange(max(0, c - 15), min(64, c + 16))
        out[:, c, :, :, k] = np.moveaxis(rpb[:, :, 4:11, k - c + 15], 3, 0)
    return out


def kernel(**inputs):
    import concourse.bacc as bacc
    from concourse.bass_utils import run_bass_kernel_spmd as run

    inputs = {k: np.asarray(v) for k, v in inputs.items()}
    c = shape_constants()
    packs = [pack(n, c) for n in (CONST1, CONST_A, CONST_M, CONST_W, CONST_D)]
    atP = param_places()
    places = [p[0] for p in packs] + [atP]

    scratch = bacc.Bacc("TRN2", target_bir_lowering=False, num_devices=1)

    def tensors(nc, total):
        shapes = {"x": (P, 8, T), "c1": packs[0][1].shape, "cA": packs[1][1].shape, "cM": packs[2][1].shape,
                  "cW": packs[3][1].shape, "cD": packs[4][1].shape, "par": (P, atP[1]), "w": (total,),
                  "rpb": (2, 64, 8, 7, 64), "lora": (P, 3, 512)}
        d = {k: nc.dram_tensor(f"in_{k}", s, F32, kind="ExternalInput").ap() for k, s in shapes.items()}
        d["out"] = nc.dram_tensor("out_0", (P, 8, T), F32, kind="ExternalOutput").ap()
        return d

    specs = program(scratch, tensors(scratch, P), places, None, [])
    offsets, total = [], 0
    for _, _, rows, cols in specs:
        offsets.append(total)
        total += P * len(rows) * len(cols)
    nc = bacc.Bacc("TRN2", target_bir_lowering=False, num_devices=1)
    program(nc, tensors(nc, total), places, specs, offsets)

    lora = np.zeros((P, 3, 512), np.float32)
    lora[0:64, 0] = inputs["ab_w_up_2"][0]
    lora[64:128, 0] = inputs["ab_a_up_2"][0]
    lora[:, 1] = inputs["ab_g_up_2"][0][0:128]
    lora[0:32, 2] = inputs["ab_g_up_2"][0][128:160]
    feed = {"in_x": np.ascontiguousarray(inputs["x"][0].T.reshape(8, P, T).transpose(1, 0, 2)),
            "in_c1": packs[0][1], "in_cA": packs[1][1], "in_cM": packs[2][1], "in_cW": packs[3][1], "in_cD": packs[4][1],
            "in_par": lay_params(inputs), "in_rpb": lay_bias(inputs["na_rpb"]), "in_lora": lora,
            "in_w": np.concatenate([lay_unit(inputs, s) for s in specs])}
    got = run(nc, [feed], core_ids=[0]).results[0]["out_0"]
    return np.ascontiguousarray(got.transpose(1, 0, 2).reshape(D, T).T)[None]
```

```python
from contextlib import ExitStack

import numpy as np
import concourse.bass as bass
from concourse import mybir

F32 = mybir.dt.float32
F32R = mybir.dt.float32r
ALU = mybir.AluOpType
ACT = mybir.ActivationFunctionType
AX = mybir.AxisListType

P = 128
T = 256
D = 1024
DFF = 2816
BIG = 1e30
KAPPA = float(np.exp(np.float32(-0.5)))
ALPHA = float(4.0 ** 0.25)
UNIT = 2048
NRAW, NHI, NLO, AHEAD_HI, AHEAD_LO = 4, 4, 3, 3, 2


def shape_constants():
    i = np.arange(P)
    tok = np.arange(T)
    c = {}
    c["ident"] = np.eye(P)
    c["ones"] = np.ones((P, P))
    c["half"] = (i[:, None] // 64 == i[None, :] // 64) * 1.0

    def rope(dim, rot, theta, width):
        half = rot // 2
        f = i % width
        if dim == rot:
            inv = 1.0 / (np.float32(theta) ** (np.arange(0, dim, 2, dtype=np.float32) / np.float32(dim)))
        else:
            inv = np.float32(theta) ** (-np.arange(half, dtype=np.float32) / np.float32(half))
        ang = tok.astype(np.float32)[None, :] * inv.astype(np.float32)[f % half][:, None]
        cs = np.where((f < rot)[:, None], np.cos(ang), 1.0)
        sn = np.where((f < rot)[:, None], np.sin(ang), 0.0)
        perm = np.zeros((P, P))
        for m in range(P):
            if f[m] < half:
                perm[m + half, m] = -1.0
            elif f[m] < rot:
                perm[m - half, m] = 1.0
        return cs, sn, perm

    c["cos1"], c["sin1"], c["perm1"] = rope(64, 64, 10000.0, 64)
    c["cos2"], c["sin2"], c["perm2"] = rope(128, 32, 500000.0, 128)
    cq = np.arange(64)
    start = np.clip(cq - 8, 0, 48)
    inside = (cq[None, :] >= start[:, None]) & (cq[None, :] < start[:, None] + 16)
    c["namask"] = np.tile(np.where(inside, 0.0, BIG), (2, 1))

    def both(ok):
        m = np.where(ok, 0.0, BIG)
        return np.concatenate([m[0:P], m[P:T]], axis=1)

    q, k = tok[:, None], tok[None, :]
    c["gmask"] = both(np.abs(q - k) <= 128)
    c["causal"] = both(k <= q)
    c["dil0"] = both((k <= q) & (q - k <= 128))
    c["dil1"] = both((k <= q) & ((q - k) % 4 == 0))
    c["dil2"] = both((k <= q) & ((q - k) % 16 == 0))
    a = i % 64
    j = np.arange(64)
    for n in range(6):
        m = 1 << n
        t, s = j[None, :], a[:, None]
        c[f"lev{n}"] = ((t // (2 * m) == s // (2 * m)) & (t % (2 * m) >= m) & (s % (2 * m) < m)) * 1.0
    c["strict"] = (j[None, :] > a[:, None]) * 1.0
    c["incl"] = (j[None, :] >= a[:, None]) * 1.0
    c["id64"] = (j[None, :] == a[:, None]) * 1.0
    c["eps"] = np.tile(np.array([[1e-6, 1e-5, 64e-5, 0.0]]), (P, 1))
    return c


CONST1 = ["ident", "ones", "half", "eps"]
CONST_A = ["cos1", "sin1", "perm1", "namask", "gmask"]
CONST_M = ["cos2", "sin2", "perm2", "causal"]
CONST_W = ["lev0", "lev1", "lev2", "lev3", "lev4", "lev5", "strict", "incl", "id64"]
CONST_D = ["cos2", "sin2", "perm2", "dil0", "dil1", "dil2"]


def pack(names, c):
    at, cols, n = {}, [], 0
    for name in names:
        at[name] = (n, c[name].shape[1])
        cols.append(c[name])
        n += c[name].shape[1]
    return at, np.ascontiguousarray(np.concatenate(cols, axis=1).astype(np.float32))


def param_list():
    out = []
    for l in range(2):
        for name in ("norm1_g", "b_gate", "mla_qa_g", "mla_kva_g", "norm2_g", "conv_b"):
            out.append((f"{name}{l}", name, (l,)))
        for t in range(3):
            out.append((f"conv{t}_{l}", "conv_w", (l, t)))
        for name in ("ln1_g_2", "ln1_b_2", "ln2_g_2", "ln2_b_2"):
            out.append((f"{name}{l}", name, (l,)))
    out.append(("final_g", "final_g", ()))
    for name in ("ab_shift_mix_2", "ab_w0_2", "ab_a0_2", "ab_k_k_2", "ab_k_a_2", "ab_r_k_2", "ab_lnx_g_2", "ab_lnx_b_2"):
        out.append((name, name, (0,)))
    return out


PARAM_LEN = {"norm1_g": 1024, "b_gate": 3072, "mla_qa_g": 384, "mla_kva_g": 256, "norm2_g": 1024, "conv_b": 5632,
             "conv_w": 5632, "ln1_g_2": 1024, "ln1_b_2": 1024, "ln2_g_2": 1024, "ln2_b_2": 1024, "final_g": 1024,
             "ab_shift_mix_2": 1824, "ab_w0_2": 512, "ab_a0_2": 512, "ab_k_k_2": 512, "ab_k_a_2": 512,
             "ab_r_k_2": 512, "ab_lnx_g_2": 512, "ab_lnx_b_2": 512}


def param_places():
    at, n = {}, 0
    for key, name, _ in param_list():
        w = -(-PARAM_LEN[name] // P)
        at[key] = n
        n += w
    at["sink0"] = n
    at["sink1"] = n + 8
    return at, n + 16


class Prog:

    ENGINES = ("pe", "dve", "act", "pool", "sp")

    def __init__(self):
        self.q = {e: [] for e in self.ENGINES}
        self.count = {}
        self.seen = {e: {} for e in self.ENGINES}
        self.extra = {e: [] for e in self.ENGINES}

    def waits(self, e, deps):
        need = {}
        stack = [deps, self.extra[e]]
        while stack:
            x = stack.pop()
            if x is None:
                continue
            if isinstance(x, list):
                stack.extend(x)
            else:
                need[x[0]] = max(need.get(x[0], 0), x[1])
        self.extra[e] = []
        out = []
        for s, v in need.items():
            if self.seen[e].get(s, 0) < v:
                self.seen[e][s] = v
                out.append((s, v))
        return out

    def op(self, e, fn, deps=None, sig=True, sem=None, step=1):
        w = self.waits(e, [deps])
        s = sem or e
        self.q[e].append((w, fn, s if sig else None, step))
        if sig:
            self.count[s] = self.count.get(s, 0) + step
            return (s, self.count[s])
        return None

    def last(self, e):
        return (e, self.count[e]) if self.count.get(e) else None

    def fence(self, engines, after=("pe", "dve", "act", "pool")):
        tokens = [self.last(x) for x in after]
        for e in engines:
            self.extra[e] = self.extra[e] + tokens


class Banks:

    def __init__(self, tiles):
        self.tiles = tiles
        self.free = [[] for _ in tiles]
        self.open = [False] * len(tiles)
        self.sets = {}
        self.n = {}

    def assign(self, **sets):
        self.sets = sets
        self.n = {k: 0 for k in sets}

    def get(self, kind="lin"):
        ring = self.sets[kind]
        b = ring[self.n[kind] % len(ring)]
        self.n[kind] += 1
        assert not self.open[b], "PSUM bank still in use"
        self.open[b] = True
        return b

    def done(self, b, tokens):
        self.free[b] = tokens
        self.open[b] = False

    def done_stat(self, tokens):
        self.free[7] = tokens


class Weights:

    def __init__(self, pr, specs):
        self.pr, self.specs, self.known = pr, [], specs
        self.n = self.hi_to = self.lo_to = self.loaded = 0
        self.pe_done, self.hi_done, self.parts_done, self.raw_done = {}, {}, {}, {}

    def start(self, dram, raw, hi, lo, offsets):
        self.dram, self.raw, self.hi, self.lo, self.offsets = dram, raw, hi, lo, offsets
        for _ in range(min(NRAW, len(self.known or []))):
            self.load()

    def width(self, u):
        name, layer, rows, cols = self.known[u]
        return len(rows) * len(cols)

    def load(self):
        u = self.loaded
        if u >= len(self.known):
            return
        self.loaded += 1
        n = self.width(u)
        src = self.dram[self.offsets[u]:self.offsets[u] + P * n].rearrange("(p n) -> p n", p=P)
        dst = self.raw[u % NRAW][:, 0:n]
        self.raw_done[u] = self.pr.op("sp", lambda e: e.dma_start(dst, src),
                                      [self.parts_done.get(u - NRAW)], sem=f"w{u % NRAW}", step=16)

    def split_hi(self, u):
        n = self.width(u)
        raw, hi = self.raw[u % NRAW][:, 0:n], self.hi[u % NHI][:, 0:n]
        self.hi_done[u] = self.pr.op("act", lambda e: e.activation(hi, raw, ACT.Copy), [self.raw_done[u], self.pe_done.get(u - NHI)])

    def split_lo(self, u):
        n = self.width(u)
        raw, hi, lo = self.raw[u % NRAW][:, 0:n], self.hi[u % NHI][:, 0:n], self.lo[u % NLO][:, 0:n]
        t = self.pr.op("dve", lambda e: e.tensor_tensor(lo, raw, hi.bitcast(F32), ALU.subtract),
                       [self.hi_done[u], self.raw_done[u], self.pe_done.get(u - NLO)])
        self.parts_done[u] = [self.hi_done[u], t]
        self.load()

    def use(self, name, layer, rows, cols):
        u = self.n
        self.n += 1
        self.specs.append((name, layer, tuple(rows), tuple(int(c) for c in cols)))
        assert u == 0 or u - 1 in self.pe_done, "weight units are used one after another"
        self.ahead(u)
        if not self.known:
            self.parts_done[u] = []
        return u

    def ahead(self, u):
        if self.known:
            while self.hi_to < min(u + AHEAD_HI + 1, len(self.known)) or self.lo_to < min(u + AHEAD_LO + 1, len(self.known)):
                if self.hi_to < len(self.known):
                    self.split_hi(self.hi_to)
                    self.hi_to += 1
                if self.lo_to < self.hi_to - (AHEAD_HI - AHEAD_LO) or self.hi_to == len(self.known):
                    self.split_lo(self.lo_to)
                    self.lo_to += 1

    def first(self):
        if self.known:
            self.split_hi(0)
            self.split_lo(0)
            self.hi_to = self.lo_to = 1

    def part(self, u, k, c0, c1, low):
        nc = len(self.specs[u][3])
        t = (self.lo if low else self.hi)[u % (NLO if low else NHI)]
        return t[:, k * nc + c0:k * nc + c1]

    def done(self, u, token):
        self.pe_done[u] = token


def program(nc, dram, places, specs, offsets):
    tag = "a" if specs is None else "b"
    pr = Prog()
    W = Weights(pr, specs)
    names = [0]
    at1, atA, atM, atW, atD, atP = places
    top = ExitStack()

    def sb(ctx, shape, dt=F32):
        names[0] += 1
        return ctx.enter_context(nc.sbuf_tensor(f"{tag}{names[0]}", shape, dt))

    def op(e, fn, *deps):
        return pr.op(e, fn, list(deps))

    def dve(fn, *deps):
        return pr.op("dve", fn, list(deps))

    def act(fn, *deps):
        return pr.op("act", fn, list(deps))

    def pool(fn, *deps):
        return pr.op("pool", fn, list(deps))

    def mm(out, lhsT, rhs, start, stop, deps=None, sig=False):
        return pr.op("pe", lambda e: e.matmul(out, lhsT, rhs, start=start, stop=stop), deps, sig=sig)

    banks = Banks([top.enter_context(nc.psum_tensor(f"{tag}ps{b}", [P, 512], F32)) for b in range(8)])
    raw = [sb(top, [P, UNIT]) for _ in range(NRAW)]
    whi = [sb(top, [P, UNIT], F32R) for _ in range(NHI)]
    wlo = [sb(top, [P, UNIT], F32R) for _ in range(NLO)]
    X = sb(top, [P, 8, T])
    Hh = sb(top, [P, 8, T], F32R)
    Hl = sb(top, [P, 8, T], F32R)
    c1 = sb(top, [P, sum(w for _, w in at1.values())])
    par = sb(top, [P, atP[1]])
    shift = sb(top, [P, T])
    nst = sb(top, [P, 16])
    STAT = 7
    banks.assign(lin=list(range(7)), att=list(range(7)))

    def C(name, a=0, b=None):
        o, w = at1[name]
        return c1[:, o + a:o + (w if b is None else b)]

    def par_col(key, j=0):
        o = atP[0][key] + j
        return par[:, o:o + 1]

    ident, ones, half = C("ident"), C("ones"), C("half")
    eps_rms, eps_ln, eps_gn = C("eps", 0, 1), C("eps", 1, 2), C("eps", 2, 3)

    t_x = pr.op("sp", lambda e: e.dma_start(X[:, :, :], dram["x"]), sem="ld_x", step=16)
    t_c1 = pr.op("sp", lambda e: e.dma_start(c1[:, :], dram["c1"]), sem="ld_c", step=16)
    t_par = pr.op("sp", lambda e: e.dma_start(par[:, :], dram["par"]), sem="ld_p", step=16)
    W.start(dram["w"], raw, whi, wlo, offsets)
    for e in ("pe", "act", "dve", "pool"):
        pr.extra[e] = [t_c1, t_par]

    class Ring:
        def __init__(self, tiles):
            self.tiles, self.free, self.n = tiles, [None] * len(tiles), 0

        def get(self):
            i = self.n % len(self.tiles)
            self.n += 1
            return i

    scr = Ring([sb(top, [P, T]) for _ in range(4)])

    class Act2:

        def __init__(self, hi, lo, toks):
            self.hi, self.lo, self.toks = hi, lo, toks

    def split_act(src, hi, lo, *deps, eng="dve"):
        t1 = act(lambda e: e.activation(hi, src, ACT.Copy), *deps)
        t2 = op(eng, lambda e: e.tensor_tensor(lo, src, hi.bitcast(F32), ALU.subtract), t1, *deps)
        return [t1, t2]

    def feature_tiles(name, layer, rows, tile_cols, x, per_unit=None, kpart=None, xk=None, together=False):
        nk = len(rows)
        xk = xk or list(range(nk))
        kpart = kpart or nk
        per_unit = per_unit or max(1, UNIT // (kpart * P))
        n = len(tile_cols)
        b = None
        for j in range(0, n, per_unit):
            g = list(range(j, min(j + per_unit, n)))
            cols = np.concatenate([tile_cols[i] for i in g])
            parts = [list(range(a, min(a + kpart, nk))) for a in range(0, nk, kpart)]
            assert len(parts) == 1 or len(g) == 1
            for pi, ks in enumerate(parts):
                u = W.use(name, layer, [rows[k] for k in ks], cols)
                if together and j == 0:
                    bs = [banks.get() for _ in g]
                    for k in ks:
                        for gi, b in enumerate(bs):
                            out = banks.tiles[b][:, 0:T]
                            wh, wl = W.part(u, k, gi * P, gi * P + P, False), W.part(u, k, gi * P, gi * P + P, True)
                            mm(out, wh, x.hi[:, xk[k], :], k == 0, False, [W.parts_done[u], banks.free[b], x.toks[xk[k]]])
                            mm(out, wl, x.hi[:, xk[k], :], False, False)
                            tok = mm(out, wh, x.lo[:, xk[k], :], False, k == nk - 1, sig=True)
                    W.done(u, tok)
                    for i, b in zip(g, bs):
                        yield i, banks.tiles[b][:, 0:T], b, tok
                    continue
                for gi, i in enumerate(g):
                    if pi == 0:
                        b = banks.get()
                    out = banks.tiles[b][:, 0:T]
                    deps = [W.parts_done[u], banks.free[b]]
                    for q, k in enumerate(ks):
                        first, last = k == 0, k == nk - 1
                        wh = W.part(u, q, gi * P, gi * P + P, False)
                        wl = W.part(u, q, gi * P, gi * P + P, True)
                        mm(out, wh, x.hi[:, xk[k], :], first, False, [deps if q == 0 else None, x.toks[xk[k]]])
                        mm(out, wh, x.lo[:, xk[k], :], False, False)
                        tok = mm(out, wl, x.hi[:, xk[k], :], False, last, sig=(q == len(ks) - 1))
                    if gi == len(g) - 1:
                        W.done(u, tok)
                    if pi == len(parts) - 1:
                        yield i, out, b, tok

    def project(name, layer, rows, tile_cols, x, evac, **kw):
        for j, out, b, tok in feature_tiles(name, layer, rows, tile_cols, x, **kw):
            banks.done(b, evac(j, out, tok))
            yield

    def by_token(name, layer, rows, cols, x, width, dst, tokens, *deps):
        nk = len(rows)
        for c0 in range(0, len(cols), width):
            cc = cols[c0:c0 + width]
            w = len(cc)
            u = W.use(name, layer, rows, cc)
            b = banks.get()
            for tb in range(2):
                out = banks.tiles[b][:, tb * w:tb * w + w]
                first = [W.parts_done[u], banks.free[b]]
                for k in range(nk):
                    xh, xl = x.hi[:, k, tb * P:tb * P + P], x.lo[:, k, tb * P:tb * P + P]
                    mm(out, xh, W.part(u, k, 0, w, False), k == 0, False, [first if k == 0 else None, x.toks[k]])
                    mm(out, xl, W.part(u, k, 0, w, False), False, False)
                    tok = mm(out, xh, W.part(u, k, 0, w, True), False, k == nk - 1, sig=(k == nk - 1))
            W.done(u, tok)
            d, s_ = dst[:, :, c0:c0 + w], banks.tiles[b][:, 0:2 * w].rearrange("p (a c) -> p a c", a=2)
            t = act(lambda e, d=d, s_=s_: e.activation(d, s_, ACT.Copy), tok, *deps)
            tokens.append(t)
            banks.done(b, [t])
            yield

    def pieces(a, b):
        return [np.arange(c, c + P) for c in range(a, b, P)]

    def run(*gens):
        for g in gens:
            for _ in g:
                pass

    def chain(*gens):
        for g in gens:
            yield from g

    def weave(main, filler, per_step):
        for i, _ in enumerate(main):
            for _ in range(per_step):
                next(filler, None)

    class Sums:

        def __init__(self, n, values=False):
            self.n, self.values, self.k, self.pend = n, values, 0, None
            self.out = banks.tiles[STAT]

        def add(self, src, dep):
            i = scr.get()
            sq = scr.tiles[i][:, :]
            t = act(lambda e: e.activation(sq, src, ACT.Square), dep, scr.free[i])
            self.flush()
            self.pend = (src, sq, t, i)

        def flush(self):
            if self.pend is None:
                return
            src, sq, t, i = self.pend
            kinds = [(0, src), (2, sq)] if self.values else [(2, sq)]
            first, last = self.k == 0, self.k == self.n - 1
            for c, x in kinds:
                for tb in range(2):
                    mm(self.out[:, c + tb:c + tb + 1], x[:, tb * P:tb * P + P], ones[:, 0:1], first, last and c + tb == 3,
                       [t, banks.free[STAT] if first else None], sig=(c + tb == 3))
                    first = False
            scr.free[i] = self.tok = pr.last("pe")
            self.k += 1
            self.pend = None

        def finish(self):
            self.flush()
            assert self.k == self.n
            return self.tok

    def ready_root():
        act(lambda e: e.activation(nst[:, 12:13], eps_rms, ACT.Sqrt))

    norm_free = [None]

    def spread(cols, deps):
        b = banks.get()
        for n, c in enumerate(cols):
            i = scr.get()
            diag = scr.tiles[i]
            td = [dve(lambda e, diag=diag, tb=tb, c=c: e.tensor_scalar(diag[:, tb * P:tb * P + P], ident, nst[:, c + tb:c + tb + 1], None, ALU.mult),
                      deps, scr.free[i]) for tb in range(2)]
            for tb in range(2):
                tok = mm(banks.tiles[b][:, n * T + tb * P:n * T + tb * P + P], ones, diag[:, tb * P:tb * P + P], True, True,
                         [td, banks.free[b]], sig=True)
            scr.free[i] = tok
        norm_free[0] = tok
        return b, tok

    def rms_split(src, n, gkey, sums, hi, lo, keep=None):
        tok = sums.finish()
        t = act(lambda e: e.activation(nst[:, 0:2], sums.out[:, 2:4], ACT.Sqrt, bias=eps_rms, scale=1.0 / (n * P)), tok, norm_free[0])
        banks.done_stat([t])
        t = dve(lambda e: e.reciprocal(nst[:, 2:4], nst[:, 0:2]), t, norm_free[0])
        b, t = spread([2], t)
        root = banks.tiles[b][:, 0:T]
        toks, td = [], []
        for k in range(n):
            if keep is None:
                i = scr.get()
                d, free = scr.tiles[i][:, :], scr.free[i]
            else:
                i, d, free = None, keep[:, k, :], None
            g = par_col(gkey, k)
            s_ = src[:, k, :]
            t1 = dve(lambda e, d=d, s_=s_, g=g: e.scalar_tensor_tensor(d, s_, g, root, ALU.mult, ALU.mult), t, free)
            td.append(t1)
            tt = split_act(d, hi[:, k, :], lo[:, k, :], t1, eng="pool" if k % 2 else "dve")
            if i is not None:
                scr.free[i] = tt
            toks.append(tt)
        banks.done(b, td)
        return Act2(hi, lo, toks)

    def layer_norm(sums, key_g, key_b, split=True):
        tok = sums.finish()
        mean, var, r, mr = nst[:, 4:6], nst[:, 0:2], nst[:, 2:4], nst[:, 8:10]
        t = dve(lambda e: e.tensor_scalar(mean, sums.out[:, 0:2], 1.0 / D, None, ALU.mult), tok, norm_free[0])
        t = dve(lambda e: e.tensor_tensor(nst[:, 6:8], mean, mean, ALU.mult), t)
        t = dve(lambda e: e.scalar_tensor_tensor(var, sums.out[:, 2:4], 1.0 / D, nst[:, 6:8], ALU.mult, ALU.subtract), t)
        banks.done_stat([t])
        t = dve(lambda e: e.tensor_scalar(var, var, 0.0, None, ALU.max), t)
        t = act(lambda e: e.activation(var, var, ACT.Sqrt, bias=eps_ln), t)
        t = dve(lambda e: e.reciprocal(r, var), t)
        t = [t, dve(lambda e: e.tensor_tensor(mr, mean, r, ALU.mult), t)]
        b, t = spread([2, 8], t)
        root, off = banks.tiles[b][:, 0:T], banks.tiles[b][:, T:2 * T]
        toks, td = [], []
        for k in range(8):
            x, g, bb = X[:, k, :], par_col(key_g, k), par_col(key_b, k)
            t1 = dve(lambda e, x=x: e.tensor_tensor(x, x, root, ALU.mult), t)
            t1 = dve(lambda e, x=x: e.tensor_tensor(x, x, off, ALU.subtract), t1)
            td.append(t1)
            if split:
                hi, lo = Hh[:, k, :], Hl[:, k, :]
                t2 = act(lambda e, x=x, g=g, bb=bb, hi=hi: e.activation(hi, x, ACT.Identity, bias=bb, scale=g), t1)
                t3 = act(lambda e, x=x, g=g, bb=bb: e.activation(x, x, ACT.Identity, bias=bb, scale=g), t1, t2)
                toks.append([t2, pool(lambda e, x=x, hi=hi, lo=lo: e.tensor_tensor(lo, x, hi.bitcast(F32), ALU.subtract), t2, t3)])
            else:
                toks.append(act(lambda e, x=x, g=g, bb=bb: e.activation(x, x, ACT.Identity, bias=bb, scale=g), t1))
        banks.done(b, td)
        return Act2(Hh, Hl, toks) if split else toks

    def residual(name, layer, rows, x, scale, sums=None, **kw):
        early = []

        def take_shift(t):
            b = banks.get()
            tok = mm(banks.tiles[b][:, 0:T], ones, X[:, 0, :], True, True, [t, banks.free[b]], sig=True)
            ts = act(lambda e: e.mul(shift[:, :], banks.tiles[b][:, 0:T], 1.0 / P), tok)
            banks.done(b, [ts])
            return ts

        def less_shift(k, t, t_shift):
            xk = X[:, k, :]
            return op("dve" if k == 7 else "pool", lambda e: e.tensor_tensor(xk, xk, shift[:, :], ALU.subtract), t, t_shift)

        t_shift = []

        def evac(j, out, tok):
            xj = X[:, j, :]
            if scale == 1.0:
                t = dve(lambda e: e.tensor_tensor(xj, xj, out, ALU.add), tok)
            else:
                t = dve(lambda e: e.scalar_tensor_tensor(xj, xj, scale, out, ALU.mult, ALU.add), tok)
            if sums is not None:
                if j == 2:
                    ready_root()
                if not sums.values:
                    sums.add(xj, t)
                elif j == 0:
                    early.append(t)
                else:
                    if j == 1:
                        t_shift.append(take_shift(early[0]))
                        sums.add(X[:, 0, :], less_shift(0, early[0], t_shift))
                    sums.add(xj, less_shift(j, t, t_shift))
            return [t]
        return project(name, layer, rows, pieces(0, D), x, evac, **kw)

    def mk_turning(ctx, cos, sin, perm, t_tables):
        return {"raw": [sb(ctx, [P, T]) for _ in range(2)], "tmp": [sb(ctx, [P, T]) for _ in range(2)],
                "cos": cos, "sin": sin, "perm": perm, "t_tables": t_tables, "n": 0, "read": [None, None]}

    def rotated(name, layer, rows, tile_cols, x, tn, place, **kw):
        moved = {}

        def turn(j):
            i, t_moved = moved.pop(j)
            z, tmp = tn["raw"][i][:, :], tn["tmp"][i][:, :]
            dst, scale, sink, t_dst = place(j)
            b = banks.get()
            out = banks.tiles[b][:, 0:T]
            tok = mm(out, tn["perm"], z, True, True, [t_moved, tn["t_tables"], banks.free[b]], sig=True)
            t_sin = dve(lambda e: e.scalar_tensor_tensor(tmp, out, scale, tn["sin"], ALU.mult, ALU.mult), tok, tn["read"][i])
            banks.done(b, [t_sin])
            t_cos = dve(lambda e: e.scalar_tensor_tensor(z, z, scale, tn["cos"], ALU.mult, ALU.mult), tok)
            res = [dve(lambda e, d=d, r0=r0, r1=r1: e.tensor_tensor(d, z[r0:r1, :], tmp[r0:r1, :], ALU.add), t_sin, t_cos, t_dst)
                   for d, r0, r1 in dst]
            tn["read"][i] = res
            sink.extend(res)

        for j, out, b, tok in feature_tiles(name, layer, rows, tile_cols, x, **kw):
            i = tn["n"] % 2
            tn["n"] += 1
            z = tn["raw"][i][:, :]
            if not (kw.get("together") and j == 1):
                for k in sorted(moved):
                    turn(k)
            t_moved = act(lambda e, z=z, out=out: e.activation(z, out, ACT.Copy), tok, tn["read"][i])
            banks.done(b, [t_moved])
            moved[j] = (i, t_moved)
            yield
        turn(len(tile_cols) - 1)

    def attention(heads, rS, rT, small):
        lag = {"s": 0, "t": 2, "v": 3}
        n = len(heads)

        def scores(h):
            h["col"] = col = small["n"] % small["size"]
            small["n"] += 1
            w = h["widths"]
            st = small["tile"]
            mn, l, r = st[:, col, 0:2], st[:, col, 2:4], st[:, col, 4:6]
            ng = len(h["qk"])
            h["bufs"] = []
            prev = [[small["free"][col]], [small["free"][col]]]
            toks_min = [None, None]
            for g in range(ng):
                b = banks.get("att")
                tok = h["qk"][g](banks.tiles[b], banks.free[b])
                i = rS.get()
                S = rS.tiles[i]
                h["bufs"].append(i)
                if h["masks"][g] is None:
                    t = dve(lambda e, b=b: e.tensor_reduce(mn, banks.tiles[b][:, :].rearrange("p (a k) -> p a k", a=2),
                                                           AX.X, ALU.min), tok, prev[0])
                    toks_min = [t, t]
                    h["src"] = banks.tiles[b]
                    h["bank"] = b
                else:
                    ts = []
                    o = 0
                    for qb in range(2):
                        init = 3.0e38 if g == 0 else mn[:, qb:qb + 1]
                        if h.get("sink") is not None:
                            init = h["sink"]
                        dst, ps, mk = S[:, o:o + w[qb]], banks.tiles[b][:, o:o + w[qb]], h["masks"][g][qb]
                        t = dve(lambda e, dst=dst, ps=ps, mk=mk, init=init, qb=qb: e.tensor_tensor_reduce(
                            dst, ps, mk, 1.0, init, ALU.add, ALU.min, mn[:, qb:qb + 1]), tok, rS.free[i], prev[qb], h["deps"])
                        toks_min[qb] = t
                        prev[qb] = [t]
                        ts.append(t)
                        o += w[qb]
                    banks.done(b, ts)
            te = []
            for g in range(ng):
                S = rS.tiles[h["bufs"][g]]
                o = 0
                for qb in range(2):
                    src = S if h["masks"][g] is not None else h["src"]
                    acc = l[:, qb:qb + 1] if ng == 1 else st[:, col, 6 + 2 * g + qb:7 + 2 * g + qb]
                    t = act(lambda e, S=S, src=src, o=o, qb=qb, acc=acc: e.activation(
                        S[:, o:o + w[qb]], src[:, o:o + w[qb]], ACT.Exp, bias=mn[:, qb:qb + 1], scale=-1.0, accum_out=acc),
                        toks_min, rS.free[h["bufs"][g]] if h["masks"][g] is None else None)
                    te.append(t)
                    o += w[qb]
                if h["masks"][g] is None:
                    banks.done(h["bank"], te)
            tot = sum(w)
            S0 = rS.tiles[h["bufs"][0]]
            if ng == 1 and h.get("sink") is not None:
                for qb in range(2):
                    te.append(act(lambda e, qb=qb: e.activation(st[:, col, 6 + qb:7 + qb], h["sink"], ACT.Exp,
                                                                bias=mn[:, qb:qb + 1], scale=-1.0), toks_min))
                t = dve(lambda e: e.tensor_tensor(l, l, st[:, col, 6:8], ALU.add), te)
            elif ng == 3:
                t = dve(lambda e: e.tensor_tensor(l, st[:, col, 6:8], st[:, col, 8:10], ALU.add), te)
                t = dve(lambda e: e.tensor_tensor(l, l, st[:, col, 10:12], ALU.add), t)
                S1, S2 = rS.tiles[h["bufs"][1]], rS.tiles[h["bufs"][2]]
                t2 = pool(lambda e: e.tensor_tensor(S0[:, 0:tot], S0[:, 0:tot], S1[:, 0:tot], ALU.add), te)
                t3 = dve(lambda e: e.tensor_tensor(S0[:, 0:tot], S0[:, 0:tot], S2[:, 0:tot], ALU.add), t2)
                rS.free[h["bufs"][1]] = t2
                rS.free[h["bufs"][2]] = t3
                t = [t, t3]
            else:
                t = te
            t = dve(lambda e: e.reciprocal(r, l), t, te)
            o = 0
            h["p"] = []
            for qb in range(2):
                h["p"].append(dve(lambda e, o=o, qb=qb: e.tensor_scalar(S0[:, o:o + w[qb]], S0[:, o:o + w[qb]], r[:, qb:qb + 1],
                                                                       None, ALU.mult), t))
                o += w[qb]
            small["free"][col] = h["p"]

        def turn(h):
            w = h["widths"]
            i = h["bufs"][0]
            S = rS.tiles[i]
            b = banks.get("att")
            h["pt"] = []
            o = 0
            first = [banks.free[b], h["p"]]
            for qb in range(2):
                for kb in range(w[qb] // P):
                    slot = len(h["pt"])
                    h["pt"].append((kb, qb))
                    out, src = banks.tiles[b][:, slot * P:slot * P + P], S[:, o + kb * P:o + kb * P + P]
                    tok = pr.op("pe", lambda e, out=out, src=src: e.transpose(out, src, ident), first, sig=True)
                    first = None
                o += w[qb]
            rS.free[i] = tok
            j = rT.get()
            h["T"] = j
            n_ = len(h["pt"]) * P
            dst, src = rT.tiles[j][:, 0:n_], banks.tiles[b][:, 0:n_]
            t = act(lambda e: e.activation(dst, src, ACT.Copy), tok, rT.free[j])
            banks.done(b, [t])
            h["tt"] = t

        pair = {}

        def values(h):
            d = h["d"]
            TT = rT.tiles[h["T"]]
            base = h["base"]
            if base == 0:
                pair["b"] = banks.get("att")
            b = pair["b"]
            first = [banks.free[b], h["tt"], h["vdeps"]]
            w = h["widths"]
            for qb in range(2):
                kbs = [kb for kb, q in h["pt"] if q == qb]
                out = banks.tiles[b][base:base + d, qb * P:qb * P + P]
                for x, kb in enumerate(kbs):
                    slot = h["pt"].index((kb, qb))
                    tok = mm(out, h["v"](kb), TT[:, slot * P:slot * P + P], x == 0, x == len(kbs) - 1, first, sig=(x == len(kbs) - 1))
                    first = None
            rT.free[h["T"]] = tok
            if base + d == P:
                src = banks.tiles[b][:, 0:T]
                hi, lo, sink_list = h["out"]
                t1 = act(lambda e: e.activation(hi, src, ACT.Copy), tok, h["odeps"])
                t2 = dve(lambda e: e.tensor_tensor(lo, src, hi.bitcast(F32), ALU.subtract), t1)
                banks.done(b, [t1, t2])
                sink_list.append([t1, t2])

        for i in range(n + 3):
            if i < n:
                scores(heads[i])
            if 0 <= i - lag["t"] < n:
                turn(heads[i - lag["t"]])
            if 0 <= i - lag["v"] < n:
                values(heads[i - lag["v"]])
            yield

    def mk_small(ctx):
        return {"tile": sb(ctx, [P, 6, 12]), "n": 0, "size": 6, "free": [None] * 6}

    ALL, SOME, ATT = list(range(7)), [0, 1, 2], [3, 4, 5, 6]

    def head(**kw):
        return dict(dict(deps=None, base=0, sink=None, odeps=None), **kw)

    def mixer1(l, sums_in):
        with ExitStack() as s1:
            cA = sb(s1, [P, sum(w for _, w in atA.values())])
            t_cA = pr.op("act", lambda e: e.dma_start(cA[:, :], dram["cA"]), None, sem="ld_A", step=16)

            def CA(name):
                o, w = atA[name]
                return cA[:, o:o + w]

            y0, y1 = sb(s1, [P, 8, T], F32R), None
            ytok = [[], [], []]
            S_ring = Ring([sb(s1, [P, 512]) for _ in range(3)])
            T_ring = Ring([sb(s1, [P, 512]) for _ in range(2)])
            small = mk_small(s1)
            nsink = sb(s1, [P, 8])
            gq, gk, gv, kp = sb(s1, [P, 4, T]), sb(s1, [P, 4, T]), sb(s1, [P, 2, P]), sb(s1, [P, 2, T])
            cqn_h, cqn_l = sb(s1, [P, 3, T], F32R), sb(s1, [P, 3, T], F32R)
            ckn_h, ckn_l = sb(s1, [P, 2, T], F32R), sb(s1, [P, 2, T], F32R)
            pr.fence(["act", "dve", "pool"])
            turning = mk_turning(s1, CA("cos1"), CA("sin1"), CA("perm1"), t_cA)
            o_s = atP[0][f"sink{l}"]
            t_sink = pool(lambda e: e.tensor_scalar(nsink[:, :], par[:, o_s:o_s + 8], -1.0, None, ALU.mult))
            tz1 = pool(lambda e: e.memset(kp[:, :, :], 0.0))
            tz2 = pool(lambda e: e.memset(gk[:, :, :], 0.0))
            made = {}
            tkp, tgq, tgk, tgv = [], [], [], []

            with ExitStack() as s2:
                bias = sb(s2, [P, 8, 2, T])
                Q, K, V = sb(s2, [P, 4, T]), sb(s2, [P, 8, T]), sb(s2, [P, 2, 512])
                cq, ck = sb(s2, [P, 3, T]), sb(s2, [P, 2, T])
                t_z = pool(lambda e: e.memset(K[:, :, :], 0.0))
                tb = []
                for rq in range(4):
                    src = dram["rpb"][l, :, :, 3 - rq:7 - rq, :].rearrange("p h r c -> p h (r c)")
                    r2, qb = rq % 2, rq // 2
                    dst = bias[64 * r2:64 * r2 + 64, :, qb, :]
                    tb.append(pr.op("act", lambda e, src=src, dst=dst: e.dma_start(dst, src), None, sem=f"ld_b{rq}", step=16))
                nm = CA("namask").unsqueeze(1).broadcast_to([P, 64, 64])
                bv = bias[:, :, :, :].rearrange("p h q (r c) -> p (h q r) c", c=64)
                H = rms_split(X, 8, f"norm1_g{l}", sums_in, Hh, Hl)
                t_bias = pool(lambda e: e.tensor_tensor(bv, nm, bv, ALU.subtract), tb, t_cA)
                tq, tk, tv = [], [], []

                def evac_q(j, out, tok):
                    tq.append(act(lambda e: e.mul(Q[:, j, :], out, -0.125), tok))
                    return tq[-1:]

                def evac_k(j, out, tok):
                    t1 = dve(lambda e: e.tensor_copy(K[0:64, 2 * j, :], out[0:64, :]), tok, t_z)
                    t2 = act(lambda e: e.activation(K[64:128, 2 * j + 1, :], out[64:128, :], ACT.Copy), tok, t_z)
                    tk.extend([t1, t2])
                    return [t1, t2]

                run(project("w_in", l, range(8), pieces(0, 512), H, evac_q, together=True),
                    project("w_in", l, range(8), pieces(512, 1024), H, evac_k),
                    by_token("w_in", l, range(8), np.arange(1024, 1536), H, T, V, tv))

                def latent():
                    sums = Sums(3)

                    def evac(j, out, tok):
                        dst = cq[:, j, :] if j < 3 else ck[:, j - 3, :]
                        t = act(lambda e: e.activation(dst, out, ACT.Copy), tok)
                        made["s"].add(dst, t)
                        return [t]
                    made["s"] = sums
                    for n, _ in enumerate(project("w_in", l, range(8), pieces(1536, 2176), H, evac)):
                        if n == 2:
                            made["cq"] = rms_split(cq, 3, f"mla_qa_g{l}", sums, cqn_h, cqn_l)
                            made["s"] = Sums(2)
                        yield
                    made["ck"] = rms_split(ck, 2, f"mla_kva_g{l}", made["s"], ckn_h, ckn_l)

                kr = np.arange(2176, 2240)
                tiles = [np.concatenate([kr, kr])] + pieces(2240, 2752)
                for g in range(2):
                    k0 = np.arange(2752 + 64 * g, 2816 + 64 * g)
                    tiles.append(np.concatenate([k0, k0]))

                def place_g(j):
                    if j == 0:
                        return [(kp[0:64, 0, :], 0, 64), (kp[64:128, 1, :], 64, 128)], 1.0, tkp, tz1
                    if j < 5:
                        return [(gq[:, j - 1, :], 0, 128)], -0.125, tgq, None
                    g = j - 5
                    return [(gk[0:64, 2 * g, :], 0, 64), (gk[64:128, 2 * g + 1, :], 64, 128)], 1.0, tgk, tz2

                filler = chain(latent(), rotated("w_in", l, range(8), tiles, H, turning, place_g),
                               by_token("w_in", l, range(8), np.arange(2880, 3008), H, P, gv, tgv))
                heads = []
                for h in range(8):
                    def qk(ps, free, h=h):
                        for qb in range(2):
                            tok = mm(ps[:, qb * T:qb * T + T], Q[:, h // 2, qb * P:qb * P + P], K[:, h, :], True, True,
                                     [free, tq, tk] if qb == 0 else None, sig=True)
                        return tok
                    heads.append(head(qk=[qk], masks=[[bias[:, h, 0, :], bias[:, h, 1, :]]], widths=[T, T], deps=[t_bias], d=64,
                                      base=64 * (h % 2), v=lambda kb, h=h: V[:, kb, 64 * h:64 * h + 64], vdeps=tv,
                                      out=(y0[:, h // 2, :], y0[:, 4 + h // 2, :], ytok[0])))
                banks.assign(lin=SOME, att=ATT)
                weave(attention(heads, S_ring, T_ring, small), filler, 1)
                run(filler)
                banks.assign(lin=ALL, att=ALL)

            with ExitStack() as s2:
                pr.fence(["act", "dve", "pool"])
                y1, y2 = sb(s2, [P, 8, T], F32R), sb(s2, [P, 8, T], F32R)
                mg = sb(s2, [P, 8, T])
                qn, qp, kn, vm = sb(s2, [P, 4, T]), sb(s2, [P, 2, T]), sb(s2, [P, 4, T]), sb(s2, [P, 2, 512])
                sc = -(192.0 ** -0.5)
                tiles = [np.arange(192 * h, 192 * h + P) for h in range(4)]
                tiles += [np.concatenate([np.arange(192 * h + P, 192 * h + 192) for h in (2 * c, 2 * c + 1)]) for c in range(2)]
                tqn, tqp, tkn, tvm = [], [], [], []

                def evac_uq(j, out, tok):
                    tqn.append(act(lambda e: e.mul(qn[:, j, :], out, sc), tok))
                    return tqn[-1:]

                def evac_uk(j, out, tok):
                    tkn.append(dve(lambda e: e.tensor_copy(kn[:, j, :], out), tok))
                    return tkn[-1:]

                vc = np.concatenate([np.arange(256 * h + P, 256 * h + 256) for h in range(4)])
                run(rotated("mla_w_uq", l, range(3), tiles[4:6], made["cq"], turning, lambda j: ([(qp[:, j, :], 0, 128)], sc, tqp, None), per_unit=2),
                    project("mla_w_uq", l, range(3), tiles[0:4], made["cq"], evac_uq, per_unit=4),
                    project("mla_w_ukv", l, range(2), [np.arange(256 * h, 256 * h + P) for h in range(4)], made["ck"], evac_uk, per_unit=4),
                    by_token("mla_w_ukv", l, range(2), vc, made["ck"], T, vm, tvm))
                ys = [y0, y1, y2]
                mtok = [None] * 8
                last_pe = {}

                def branch(br):
                    name = ["w_br_na", "w_br_mla", "w_br_gqa"][br]
                    Y = Act2(ys[br][:, 0:4, :], ys[br][:, 4:8, :], ytok[br])
                    G = {}

                    def evac_gate(j, out, tok):
                        i = scr.get()
                        G[j] = i
                        bg = par_col(f"b_gate{l}", 8 * br + j)
                        t = act(lambda e: e.activation(scr.tiles[i][:, :], out, ACT.Sigmoid, bias=bg), tok, scr.free[i])
                        G[j] = (i, t)
                        return [t]

                    def evac_br(j, out, tok):
                        i, tg = G[j]
                        g, m = scr.tiles[i][:, :], mg[:, j, :]
                        if br == 0:
                            t = dve(lambda e: e.tensor_tensor(m, g, out, ALU.mult), tok, tg)
                            mtok[j] = t
                            scr.free[i] = t
                            return [t]
                        t = dve(lambda e: e.tensor_tensor(g, g, out, ALU.mult), tok, tg)
                        t2 = pool(lambda e: e.tensor_tensor(m, m, g, ALU.add), t, mtok[j])
                        scr.free[i] = t2
                        mtok[j] = t2
                        if br == 2:
                            mtok[j] = split_act(m, y0[:, j, :], y1[:, j, :], t2, last_pe["t"], eng="dve")
                        last_pe["t"] = tok
                        return [t]

                    gates = project("w_in", l, range(8), pieces(3008 + D * br, 3008 + D * br + D), H, evac_gate)
                    brs = project(name, l, range(4), pieces(0, D), Y, evac_br, per_unit=2)
                    for j in range(4):
                        for g in (gates, brs):
                            next(g)
                            next(g)
                            yield
                    run(gates, brs)

                heads = []
                for h in range(4):
                    def qk(ps, free, h=h):
                        for qb in range(2):
                            mm(ps[:, qb * T:qb * T + T], qn[:, h, qb * P:qb * P + P], kn[:, h, :], True, False,
                               [free, tqn, tqp, tkn, tkp] if qb == 0 else None)
                            tok = mm(ps[:, qb * T:qb * T + T], qp[:, h // 2, qb * P:qb * P + P], kp[:, h % 2, :], False, True, sig=True)
                        return tok
                    heads.append(head(qk=[qk], masks=[None], widths=[T, T], d=P, v=lambda kb, h=h: vm[:, kb, P * h:P * h + P], vdeps=tvm,
                                      out=(y1[:, h, :], y1[:, 4 + h, :], ytok[1])))
                gm = CA("gmask")
                for h in range(8):
                    def qk(ps, free, h=h):
                        for qb in range(2):
                            tok = mm(ps[:, qb * T:qb * T + T], gq[:, h // 2, qb * P:qb * P + P], gk[:, 2 * (h // 4) + h % 2, :], True, True,
                                     [free, tgq, tgk] if qb == 0 else None, sig=True)
                        return tok
                    heads.append(head(qk=[qk], masks=[[gm[:, 0:T], gm[:, T:2 * T]]], widths=[T, T], deps=[t_cA, t_sink], d=64,
                                      base=64 * (h % 2), sink=nsink[:, h:h + 1], v=lambda kb, h=h: gv[:, kb, 64 * (h // 4):64 * (h // 4) + 64],
                                      vdeps=tgv, out=(y2[:, h // 2, :], y2[:, 4 + h // 2, :], ytok[2])))
                banks.assign(lin=SOME, att=ATT)
                filler = chain(branch(0), branch(1))
                weave(attention(heads, S_ring, T_ring, small), filler, 1)
                run(filler)
                banks.assign(lin=ALL, att=ALL)
                run(branch(2))
                sums = Sums(8)
                run(residual("w_out", l, range(8), Act2(y0, y1, mtok), 1.0, sums))
                return sums

    def ffn1(l, sums_in):
        with ExitStack() as s1:
            pr.fence(["act", "dve", "pool"])
            fh, fl = sb(s1, [P, 22, T], F32R), sb(s1, [P, 22, T], F32R)
            H = rms_split(X, 8, f"norm2_g{l}", sums_in, Hh, Hl)
            ab = Ring([sb(s1, [P, 2, T]) for _ in range(4)])
            ft = [None] * 22
            tiles = []
            for m in range(22):
                tiles += [np.arange(P * m, P * m + P), np.arange(DFF + P * m, DFF + P * m + P)]
            cur = {}

            def second(m, i, tt):
                A = ab.tiles[i]
                t = act(lambda e: e.activation(A[:, 1, :], A[:, 1, :], ACT.Gelu_apprx_tanh), tt)
                t = dve(lambda e: e.tensor_tensor(A[:, 0, :], A[:, 0, :], A[:, 1, :], ALU.mult), t)
                ft[m] = split_act(A[:, 0, :], fh[:, m, :], fl[:, m, :], t, eng="pool")
                ab.free[i] = ft[m]

            def evac(j, out, tok):
                m, g = j // 2, j % 2
                f = 22 * g + m
                if g == 0:
                    if "pend" in cur:
                        cur["late"] = cur.pop("pend")
                    cur["i"], cur["tt"] = ab.get(), []
                i = cur["i"]
                A = ab.tiles[i][:, g, :]
                t = act(lambda e: e.activation(A, out, ACT.Identity, bias=par_col(f"conv_b{l}", f), scale=par_col(f"conv1_{l}", f)), tok, ab.free[i])
                t = dve(lambda e: e.scalar_tensor_tensor(A[:, 1:T], out[:, 0:T - 1], par_col(f"conv0_{l}", f), A[:, 1:T], ALU.mult, ALU.add), t)
                t = dve(lambda e: e.scalar_tensor_tensor(A[:, 0:T - 1], out[:, 1:T], par_col(f"conv2_{l}", f), A[:, 0:T - 1], ALU.mult, ALU.add), t)
                cur["tt"].append(t)
                if g:
                    if "late" in cur:
                        second(*cur.pop("late"))
                    cur["pend"] = (m, i, cur["tt"])
                return [t]

            run(project("w_up", l, range(8), tiles, H, evac, together=True))
            second(*cur["pend"])
            sums = Sums(8)
            run(residual("w_down", l, range(22), Act2(fh, fl, ft), 1.0, sums, kpart=11))
            return sums

    def mlp2(l, H):
        with ExitStack() as s1:
            pr.fence(["act", "dve", "pool"])
            fh, fl = sb(s1, [P, 32, T], F32R), sb(s1, [P, 32, T], F32R)
            ring = Ring([sb(s1, [P, T]) for _ in range(4)])
            ft = [None] * 32

            def evac(j, out, tok):
                i = ring.get()
                R = ring.tiles[i][:, :]
                t0 = dve(lambda e: e.tensor_scalar(R, out, 0.0, None, ALU.max), tok, ring.free[i])
                t = act(lambda e: e.activation(R, R, ACT.Square), t0)
                ft[j] = split_act(R, fh[:, j, :], fl[:, j, :], t, eng="pool")
                ring.free[i] = ft[j]
                return [t0]

            run(project("mlp_w1_2", l, range(8), pieces(0, 4096), H, evac, together=True))
            sums = Sums(8, True)
            run(residual("mlp_w2_2", l, range(32), Act2(fh, fl, ft), ALPHA, sums, kpart=16))
            return sums

    def turn_tokens(src, dst, dep):
        res = []
        for tb in range(2):
            b = banks.get()
            first = [dep, banks.free[b]]
            for c in range(4):
                o, s = banks.tiles[b][:, c * P:c * P + P], src[:, c, tb * P:tb * P + P]
                tok = pr.op("pe", lambda e, o=o, s=s: e.transpose(o, s, ident), first, sig=True)
                first = None
            t = act(lambda e, tb=tb, b=b: e.activation(dst[:, tb, :], banks.tiles[b][:, :], ACT.Copy), tok)
            banks.done(b, [t])
            res.append(t)
        return res

    def rwkv_moba(H):
        with ExitStack() as s1:
            pr.fence(["act", "dve", "pool"])
            ym = sb(s1, [P, 8, T], F32R)
            ytok = []
            bonus, gate, KH, BH = (sb(s1, [P, 4, T]) for _ in range(4))
            AR = sb(s1, [P, 4, 4, 2, 64])
            Vt, FC = sb(s1, [P, 2, 512]), sb(s1, [P, 4, 4])

            def prep(Z, tz):
                with ExitStack() as s3:
                    lora = sb(s3, [P, 3, 512])
                    sig, aa, cs, kk, ex = (sb(s3, [P, 4, T]) for _ in range(5))
                    mid, end = sb(s3, [P, 4, 4]), sb(s3, [P, 4, 4])
                    pr.fence(["act", "dve", "pool"])
                    t_l = pr.op("act", lambda e: e.dma_start(lora[:, :, :], dram["lora"]), None, sem="ld_l", step=16)
                    v4 = lambda t: t.rearrange("p c (k i) -> p c k i", i=64)
                    fl2 = lambda t: t.rearrange("p c t -> p (c t)")
                    R, K, V = Z[:, 0:4, 1:T + 1], Z[:, 4:8, 1:T + 1], Z[:, 8:12, 1:T + 1]
                    wd, ad, g1, g2 = Z[0:64, 12, 1:T + 1], Z[64:128, 12, 1:T + 1], Z[:, 13, 1:T + 1], Z[0:32, 14, 1:T + 1]
                    t_w = act(lambda e: e.activation(wd, wd, ACT.Tanh), tz[12])
                    t_g1 = act(lambda e: e.activation(g1, g1, ACT.Sigmoid), tz[13])
                    t_g2 = act(lambda e: e.activation(g2, g2, ACT.Sigmoid), tz[14])
                    tk = [pool(lambda e, c=c: e.tensor_scalar(kk[:, c, :], K[:, c, :], par_col("ab_k_k_2", c), None, ALU.mult), tz[4 + c])
                          for c in range(4)]
                    t_one = dve(lambda e: e.memset(ex[:, :, :], 1.0))
                    t_one = dve(lambda e: e.memset(v4(ex[:, :, :])[:, :, :, 0:1], 0.0), t_one)
                    ts, ta, tg = [], [], []
                    for c in range(4):
                        cc = slice(P * c, P * c + P)
                        b = banks.get()
                        o1 = banks.tiles[b][:, 0:T]
                        t1 = mm(o1, lora[0:64, 0, cc], wd, True, True, [t_w, t_l, banks.free[b]], sig=True)
                        ts.append(act(lambda e, c=c, o1=o1: e.activation(sig[:, c, :], o1, ACT.Sigmoid, bias=par_col("ab_w0_2", c)), t1))
                        banks.done(b, ts[-1:])
                    for c in range(4):
                        cc = slice(P * c, P * c + P)
                        b = banks.get()
                        o2 = banks.tiles[b][:, 0:T]
                        t2 = mm(o2, lora[64:128, 0, cc], ad, True, True, [t_l, tz[12], banks.free[b]], sig=True)
                        ta.append(act(lambda e, c=c, o2=o2: e.activation(aa[:, c, :], o2, ACT.Sigmoid, bias=par_col("ab_a0_2", c)), t2))
                        banks.done(b, ta[-1:])
                    for c in range(4):
                        cc = slice(P * c, P * c + P)
                        b = banks.get()
                        o3 = banks.tiles[b][:, 0:T]
                        mm(o3, lora[:, 1, cc], g1, True, False, [t_g1, t_g2, t_l, banks.free[b]])
                        t3 = mm(o3, lora[0:32, 2, cc], g2, False, True, sig=True)
                        tg.append(act(lambda e, c=c, o3=o3: e.activation(gate[:, c, :], o3, ACT.Copy), t3))
                        banks.done(b, tg[-1:])
                    t_cs = dve(lambda e: e.tensor_tensor_scan(fl2(cs[:, :, :]), fl2(ex[:, :, :]), fl2(sig[:, :, :]), 0.0, ALU.mult, ALU.add), t_one, ts)
                    cs4, sg4, ex4 = v4(cs[:, :, :]), v4(sig[:, :, :]), v4(ex[:, :, :])
                    t_m = dve(lambda e: e.tensor_copy(mid[:, :, :], cs4[:, :, :, 31]), t_cs)
                    t_c = []
                    for c in range(4):
                        mb = mid[:, c, :].unsqueeze(2).broadcast_to([P, 4, 64])
                        t_c.append(dve(lambda e, c=c, mb=mb: e.tensor_tensor(cs4[:, c], cs4[:, c], mb, ALU.subtract), t_m))
                    t_d = dve(lambda e: e.tensor_tensor(sig[:, :, :], cs[:, :, :], sig[:, :, :], ALU.subtract), t_c)
                    t_e = pool(lambda e: e.tensor_tensor(end[:, :, 0:3], cs4[:, :, 0:3, 63], mid[:, :, 1:4], ALU.add), t_c)
                    t_one = pool(lambda e: e.memset(FC[:, :, 3:4], 1.0))
                    t_x = act(lambda e: e.activation(ex[:, :, :], cs[:, :, :], ACT.Exp, scale=-KAPPA), t_c, t_cs)
                    t_xa = act(lambda e: e.activation(sig[:, :, :], sig[:, :, :], ACT.Exp, scale=-KAPPA), t_d)
                    t_F = [act(lambda e: e.activation(FC[:, :, 0:3], end[:, :, 0:3], ACT.Exp, scale=-KAPPA), t_e), t_one]
                    t_xk = act(lambda e: e.activation(cs[:, :, :], cs[:, :, :], ACT.Exp, scale=KAPPA), t_e, t_x)
                    t_r = [dve(lambda e, c=c: e.tensor_tensor(AR[:, c, :, 1, :], v4(R)[:, c], ex4[:, c], ALU.mult), t_x, tz[c]) for c in range(4)]
                    t_sq = act(lambda e: e.activation(ex[:, :, :], kk[:, :, :], ACT.Square), tk, t_r)
                    tn = []
                    for c2 in range(2):
                        b = banks.get()
                        for c in range(2):
                            tok = mm(banks.tiles[b][:, c * T:c * T + T], half, ex[:, 2 * c2 + c, :], True, True, [t_sq, banks.free[b]], sig=True)
                        e2 = ex[:, 2 * c2:2 * c2 + 2, :]
                        t = dve(lambda e, e2=e2, b=b: e.tensor_scalar(e2, banks.tiles[b][:, :].rearrange("p (c t) -> p c t", c=2),
                                                                     1e-24, None, ALU.max), tok)
                        banks.done(b, [t])
                        t = act(lambda e, e2=e2: e.activation(e2, e2, ACT.Sqrt), t)
                        t = dve(lambda e, e2=e2: e.reciprocal(e2, e2), t)
                        tn.append(dve(lambda e, e2=e2, c2=c2: e.tensor_tensor(kk[:, 2 * c2:2 * c2 + 2, :], kk[:, 2 * c2:2 * c2 + 2, :], e2, ALU.mult), t))
                    t_a = [dve(lambda e, c=c: e.scalar_tensor_tensor(AR[:, c, :, 0, :], v4(kk[:, :, :])[:, c], -1.0, sg4[:, c],
                                                                     ALU.mult, ALU.mult), tn[c // 2], t_xa) for c in range(4)]
                    t = dve(lambda e: e.tensor_tensor(kk[:, :, :], kk[:, :, :], aa[:, :, :], ALU.mult), t_a, ta, tn)
                    t_b = dve(lambda e: e.tensor_tensor(BH[:, :, :], kk[:, :, :], cs[:, :, :], ALU.mult), t, t_xk)
                    tk2 = []
                    for c in range(4):
                        ta2 = pool(lambda e, c=c: e.tensor_scalar(aa[:, c, :], aa[:, c, :], -1.0, par_col("ab_k_a_2", c), ALU.add, ALU.mult), t)
                        tk2.append(dve(lambda e, c=c: e.scalar_tensor_tensor(K[:, c, :], aa[:, c, :], 1.0, K[:, c, :], ALU.add, ALU.mult), ta2, tk))
                    t_k = dve(lambda e: e.tensor_tensor(KH[:, :, :], K, cs[:, :, :], ALU.mult), tk2, t_xk)
                    tb = [dve(lambda e, c=c: e.scalar_tensor_tensor(ex[:, c, :], R[:, c, :], par_col("ab_r_k_2", c), K[:, c, :],
                                                                    ALU.mult, ALU.mult), tk2[c], tn, tz[c]) for c in range(4)]
                    t_bon = []
                    for c2 in range(2):
                        b = banks.get()
                        for c in range(2):
                            tok = mm(banks.tiles[b][:, c * T:c * T + T], half, ex[:, 2 * c2 + c, :], True, True, [tb, banks.free[b]], sig=True)
                        t = dve(lambda e, c2=c2, b=b: e.tensor_tensor(
                            bonus[:, 2 * c2:2 * c2 + 2, :], banks.tiles[b][:, :].rearrange("p (c t) -> p c t", c=2),
                            V[:, 2 * c2:2 * c2 + 2, :], ALU.mult), tok, tz[8:12])
                        banks.done(b, [t])
                        for f in (2 * c2, 2 * c2 + 1):
                            t_bon.append(pool(lambda e, f=f: e.tensor_scalar(bonus[:, f, :], bonus[:, f, :], par_col("ab_lnx_b_2", f), None, ALU.add), t))
                    t_vt = turn_tokens(V, Vt, tz[8:12])
                    return dict(a=t_a, r=t_r, b=t_b, k=t_k, F=t_F, bonus=t_bon, gate=tg, v=t_vt)

            def scan(tp, Yh, Yl, t_y, filler):
                with ExitStack() as s3:
                    cW = sb(s3, [P, sum(w for _, w in atW.values())])
                    Bt, Kt = sb(s3, [P, 2, 512]), sb(s3, [P, 2, 512])
                    NT, RB, AK, RK, XX, XT, YY = (sb(s3, [P, 8, 2, 64]) for _ in range(7))
                    ET = [sb(s3, [P, 8, 2, 64]) for _ in range(2)]
                    SZ, SF = sb(s3, [P, 8, 64]), sb(s3, [P, 4, 64])
                    pr.fence(["act", "dve", "pool"])
                    t_cW = pr.op("act", lambda e: e.dma_start(cW[:, :], dram["cW"]), None, sem="ld_W", step=16)

                    def CW(name):
                        o, w = atW[name]
                        return cW[:, o:o + w]

                    strict, incl, id64 = CW("strict"), CW("incl"), CW("id64")
                    flat = lambda t: t[:, :, :, :].rearrange("p h b i -> p (h b) i")
                    chunks = lambda t: t[:, :, :, :].rearrange("p (f a) b i -> p f (a b) i", f=4)
                    t_s0 = pool(lambda e: e.memset(SZ[:, :, :], 0.0))
                    t_by = []
                    for src, buf, dst, dep in ((BH, XX, Bt, tp["b"]), (KH, YY, Kt, tp["k"])):
                        tt = []
                        for f in range(4):
                            s_ = src[:, f, :].rearrange("p (k i) -> p k i", i=64)
                            fb = FC[:, f, :].unsqueeze(2).broadcast_to([P, 4, 64])
                            o = chunks(buf)[:, f, :, :]
                            tt.append(pool(lambda e, o=o, s_=s_, fb=fb: e.tensor_tensor(o, s_, fb, ALU.mult), dep, tp["F"]))
                        t_by.append((buf, dst, tt))
                    tsc = {}
                    for n, L, dst, dep in ((0, BH, (NT, RB), tp["b"]), (1, KH, (AK, RK), tp["k"])):
                        tsc[n] = []
                        for tbk in range(2):
                            bb = [banks.get(), banks.get()]
                            tok = [None, None]
                            for f in range(4):
                                for c2, par2 in ((0, 0), (1, 1), (1, 0), (0, 1)):
                                    c, r0, p0 = 2 * tbk + c2, 64 * par2, 64 * c2
                                    tok[par2] = mm(banks.tiles[bb[par2]][p0:p0 + 64, f * P:f * P + P], L[r0:r0 + 64, f, 64 * c:64 * c + 64],
                                                   AR[r0:r0 + 64, f, c, :, :].rearrange("p a i -> p (a i)"), True, True,
                                                   [dep, tp["a"], tp["r"], banks.free[bb[0]], banks.free[bb[1]]] if f == 0 else None, sig=(f == 3))
                            for par2 in range(2):
                                src = banks.tiles[bb[par2]][:, :].rearrange("p (f a i) -> p f a i", f=4, a=2)
                                ts2 = []
                                for a2, m in ((0, strict), (1, incl)):
                                    mk = m.unsqueeze(1).broadcast_to([P, 4, 64])
                                    o = dst[a2][:, par2:8:2, tbk, :]
                                    ts2.append(dve(lambda e, o=o, a2=a2, mk=mk, src=src: e.tensor_tensor(o, src[:, :, a2, :], mk, ALU.mult),
                                                   tok[par2], t_cW))
                                banks.done(bb[par2], ts2)
                                tsc[n] += ts2

                    def products(lhs, rhs, deps):
                        res = []
                        for tbk in range(2):
                            b = banks.get()
                            for h in range(8):
                                for c2 in range(2):
                                    p = slice(64 * c2, 64 * c2 + 64)
                                    r = id64[p, :] if rhs is None else rhs[p, h, tbk, :]
                                    tok = mm(banks.tiles[b][p, 64 * h:64 * h + 64], lhs[p, h, tbk, :], r, True, True,
                                             [deps[tbk], banks.free[b]] if h + c2 == 0 else None, sig=(h == 7 and c2 == 1))
                            res.append((tbk, b, tok, banks.tiles[b][:, :].rearrange("p (h i) -> p h i", h=8)))
                        return res

                    idb = id64.unsqueeze(1).broadcast_to([P, 8, 64])
                    t_E = {}

                    def level(n, dep):
                        m = CW(f"lev{n}").unsqueeze(1).broadcast_to([P, 16, 64])
                        t_E[n] = pool(lambda e: e.tensor_tensor(flat(ET[n % 2]), flat(NT), m, ALU.mult), dep, tsc[0], t_cW)

                    level(0, None)
                    level(1, None)
                    t_X, t_XT = [None] * 2, [None] * 2
                    for tbk in range(2):
                        t_XT[tbk] = dve(lambda e, tbk=tbk: e.tensor_tensor(XT[:, :, tbk, :], ET[0][:, :, tbk, :], idb, ALU.add), t_E[0])
                    t_turned = [turn_tokens(buf[:, :, :, :].rearrange("p (f a) b i -> p f (a b i)", f=4), dst, tt) for buf, dst, tt in t_by]
                    for tbk, b, tok, ps in products(ET[0], None, [t_E[0]] * 2):
                        t_X[tbk] = dve(lambda e, ps=ps, tbk=tbk: e.tensor_tensor(XX[:, :, tbk, :], ps, idb, ALU.add), tok, t_turned)
                        banks.done(b, [t_X[tbk]])
                    for n in range(1, 6):
                        if n < 5:
                            level(n + 1, [pr.last("pe"), t_XT])
                        t_Y = [None] * 2
                        for tbk, b, tok, ps in products(ET[n % 2], XX, [[t_E[n], t_X[i]] for i in range(2)]):
                            t_Y[tbk] = dve(lambda e, ps=ps, tbk=tbk: e.tensor_tensor(YY[:, :, tbk, :], ps, idb, ALU.add), tok, t_turned)
                            banks.done(b, [t_Y[tbk]])
                        next(filler, None)
                        ry = [[t_Y[i], t_XT[i]] for i in range(2)]
                        rx = products(XT, YY, ry) if n < 5 else []
                        rt = products(YY, XT, ry)
                        for tbk, b, tok, ps in rx:
                            t_X[tbk] = act(lambda e, ps=ps, tbk=tbk: e.activation(XX[:, :, tbk, :], ps, ACT.Copy), tok)
                            banks.done(b, [t_X[tbk]])
                        for tbk, b, tok, ps in rt:
                            t_XT[tbk] = dve(lambda e, ps=ps, tbk=tbk: e.tensor_copy(XT[:, :, tbk, :], ps), tok)
                            banks.done(b, [t_XT[tbk]])
                    spare = ET[0][:, :, :, :].rearrange("p h b i -> p (h b i)")
                    Gs, Us = spare[:, 0:512], spare[:, 512:1024]
                    Yo = KH
                    sq = YY[:, :, :, :].rearrange("p (f a) b i -> p f (a b i)", f=4)
                    hd = lambda h: slice(64 * h, 64 * h + 64)

                    def norm(tb, t_yo):
                        tt = slice(P * tb, P * tb + P)
                        yv, sv = Yo[:, :, tt], sq[:, :, tt]
                        b = banks.get()
                        tok = mm(banks.tiles[b][:, :], half, yv, True, True, [t_yo, banks.free[b]], sig=True)
                        ps = banks.tiles[b][:, :].rearrange("p (f t) -> p f t", f=4)
                        t = dve(lambda e: e.scalar_tensor_tensor(yv, ps, -1.0 / 64, yv, ALU.mult, ALU.add), tok)
                        banks.done(b, [t])
                        yield
                        t2 = act(lambda e: e.activation(sv, yv, ACT.Square), t)
                        b2 = banks.get()
                        tok = mm(banks.tiles[b2][:, :], half, sv, True, True, [t2, banks.free[b2]], sig=True)
                        ps2 = banks.tiles[b2][:, :].rearrange("p (f t) -> p f t", f=4)
                        t3 = act(lambda e: e.activation(sv, ps2, ACT.Sqrt, bias=eps_gn, scale=1.0 / 64), tok)
                        banks.done(b2, [t3])
                        yield
                        t3 = dve(lambda e: e.reciprocal(sv, sv), t3)
                        t3 = dve(lambda e: e.tensor_tensor(yv, yv, sv, ALU.mult), t3)
                        yield
                        for f in range(4):
                            y1 = yv[:, f, :]
                            t4 = dve(lambda e, y1=y1, f=f: e.scalar_tensor_tensor(y1, y1, par_col("ab_lnx_g_2", f), bonus[:, f, tt], ALU.mult, ALU.add),
                                     t3, tp["bonus"])
                            t4 = dve(lambda e, y1=y1, f=f: e.tensor_tensor(y1, y1, gate[:, f, tt], ALU.mult), t4, tp["gate"])
                            t_y[f].append(split_act(y1, Yh[:, f, tt], Yl[:, f, tt], t4, eng="pool"))
                            yield

                    def source(c, bank):
                        rows, tbk = slice(64 * (c % 2), 64 * (c % 2) + 64), c // 2
                        for h in range(8):
                            tok = mm(banks.tiles[bank][rows, hd(h)], AK[rows, h, tbk, :], Vt[rows, tbk, hd(h)], h == 0, c == 0 and h == 7,
                                     [tp["v"], tsc[1], banks.free[bank]] if h == 0 else None, sig=True)
                        return tok

                    t_s, t_sf = [t_s0], [None, None]
                    t_yo = []
                    after = iter(())
                    bg = banks.get()
                    tok = source(0, bg)
                    for c in range(4):
                        rows, tbk = slice(64 * (c % 2), 64 * (c % 2) + 64), c // 2
                        if c:
                            for h in range(8):
                                tok = mm(banks.tiles[bg][rows, hd(h)], AR[:, h // 2, c, 0, :], SZ[:, h, :], False, h == 7,
                                         t_s if h == 0 else None, sig=(h == 7))
                        g = banks.tiles[bg]
                        t_g = act(lambda e, g=g, rows=rows: e.activation(Gs[rows, :], g[rows, :], ACT.Copy), tok, pr.last("pe"))
                        banks.done(bg, [t_g])
                        bs = banks.get() if c < 3 else None
                        by = banks.get()
                        half_of = lambda bank, h: banks.tiles[bank][64 * (h % 2):64 * (h % 2) + 64, 64 * (h // 2):64 * (h // 2) + 64]
                        for h in range(8):
                            if c < 3:
                                mm(half_of(bs, h), Kt[rows, tbk, hd(h)], Vt[rows, tbk, hd(h)], h < 2, False,
                                   [t_turned, banks.free[bs]] if h == 0 else None)
                            mm(half_of(by, h), Vt[rows, tbk, hd(h)], RK[rows, h, tbk, :], h < 2, False, [banks.free[by]] if h == 0 else None)
                            if c:
                                mm(half_of(by, h), SZ[:, h, :], AR[:, h // 2, c, 1, :], False, False)
                        bu = banks.get()
                        for h in range(8):
                            tok = mm(banks.tiles[bu][rows, hd(h)], XT[rows, h, tbk, :], Gs[rows, hd(h)], True, True,
                                     [t_g, t_XT, banks.free[bu]] if h == 0 else None, sig=(h == 7))
                        u = banks.tiles[bu]
                        t_u = dve(lambda e, u=u, rows=rows: e.tensor_copy(Us[rows, :], u[rows, :]), tok)
                        banks.done(bu, [t_u])
                        if c < 3:
                            bg = banks.get()
                            tok = source(c + 1, bg)
                        next(filler, None)
                        if c < 3:
                            for h in range(8):
                                tok_s = mm(half_of(bs, h), Bt[rows, tbk, hd(h)], Us[rows, hd(h)], False, h > 5, t_u if h == 0 else None, sig=(h == 7))
                            new, ts_old = [], t_s
                            for par2 in range(2):
                                r = slice(64 * par2, 64 * par2 + 64)
                                z_, f_ = SZ[r, par2:8:2, :], SF[r, :, :]
                                ps = banks.tiles[bs][r, 0:T].rearrange("p (f i) -> p f i", f=4)
                                if c == 0:
                                    t = dve(lambda e, z_=z_, ps=ps: e.tensor_copy(z_, ps), tok_s, ts_old)
                                else:
                                    t = dve(lambda e, z_=z_, ps=ps, f_=f_: e.tensor_tensor(z_, f_, ps, ALU.add), tok_s, ts_old, t_sf[par2])
                                new.append(t)
                                if c < 2:
                                    fb = FC[r, :, c + 1:c + 2].broadcast_to([64, 4, 64])
                                    t_sf[par2] = pool(lambda e, z_=z_, f_=f_, fb=fb: e.tensor_tensor(f_, z_, fb, ALU.mult), t, tp["F"])
                            t_s = new + [t_s0]
                            banks.done(bs, new)
                        for h in range(8):
                            tok = mm(half_of(by, h), Us[rows, hd(h)], RB[rows, h, tbk, :], False, h > 5, [t_u, tsc[0]] if h == 0 else None, sig=(h == 7))
                        y_ = banks.tiles[by]
                        t = act(lambda e, y_=y_, c=c: e.activation(Yo[:, :, 64 * c:64 * c + 64], y_[:, 0:T].rearrange("p (f i) -> p f i", f=4), ACT.Copy), tok)
                        banks.done(by, [t])
                        t_yo.append(t)
                        if c % 2:
                            run(after)
                            after = norm(c // 2, t_yo)
                    run(filler)
                    run(after)

            with ExitStack() as s2:
                Z = sb(s2, [P, 15, T + 1])
                t_z0 = pool(lambda e: e.memset(Z[:, :, 0:1], 0.0))
                tz = [None] * 15
                gcol = np.concatenate([np.arange(1792, 1824), np.full(96, -1)])
                order = [12, 13, 14] + list(range(4, 8)) + list(range(0, 4)) + list(range(8, 12))
                zcols = (pieces(0, 1792) + [gcol])

                def evac_z(n, out, tok):
                    j = order[n]
                    zj, zp = Z[:, j, 1:T + 1], Z[:, j, 0:T]
                    t0 = act(lambda e: e.activation(zj, out, ACT.Copy), tok)
                    i = scr.get()
                    d = scr.tiles[i][:, :]
                    t = pool(lambda e: e.tensor_tensor(d, zp, zj, ALU.subtract), t0, t_z0, scr.free[i])
                    tz[j] = dve(lambda e: e.scalar_tensor_tensor(zj, d, par_col("ab_shift_mix_2", j), zj, ALU.mult, ALU.add), t)
                    scr.free[i] = tz[j]
                    return [t0]

                with ExitStack() as s3:
                    cM = sb(s3, [P, sum(w for _, w in atM.values())])
                    t_cM = pr.op("act", lambda e: e.dma_start(cM[:, :], dram["cM"]), None, sem="ld_M", step=16)

                    def CM(name):
                        o, w = atM[name]
                        return cM[:, o:o + w]

                    S_ring = Ring([sb(s3, [P, 512]) for _ in range(3)])
                    T_ring = Ring([sb(s3, [P, 512]) for _ in range(2)])
                    small = mk_small(s3)
                    Q, K, V = sb(s3, [P, 4, T]), sb(s3, [P, 4, T]), sb(s3, [P, 2, 512])
                    turning = mk_turning(s3, CM("cos2"), CM("sin2"), CM("perm2"), t_cM)
                    tqk, tv = [], []

                    def place_qk(j):
                        return [(Q[:, j, :] if j < 4 else K[:, j - 4, :], 0, P)], -(128.0 ** -0.5) if j < 4 else 1.0, tqk, None

                    run(rotated("ab_w_in_2", 0, range(8), pieces(1824, 2848), H, turning, place_qk, together=True))
                    run(by_token("ab_w_in_2", 0, range(8), np.arange(2848, 3360), H, T, V, tv))
                    cz = CM("causal")
                    heads = []
                    for h in range(4):
                        def qk(ps, free, h=h):
                            mm(ps[:, 0:P], Q[:, h, 0:P], K[:, h, 0:P], True, True, [free, tqk])
                            return mm(ps[:, P:P + T], Q[:, h, P:T], K[:, h, :], True, True, sig=True)
                        heads.append(head(qk=[qk], masks=[[cz[:, 0:P], cz[:, T:2 * T]]], widths=[P, T], deps=[t_cM], d=P,
                                          v=lambda kb, h=h: V[:, kb, P * h:P * h + P], vdeps=tv,
                                          out=(ym[:, h, :], ym[:, 4 + h, :], ytok)))
                    banks.assign(lin=SOME, att=ATT)
                    filler = project("ab_w_in_2", 0, range(8), [zcols[j] for j in order], H, evac_z)
                    weave(attention(heads, S_ring, T_ring, small), filler, 2)
                    run(filler)
                    banks.assign(lin=ALL, att=ALL)
                tp = prep(Z, tz)
            t_y = [[] for _ in range(4)]
            filler = residual("ab_w_out_2", 0, range(4, 8), Act2(ym[:, 0:4, :], ym[:, 4:8, :], ytok), ALPHA, per_unit=4)
            scan(tp, Hh, Hl, t_y, filler)
            sums = Sums(8, True)
            run(residual("ab_w_out_2", 0, range(4), Act2(Hh, Hl, t_y), 1.0, sums, per_unit=4))
            return sums

    def dilated(H):
        with ExitStack() as s1:
            cD = sb(s1, [P, sum(w for _, w in atD.values())])
            pr.fence(["act", "dve", "pool"])
            n_t = atD["dil0"][0]
            t_cDt = pr.op("act", lambda e: e.dma_start(cD[:, 0:n_t], dram["cD"][:, 0:n_t]), None, sem="ld_Dt", step=16)
            t_cD = pr.op("act", lambda e: e.dma_start(cD[:, n_t:], dram["cD"][:, n_t:]), None, sem="ld_D", step=16)

            def CD(name):
                o, w = atD[name]
                return cD[:, o:o + w]

            yh, yl = sb(s1, [P, 8, T], F32R), sb(s1, [P, 8, T], F32R)
            ytok = [[], []]
            S_ring = Ring([sb(s1, [P, 384]) for _ in range(9)])
            T_ring = Ring([sb(s1, [P, 384]) for _ in range(2)])
            small = mk_small(s1)
            turning = mk_turning(s1, CD("cos2"), CD("sin2"), CD("perm2"), t_cDt)
            sets = [(sb(s1, [P, 12, T]), sb(s1, [P, 4, T]), sb(s1, [P, 2, 512])) for _ in range(2)]

            def inputs_of(hg, tq, tv):
                Q, K, V = sets[hg]
                tiles = [np.arange(D * g + P * h, D * g + P * h + P) for h in range(4 * hg, 4 * hg + 4) for g in range(4)]

                def place(j):
                    h, g = j // 4, j % 4
                    return [(Q[:, 3 * h + g, :] if g < 3 else K[:, h, :], 0, P)], -(128.0 ** -0.5) if g < 3 else 1.0, tq, None

                yield from rotated("c_w_in_2", 0, range(8), tiles, H, turning, place, together=(hg == 0))
                v0 = 4 * D + 512 * hg
                yield from by_token("c_w_in_2", 0, range(8), np.arange(v0, v0 + 512), H, T, V, tv)

            def heads_of(hg, tq, tv):
                Q, K, V = sets[hg]
                heads = []
                for h in range(4):
                    def qk(ps, fr, h, g):
                        mm(ps[:, 0:P], Q[:, 3 * h + g, 0:P], K[:, h, 0:P], True, True, [fr, tq])
                        return mm(ps[:, P:P + T], Q[:, 3 * h + g, P:T], K[:, h, :], True, True, sig=True)
                    heads.append(head(qk=[lambda ps, fr, h=h, g=g: qk(ps, fr, h, g) for g in range(3)],
                                      masks=[[CD(f"dil{g}")[:, 0:P], CD(f"dil{g}")[:, T:2 * T]] for g in range(3)], widths=[P, T],
                                      deps=[t_cD], d=P, v=lambda kb, h=h: V[:, kb, P * h:P * h + P], vdeps=tv,
                                      out=(yh[:, 4 * hg + h, :], yl[:, 4 * hg + h, :], ytok[hg])))
                return heads

            tq, tv = [[], []], [[], []]
            run(inputs_of(0, tq[0], tv[0]))
            banks.assign(lin=SOME, att=ATT)
            filler = inputs_of(1, tq[1], tv[1])
            weave(attention(heads_of(0, tq[0], tv[0]), S_ring, T_ring, small), filler, 3)
            run(filler)
            Y = Act2(yh, yl, None)
            Y.toks = ytok[0] + [None] * 4
            filler = residual("c_w_out_2", 0, range(4), Y, ALPHA, per_unit=4)
            weave(attention(heads_of(1, tq[1], tv[1]), S_ring, T_ring, small), filler, 1)
            run(filler)
            banks.assign(lin=ALL, att=ALL)
            Y2 = Act2(yh, yl, [None] * 4 + ytok[1])
            sums = Sums(8, True)
            run(residual("c_w_out_2", 0, range(4, 8), Y2, 1.0, sums, per_unit=4, xk=[4, 5, 6, 7]))
            return sums

    with top:
        sums = Sums(8)
        for k in range(8):
            sums.add(X[:, k, :], t_x)
        W.first()
        for l in range(2):
            sums = mixer1(l, sums)
            sums = ffn1(l, sums)
        H = rms_split(X, 8, "final_g", sums, Hh, Hl, keep=X)
        sums = rwkv_moba(H)
        H = layer_norm(sums, "ln1_g_20", "ln1_b_20")
        sums = mlp2(0, H)
        H = layer_norm(sums, "ln2_g_20", "ln2_b_20")
        sums = dilated(H)
        H = layer_norm(sums, "ln1_g_21", "ln1_b_21")
        sums = mlp2(1, H)
        xt = layer_norm(sums, "ln2_g_21", "ln2_b_21", split=False)
        t_out = pr.op("sp", lambda e: e.dma_start(dram["out"], X[:, :, :]), [xt], sem="st", step=16)
        pr.op("sp", None, [t_out], sig=False)

        if specs is not None:
            assert W.specs == specs
            sems = {s: top.enter_context(nc.semaphore(f"s_{s}")) for s in sorted(pr.count)}
            block = top.enter_context(nc.Block())

            def play(e, name):
                for waits, fn, s, step in pr.q[name]:
                    for ws, wv in waits:
                        e.wait_ge(sems[ws], wv)
                    if fn is not None:
                        ins = fn(e)
                        if s is not None:
                            ins.then_inc(sems[s], step)

            block.sync(lambda e: play(e, "sp"))
            block.tensor(lambda e: play(e, "pe"))
            block.vector(lambda e: play(e, "dve"))
            block.scalar(lambda e: play(e, "act"))
            block.gpsimd(lambda e: play(e, "pool"))
    return W.specs


def lay_unit(inputs, spec):
    name, layer, rows, cols = spec
    a = inputs[name][layer]
    cols = np.array(cols)
    parts = []
    for k in rows:
        block = np.zeros((P, len(cols)), a.dtype)
        block[:, cols >= 0] = a[k * P:(k + 1) * P, cols[cols >= 0]]
        parts.append(block)
    return np.concatenate(parts, axis=1).reshape(-1)


def lay_params(inputs):
    cols = []
    for key, name, idx in param_list():
        v = inputs[name][idx].reshape(-1)
        w = -(-v.size // P)
        pad = np.zeros(w * P, v.dtype)
        pad[:v.size] = v
        cols.append(pad.reshape(w, P).T)
    for l in range(2):
        cols.append(np.broadcast_to(inputs["gqa_sink"][l][None, :], (P, 8)))
    return np.ascontiguousarray(np.concatenate(cols, axis=1))


def lay_bias(rpb):
    out = np.zeros((2, 64, 8, 7, 64), rpb.dtype)
    for c in range(64):
        k = np.arange(max(0, c - 15), min(64, c + 16))
        out[:, c, :, :, k] = np.moveaxis(rpb[:, :, 4:11, k - c + 15], 3, 0)
    return out


def kernel(**inputs):
    import concourse.bacc as bacc
    from concourse.bass_utils import run_bass_kernel_spmd as run

    inputs = {k: np.asarray(v) for k, v in inputs.items()}
    c = shape_constants()
    packs = [pack(n, c) for n in (CONST1, CONST_A, CONST_M, CONST_W, CONST_D)]
    atP = param_places()
    places = [p[0] for p in packs] + [atP]

    scratch = bacc.Bacc("TRN2", target_bir_lowering=False, num_devices=1)

    def tensors(nc, total):
        shapes = {"x": (P, 8, T), "c1": packs[0][1].shape, "cA": packs[1][1].shape, "cM": packs[2][1].shape,
                  "cW": packs[3][1].shape, "cD": packs[4][1].shape, "par": (P, atP[1]), "w": (total,),
                  "rpb": (2, 64, 8, 7, 64), "lora": (P, 3, 512)}
        d = {k: nc.dram_tensor(f"in_{k}", s, F32, kind="ExternalInput").ap() for k, s in shapes.items()}
        d["out"] = nc.dram_tensor("out_0", (P, 8, T), F32, kind="ExternalOutput").ap()
        return d

    specs = program(scratch, tensors(scratch, P), places, None, [])
    offsets, total = [], 0
    for _, _, rows, cols in specs:
        offsets.append(total)
        total += P * len(rows) * len(cols)
    nc = bacc.Bacc("TRN2", target_bir_lowering=False, num_devices=1)
    program(nc, tensors(nc, total), places, specs, offsets)

    lora = np.zeros((P, 3, 512), np.float32)
    lora[0:64, 0] = inputs["ab_w_up_2"][0]
    lora[64:128, 0] = inputs["ab_a_up_2"][0]
    lora[:, 1] = inputs["ab_g_up_2"][0][0:128]
    lora[0:32, 2] = inputs["ab_g_up_2"][0][128:160]
    feed = {"in_x": np.ascontiguousarray(inputs["x"][0].T.reshape(8, P, T).transpose(1, 0, 2)),
            "in_c1": packs[0][1], "in_cA": packs[1][1], "in_cM": packs[2][1], "in_cW": packs[3][1], "in_cD": packs[4][1],
            "in_par": lay_params(inputs), "in_rpb": lay_bias(inputs["na_rpb"]), "in_lora": lora,
            "in_w": np.concatenate([lay_unit(inputs, s) for s in specs])}
    got = run(nc, [feed], core_ids=[0]).results[0]["out_0"]
    return np.ascontiguousarray(got.transpose(1, 0, 2).reshape(D, T).T)[None]
```

```python
from contextlib import ExitStack

import numpy as np
import concourse.bass as bass
from concourse import mybir

F32 = mybir.dt.float32
F32R = mybir.dt.float32r
ALU = mybir.AluOpType
ACT = mybir.ActivationFunctionType
AX = mybir.AxisListType

P = 128
T = 256
D = 1024
DFF = 2816
BIG = 1e30
KAPPA = float(np.exp(np.float32(-0.5)))
ALPHA = float(4.0 ** 0.25)
UNIT = 2048
NRAW, NHI, NLO, AHEAD_HI, AHEAD_LO = 4, 4, 3, 3, 2


def shape_constants():
    i = np.arange(P)
    tok = np.arange(T)
    c = {}
    c["ident"] = np.eye(P)
    c["ones"] = np.ones((P, P))
    c["half"] = (i[:, None] // 64 == i[None, :] // 64) * 1.0

    def rope(dim, rot, theta, width):
        half = rot // 2
        f = i % width
        if dim == rot:
            inv = 1.0 / (np.float32(theta) ** (np.arange(0, dim, 2, dtype=np.float32) / np.float32(dim)))
        else:
            inv = np.float32(theta) ** (-np.arange(half, dtype=np.float32) / np.float32(half))
        ang = tok.astype(np.float32)[None, :] * inv.astype(np.float32)[f % half][:, None]
        cs = np.where((f < rot)[:, None], np.cos(ang), 1.0)
        sn = np.where((f < rot)[:, None], np.sin(ang), 0.0)
        perm = np.zeros((P, P))
        for m in range(P):
            if f[m] < half:
                perm[m + half, m] = -1.0
            elif f[m] < rot:
                perm[m - half, m] = 1.0
        return cs, sn, perm

    c["cos1"], c["sin1"], c["perm1"] = rope(64, 64, 10000.0, 64)
    c["cos2"], c["sin2"], c["perm2"] = rope(128, 32, 500000.0, 128)
    cq = np.arange(64)
    start = np.clip(cq - 8, 0, 48)
    inside = (cq[None, :] >= start[:, None]) & (cq[None, :] < start[:, None] + 16)
    c["namask"] = np.tile(np.where(inside, 0.0, BIG), (2, 1))

    def both(ok):
        m = np.where(ok, 0.0, BIG)
        return np.concatenate([m[0:P], m[P:T]], axis=1)

    q, k = tok[:, None], tok[None, :]
    c["gmask"] = both(np.abs(q - k) <= 128)
    c["causal"] = both(k <= q)
    c["dil0"] = both((k <= q) & (q - k <= 128))
    c["dil1"] = both((k <= q) & ((q - k) % 4 == 0))
    c["dil2"] = both((k <= q) & ((q - k) % 16 == 0))
    a = i % 64
    j = np.arange(64)
    for n in range(6):
        m = 1 << n
        t, s = j[None, :], a[:, None]
        c[f"lev{n}"] = ((t // (2 * m) == s // (2 * m)) & (t % (2 * m) >= m) & (s % (2 * m) < m)) * 1.0
    c["strict"] = (j[None, :] > a[:, None]) * 1.0
    c["incl"] = (j[None, :] >= a[:, None]) * 1.0
    c["id64"] = (j[None, :] == a[:, None]) * 1.0
    c["eps"] = np.tile(np.array([[1e-6, 1e-5, 64e-5, 0.0]]), (P, 1))
    return c


CONST1 = ["ident", "ones", "half", "eps"]
CONST_A = ["cos1", "sin1", "perm1", "namask", "gmask"]
CONST_M = ["cos2", "sin2", "perm2", "causal"]
CONST_W = ["lev0", "lev1", "lev2", "lev3", "lev4", "lev5", "strict", "incl", "id64"]
CONST_D = ["cos2", "sin2", "perm2", "dil0", "dil1", "dil2"]


def pack(names, c):
    at, cols, n = {}, [], 0
    for name in names:
        at[name] = (n, c[name].shape[1])
        cols.append(c[name])
        n += c[name].shape[1]
    return at, np.ascontiguousarray(np.concatenate(cols, axis=1).astype(np.float32))


def param_list():
    out = []
    for l in range(2):
        for name in ("norm1_g", "b_gate", "mla_qa_g", "mla_kva_g", "norm2_g", "conv_b"):
            out.append((f"{name}{l}", name, (l,)))
        for t in range(3):
            out.append((f"conv{t}_{l}", "conv_w", (l, t)))
        for name in ("ln1_g_2", "ln1_b_2", "ln2_g_2", "ln2_b_2"):
            out.append((f"{name}{l}", name, (l,)))
    out.append(("final_g", "final_g", ()))
    for name in ("ab_shift_mix_2", "ab_w0_2", "ab_a0_2", "ab_k_k_2", "ab_k_a_2", "ab_r_k_2", "ab_lnx_g_2", "ab_lnx_b_2"):
        out.append((name, name, (0,)))
    return out


PARAM_LEN = {"norm1_g": 1024, "b_gate": 3072, "mla_qa_g": 384, "mla_kva_g": 256, "norm2_g": 1024, "conv_b": 5632,
             "conv_w": 5632, "ln1_g_2": 1024, "ln1_b_2": 1024, "ln2_g_2": 1024, "ln2_b_2": 1024, "final_g": 1024,
             "ab_shift_mix_2": 1824, "ab_w0_2": 512, "ab_a0_2": 512, "ab_k_k_2": 512, "ab_k_a_2": 512,
             "ab_r_k_2": 512, "ab_lnx_g_2": 512, "ab_lnx_b_2": 512}


def param_places():
    at, n = {}, 0
    for key, name, _ in param_list():
        w = -(-PARAM_LEN[name] // P)
        at[key] = n
        n += w
    at["sink0"] = n
    at["sink1"] = n + 8
    return at, n + 16


class Prog:

    ENGINES = ("pe", "dve", "act", "pool", "sp")

    def __init__(self):
        self.q = {e: [] for e in self.ENGINES}
        self.count = {}
        self.seen = {e: {} for e in self.ENGINES}
        self.extra = {e: [] for e in self.ENGINES}

    def waits(self, e, deps):
        need = {}
        stack = [deps, self.extra[e]]
        while stack:
            x = stack.pop()
            if x is None:
                continue
            if isinstance(x, list):
                stack.extend(x)
            else:
                need[x[0]] = max(need.get(x[0], 0), x[1])
        self.extra[e] = []
        out = []
        for s, v in need.items():
            if self.seen[e].get(s, 0) < v:
                self.seen[e][s] = v
                out.append((s, v))
        return out

    def op(self, e, fn, deps=None, sig=True, sem=None, step=1):
        w = self.waits(e, [deps])
        s = sem or e
        self.q[e].append((w, fn, s if sig else None, step))
        if sig:
            self.count[s] = self.count.get(s, 0) + step
            return (s, self.count[s])
        return None

    def last(self, e):
        return (e, self.count[e]) if self.count.get(e) else None

    def fence(self, engines, after=("pe", "dve", "act", "pool")):
        tokens = [self.last(x) for x in after]
        for e in engines:
            self.extra[e] = self.extra[e] + tokens


class Banks:

    def __init__(self, tiles):
        self.tiles = tiles
        self.free = [[] for _ in tiles]
        self.open = [False] * len(tiles)
        self.sets = {}
        self.n = {}

    def assign(self, **sets):
        self.sets = sets
        self.n = {k: 0 for k in sets}

    def get(self, kind="lin"):
        ring = self.sets[kind]
        b = ring[self.n[kind] % len(ring)]
        self.n[kind] += 1
        assert not self.open[b], "PSUM bank still in use"
        self.open[b] = True
        return b

    def done(self, b, tokens):
        self.free[b] = tokens
        self.open[b] = False

    def done_stat(self, tokens):
        self.free[7] = tokens


class Weights:

    def __init__(self, pr, specs):
        self.pr, self.specs, self.known = pr, [], specs
        self.n = self.hi_to = self.lo_to = self.loaded = 0
        self.pe_done, self.hi_done, self.parts_done, self.raw_done = {}, {}, {}, {}

    def start(self, dram, raw, hi, lo, offsets):
        self.dram, self.raw, self.hi, self.lo, self.offsets = dram, raw, hi, lo, offsets
        for _ in range(min(NRAW, len(self.known or []))):
            self.load()

    def width(self, u):
        name, layer, rows, cols = self.known[u]
        return len(rows) * len(cols)

    def load(self):
        u = self.loaded
        if u >= len(self.known):
            return
        self.loaded += 1
        n = self.width(u)
        src = self.dram[self.offsets[u]:self.offsets[u] + P * n].rearrange("(p n) -> p n", p=P)
        dst = self.raw[u % NRAW][:, 0:n]
        self.raw_done[u] = self.pr.op("sp", lambda e: e.dma_start(dst, src),
                                      [self.parts_done.get(u - NRAW)], sem=f"w{u % NRAW}", step=16)

    def split_hi(self, u):
        n = self.width(u)
        raw, hi = self.raw[u % NRAW][:, 0:n], self.hi[u % NHI][:, 0:n]
        self.hi_done[u] = self.pr.op("act", lambda e: e.activation(hi, raw, ACT.Copy), [self.raw_done[u], self.pe_done.get(u - NHI)])

    def split_lo(self, u):
        n = self.width(u)
        raw, hi, lo = self.raw[u % NRAW][:, 0:n], self.hi[u % NHI][:, 0:n], self.lo[u % NLO][:, 0:n]
        t = self.pr.op("dve", lambda e: e.tensor_tensor(lo, raw, hi.bitcast(F32), ALU.subtract),
                       [self.hi_done[u], self.raw_done[u], self.pe_done.get(u - NLO)])
        self.parts_done[u] = [self.hi_done[u], t]
        self.load()

    def use(self, name, layer, rows, cols):
        u = self.n
        self.n += 1
        self.specs.append((name, layer, tuple(rows), tuple(int(c) for c in cols)))
        assert u == 0 or u - 1 in self.pe_done, "weight units are used one after another"
        self.ahead(u)
        if not self.known:
            self.parts_done[u] = []
        return u

    def ahead(self, u):
        if self.known:
            while self.hi_to < min(u + AHEAD_HI + 1, len(self.known)) or self.lo_to < min(u + AHEAD_LO + 1, len(self.known)):
                if self.hi_to < len(self.known):
                    self.split_hi(self.hi_to)
                    self.hi_to += 1
                if self.lo_to < self.hi_to - (AHEAD_HI - AHEAD_LO) or self.hi_to == len(self.known):
                    self.split_lo(self.lo_to)
                    self.lo_to += 1

    def first(self):
        if self.known:
            self.split_hi(0)
            self.split_lo(0)
            self.hi_to = self.lo_to = 1

    def part(self, u, k, c0, c1, low):
        nc = len(self.specs[u][3])
        t = (self.lo if low else self.hi)[u % (NLO if low else NHI)]
        return t[:, k * nc + c0:k * nc + c1]

    def done(self, u, token):
        self.pe_done[u] = token


def program(nc, dram, places, specs, offsets):
    tag = "a" if specs is None else "b"
    pr = Prog()
    W = Weights(pr, specs)
    names = [0]
    at1, atA, atM, atW, atD, atP = places
    top = ExitStack()

    def sb(ctx, shape, dt=F32):
        names[0] += 1
        return ctx.enter_context(nc.sbuf_tensor(f"{tag}{names[0]}", shape, dt))

    def op(e, fn, *deps):
        return pr.op(e, fn, list(deps))

    def dve(fn, *deps):
        return pr.op("dve", fn, list(deps))

    def act(fn, *deps):
        return pr.op("act", fn, list(deps))

    def pool(fn, *deps):
        return pr.op("pool", fn, list(deps))

    def mm(out, lhsT, rhs, start, stop, deps=None, sig=False):
        return pr.op("pe", lambda e: e.matmul(out, lhsT, rhs, start=start, stop=stop), deps, sig=sig)

    banks = Banks([top.enter_context(nc.psum_tensor(f"{tag}ps{b}", [P, 512], F32)) for b in range(8)])
    raw = [sb(top, [P, UNIT]) for _ in range(NRAW)]
    whi = [sb(top, [P, UNIT], F32R) for _ in range(NHI)]
    wlo = [sb(top, [P, UNIT], F32R) for _ in range(NLO)]
    X = sb(top, [P, 8, T])
    Hh = sb(top, [P, 8, T], F32R)
    Hl = sb(top, [P, 8, T], F32R)
    c1 = sb(top, [P, sum(w for _, w in at1.values())])
    par = sb(top, [P, atP[1]])
    shift = sb(top, [P, T])
    nst = sb(top, [P, 16])
    STAT = 7
    banks.assign(lin=list(range(7)), att=list(range(7)))

    def C(name, a=0, b=None):
        o, w = at1[name]
        return c1[:, o + a:o + (w if b is None else b)]

    def par_col(key, j=0):
        o = atP[0][key] + j
        return par[:, o:o + 1]

    ident, ones, half = C("ident"), C("ones"), C("half")
    eps_rms, eps_ln, eps_gn = C("eps", 0, 1), C("eps", 1, 2), C("eps", 2, 3)

    t_x = pr.op("sp", lambda e: e.dma_start(X[:, :, :], dram["x"]), sem="ld_x", step=16)
    t_c1 = pr.op("sp", lambda e: e.dma_start(c1[:, :], dram["c1"]), sem="ld_c", step=16)
    t_par = pr.op("sp", lambda e: e.dma_start(par[:, :], dram["par"]), sem="ld_p", step=16)
    W.start(dram["w"], raw, whi, wlo, offsets)
    for e in ("pe", "act", "dve", "pool"):
        pr.extra[e] = [t_c1, t_par]

    class Ring:
        def __init__(self, tiles):
            self.tiles, self.free, self.n = tiles, [None] * len(tiles), 0

        def get(self):
            i = self.n % len(self.tiles)
            self.n += 1
            return i

    scr = Ring([sb(top, [P, T]) for _ in range(4)])

    class Act2:

        def __init__(self, hi, lo, toks):
            self.hi, self.lo, self.toks = hi, lo, toks

    def split_act(src, hi, lo, *deps, eng="dve"):
        t1 = act(lambda e: e.activation(hi, src, ACT.Copy), *deps)
        t2 = op(eng, lambda e: e.tensor_tensor(lo, src, hi.bitcast(F32), ALU.subtract), t1, *deps)
        return [t1, t2]

    def feature_tiles(name, layer, rows, tile_cols, x, per_unit=None, kpart=None, xk=None, together=False):
        nk = len(rows)
        xk = xk or list(range(nk))
        kpart = kpart or nk
        per_unit = per_unit or max(1, UNIT // (kpart * P))
        n = len(tile_cols)
        b = None
        for j in range(0, n, per_unit):
            g = list(range(j, min(j + per_unit, n)))
            cols = np.concatenate([tile_cols[i] for i in g])
            parts = [list(range(a, min(a + kpart, nk))) for a in range(0, nk, kpart)]
            assert len(parts) == 1 or len(g) == 1
            for pi, ks in enumerate(parts):
                u = W.use(name, layer, [rows[k] for k in ks], cols)
                if together and j == 0:
                    bs = [banks.get() for _ in g]
                    for k in ks:
                        for gi, b in enumerate(bs):
                            out = banks.tiles[b][:, 0:T]
                            wh, wl = W.part(u, k, gi * P, gi * P + P, False), W.part(u, k, gi * P, gi * P + P, True)
                            mm(out, wh, x.hi[:, xk[k], :], k == 0, False, [W.parts_done[u], banks.free[b], x.toks[xk[k]]])
                            mm(out, wl, x.hi[:, xk[k], :], False, False)
                            tok = mm(out, wh, x.lo[:, xk[k], :], False, k == nk - 1, sig=True)
                    W.done(u, tok)
                    for i, b in zip(g, bs):
                        yield i, banks.tiles[b][:, 0:T], b, tok
                    continue
                for gi, i in enumerate(g):
                    if pi == 0:
                        b = banks.get()
                    out = banks.tiles[b][:, 0:T]
                    deps = [W.parts_done[u], banks.free[b]]
                    for q, k in enumerate(ks):
                        first, last = k == 0, k == nk - 1
                        wh = W.part(u, q, gi * P, gi * P + P, False)
                        wl = W.part(u, q, gi * P, gi * P + P, True)
                        mm(out, wh, x.hi[:, xk[k], :], first, False, [deps if q == 0 else None, x.toks[xk[k]]])
                        mm(out, wh, x.lo[:, xk[k], :], False, False)
                        tok = mm(out, wl, x.hi[:, xk[k], :], False, last, sig=(q == len(ks) - 1))
                    if gi == len(g) - 1:
                        W.done(u, tok)
                    if pi == len(parts) - 1:
                        yield i, out, b, tok

    def project(name, layer, rows, tile_cols, x, evac, **kw):
        for j, out, b, tok in feature_tiles(name, layer, rows, tile_cols, x, **kw):
            banks.done(b, evac(j, out, tok))
            yield

    def by_token(name, layer, rows, cols, x, width, dst, tokens, *deps):
        nk = len(rows)
        for c0 in range(0, len(cols), width):
            cc = cols[c0:c0 + width]
            w = len(cc)
            u = W.use(name, layer, rows, cc)
            b = banks.get()
            for tb in range(2):
                out = banks.tiles[b][:, tb * w:tb * w + w]
                first = [W.parts_done[u], banks.free[b]]
                for k in range(nk):
                    xh, xl = x.hi[:, k, tb * P:tb * P + P], x.lo[:, k, tb * P:tb * P + P]
                    mm(out, xh, W.part(u, k, 0, w, False), k == 0, False, [first if k == 0 else None, x.toks[k]])
                    mm(out, xl, W.part(u, k, 0, w, False), False, False)
                    tok = mm(out, xh, W.part(u, k, 0, w, True), False, k == nk - 1, sig=(k == nk - 1))
            W.done(u, tok)
            d, s_ = dst[:, :, c0:c0 + w], banks.tiles[b][:, 0:2 * w].rearrange("p (a c) -> p a c", a=2)
            t = act(lambda e, d=d, s_=s_: e.activation(d, s_, ACT.Copy), tok, *deps)
            tokens.append(t)
            banks.done(b, [t])
            yield

    def pieces(a, b):
        return [np.arange(c, c + P) for c in range(a, b, P)]

    def run(*gens):
        for g in gens:
            for _ in g:
                pass

    def chain(*gens):
        for g in gens:
            yield from g

    def weave(main, filler, per_step):
        for i, _ in enumerate(main):
            for _ in range(per_step):
                next(filler, None)

    class Sums:

        def __init__(self, n, values=False):
            self.n, self.values, self.k, self.pend = n, values, 0, None
            self.out = banks.tiles[STAT]

        def add(self, src, dep):
            self.flush()
            i = scr.get()
            sq = scr.tiles[i][:, :]
            t = act(lambda e: e.activation(sq, src, ACT.Square), dep, scr.free[i])
            self.pend = (src, sq, t, i)

        def flush(self):
            if self.pend is None:
                return
            src, sq, t, i = self.pend
            kinds = [(0, src), (2, sq)] if self.values else [(2, sq)]
            first, last = self.k == 0, self.k == self.n - 1
            for c, x in kinds:
                for tb in range(2):
                    mm(self.out[:, c + tb:c + tb + 1], x[:, tb * P:tb * P + P], ones[:, 0:1], first, last and c + tb == 3,
                       [t, banks.free[STAT] if first else None], sig=(c + tb == 3))
                    first = False
            scr.free[i] = self.tok = pr.last("pe")
            self.k += 1
            self.pend = None

        def finish(self):
            self.flush()
            assert self.k == self.n
            return self.tok

    def ready_root():
        act(lambda e: e.activation(nst[:, 12:13], eps_rms, ACT.Sqrt))

    norm_free = [None]

    def spread(c, deps):
        b = banks.get()
        for tb in range(2):
            tok = mm(banks.tiles[b][:, tb * P:tb * P + P], nst[:, c + tb:c + tb + 1].broadcast_to([P, P]), ident, True, True,
                     [deps, banks.free[b]], sig=True)
        norm_free[0] = tok
        return b, tok

    def rms_root(n, sums):
        tok = sums.finish()
        t = act(lambda e: e.activation(nst[:, 0:2], sums.out[:, 2:4], ACT.Sqrt, bias=eps_rms, scale=1.0 / (n * P)), tok, norm_free[0])
        banks.done_stat([t])
        return dve(lambda e: e.reciprocal(nst[:, 2:4], nst[:, 0:2]), t, norm_free[0])

    def rms_split(src, n, gkey, sums, hi, lo, keep=None):
        return rms_apply(src, n, gkey, rms_root(n, sums), hi, lo, keep)

    def rms_apply(src, n, gkey, t_root, hi, lo, keep=None):
        b, t = spread(2, t_root)
        root = banks.tiles[b][:, 0:T]
        toks, td, ds = [], [], []
        for m in range(n + 1):
            if m < n:
                i = scr.get() if keep is None else None
                d, free = (scr.tiles[i][:, :], scr.free[i]) if keep is None else (keep[:, m, :], None)
                g, s_ = par_col(gkey, m), src[:, m, :]
                td.append(dve(lambda e, d=d, s_=s_, g=g: e.scalar_tensor_tensor(d, s_, g, root, ALU.mult, ALU.mult), t, free))
                ds.append((i, d))
            if m:
                k = m - 1
                i, d = ds[k]
                toks.append(split_act(d, hi[:, k, :], lo[:, k, :], td[k], eng="pool" if k % 2 else "dve"))
                if i is not None:
                    scr.free[i] = toks[k]
        banks.done(b, td)
        return Act2(hi, lo, toks)

    def layer_norm(sums, key_g, key_b, split=True):
        tok = sums.finish()
        mean, var, r, mr = nst[:, 4:6], nst[:, 0:2], nst[:, 2:4], nst[:, 8:10]
        t = dve(lambda e: e.tensor_scalar(mean, sums.out[:, 0:2], 1.0 / D, None, ALU.mult), tok, norm_free[0])
        t = dve(lambda e: e.tensor_tensor(nst[:, 6:8], mean, mean, ALU.mult), t)
        t = dve(lambda e: e.scalar_tensor_tensor(var, sums.out[:, 2:4], 1.0 / D, nst[:, 6:8], ALU.mult, ALU.subtract), t)
        banks.done_stat([t])
        t = dve(lambda e: e.tensor_scalar(var, var, 0.0, None, ALU.max), t)
        t = act(lambda e: e.activation(var, var, ACT.Sqrt, bias=eps_ln), t)
        t = dve(lambda e: e.reciprocal(r, var), t)
        t_mr = dve(lambda e: e.scalar_tensor_tensor(mr, mean, -1.0, r, ALU.mult, ALU.mult), t)
        b, t = spread(2, t)
        b2, t_mr = spread(8, t_mr)
        root, off = banks.tiles[b][:, 0:T], banks.tiles[b2][:, 0:T]
        toks, td, ta, tx, offs = [None] * 8, [], [], [], []
        for n in range(10):
            if n < 8:
                x, g, bb = X[:, n, :], par_col(key_g, n), par_col(key_b, n)
                i = scr.get()
                o = scr.tiles[i][:, :]
                ta.append(act(lambda e, o=o, g=g, bb=bb: e.activation(o, off, ACT.Identity, bias=bb, scale=g), t_mr, scr.free[i]))
                td.append(dve(lambda e, x=x, g=g: e.scalar_tensor_tensor(x, x, g, root, ALU.mult, ALU.mult), t))
                offs.append((i, o))
            if 1 <= n < 9:
                k = n - 1
                x, (i, o) = X[:, k, :], offs[k]
                tx.append(dve(lambda e, x=x, o=o: e.tensor_tensor(x, x, o, ALU.add), ta[k], td[k]))
                scr.free[i] = tx[k]
                toks[k] = [tx[k]]
                if split:
                    hi = Hh[:, k, :]
                    toks[k] = [act(lambda e, x=x, hi=hi: e.activation(hi, x, ACT.Copy), tx[k])]
            if n >= 2 and split:
                k = n - 2
                x, hi, lo = X[:, k, :], Hh[:, k, :], Hl[:, k, :]
                toks[k].append(op("pool" if k % 2 else "dve", lambda e, x=x, hi=hi, lo=lo: e.tensor_tensor(lo, x, hi.bitcast(F32), ALU.subtract),
                                  toks[k], tx[k]))
        banks.done(b, td)
        banks.done(b2, ta)
        return Act2(Hh, Hl, toks) if split else toks

    def residual(name, layer, rows, x, scale, sums=None, **kw):
        early = []

        def take_shift(t):
            b = banks.get()
            tok = mm(banks.tiles[b][:, 0:T], ones, X[:, 0, :], True, True, [t, banks.free[b]], sig=True)
            ts = act(lambda e: e.mul(shift[:, :], banks.tiles[b][:, 0:T], 1.0 / P), tok)
            banks.done(b, [ts])
            return ts

        def less_shift(k, t, t_shift):
            xk = X[:, k, :]
            return op("dve" if k == 7 else "pool", lambda e: e.tensor_tensor(xk, xk, shift[:, :], ALU.subtract), t, t_shift)

        t_shift = []

        def evac(j, out, tok):
            xj = X[:, j, :]
            if scale == 1.0:
                t = dve(lambda e: e.tensor_tensor(xj, xj, out, ALU.add), tok)
            else:
                t = dve(lambda e: e.scalar_tensor_tensor(xj, xj, scale, out, ALU.mult, ALU.add), tok)
            if sums is not None:
                if j == 2:
                    ready_root()
                if not sums.values:
                    sums.add(xj, t)
                elif j == 0:
                    early.append(t)
                else:
                    if j == 1:
                        t_shift.append(take_shift(early[0]))
                        sums.add(X[:, 0, :], less_shift(0, early[0], t_shift))
                    sums.add(xj, less_shift(j, t, t_shift))
            return [t]
        return project(name, layer, rows, pieces(0, D), x, evac, **kw)

    def mk_turning(ctx, cos, sin, perm, t_tables):
        return {"raw": [sb(ctx, [P, T]) for _ in range(2)], "tmp": [sb(ctx, [P, T]) for _ in range(2)],
                "cos": cos, "sin": sin, "perm": perm, "t_tables": t_tables, "n": 0, "read": [None, None]}

    def rotated(name, layer, rows, tile_cols, x, tn, place, **kw):
        moved = {}

        def turn(j):
            i, t_moved = moved.pop(j)
            z, tmp = tn["raw"][i][:, :], tn["tmp"][i][:, :]
            dst, scale, sink, t_dst = place(j)
            b = banks.get()
            out = banks.tiles[b][:, 0:T]
            tok = mm(out, tn["perm"], z, True, True, [t_moved, tn["t_tables"], banks.free[b]], sig=True)
            t_sin = dve(lambda e: e.scalar_tensor_tensor(tmp, out, scale, tn["sin"], ALU.mult, ALU.mult), tok, tn["read"][i])
            banks.done(b, [t_sin])
            t_cos = dve(lambda e: e.scalar_tensor_tensor(z, z, scale, tn["cos"], ALU.mult, ALU.mult), tok)
            res = [dve(lambda e, d=d, r0=r0, r1=r1: e.tensor_tensor(d, z[r0:r1, :], tmp[r0:r1, :], ALU.add), t_sin, t_cos, t_dst)
                   for d, r0, r1 in dst]
            tn["read"][i] = res
            sink.extend(res)

        for j, out, b, tok in feature_tiles(name, layer, rows, tile_cols, x, **kw):
            i = tn["n"] % 2
            tn["n"] += 1
            z = tn["raw"][i][:, :]
            if not (kw.get("together") and j == 1):
                for k in sorted(moved):
                    turn(k)
            t_moved = act(lambda e, z=z, out=out: e.activation(z, out, ACT.Copy), tok, tn["read"][i])
            banks.done(b, [t_moved])
            moved[j] = (i, t_moved)
            yield
        turn(len(tile_cols) - 1)

    def attention(heads, rS, rT, small, fine=False):
        lag = {"s": 0, "t": 2, "v": 3}
        n = len(heads)

        def scores(h):
            h["col"] = col = small["n"] % small["size"]
            small["n"] += 1
            w = h["widths"]
            st = small["tile"]
            mn, l, r = st[:, col, 0:2], st[:, col, 2:4], st[:, col, 4:6]
            ng = len(h["qk"])
            h["bufs"] = []
            prev = [[small["free"][col]], [small["free"][col]]]
            toks_min = [None, None]
            for g in range(ng):
                b = banks.get("att")
                tok = h["qk"][g](banks.tiles[b], banks.free[b])
                i = rS.get()
                S = rS.tiles[i]
                h["bufs"].append(i)
                if h["masks"][g] is None:
                    t = dve(lambda e, b=b: e.tensor_reduce(mn, banks.tiles[b][:, :].rearrange("p (a k) -> p a k", a=2),
                                                           AX.X, ALU.min), tok, prev[0])
                    toks_min = [t, t]
                    h["src"] = banks.tiles[b]
                    h["bank"] = b
                else:
                    ts = []
                    o = 0
                    for qb in range(2):
                        init = 3.0e38 if g == 0 else mn[:, qb:qb + 1]
                        if h.get("sink") is not None:
                            init = h["sink"]
                        dst, ps, mk = S[:, o:o + w[qb]], banks.tiles[b][:, o:o + w[qb]], h["masks"][g][qb]
                        t = dve(lambda e, dst=dst, ps=ps, mk=mk, init=init, qb=qb: e.tensor_tensor_reduce(
                            dst, ps, mk, 1.0, init, ALU.add, ALU.min, mn[:, qb:qb + 1]), tok, rS.free[i], prev[qb], h["deps"])
                        toks_min[qb] = t
                        prev[qb] = [t]
                        ts.append(t)
                        o += w[qb]
                    banks.done(b, ts)
            te = []
            for g in range(ng):
                S = rS.tiles[h["bufs"][g]]
                o = 0
                for qb in range(2):
                    src = S if h["masks"][g] is not None else h["src"]
                    acc = l[:, qb:qb + 1] if ng == 1 else st[:, col, 6 + 2 * g + qb:7 + 2 * g + qb]
                    t = act(lambda e, S=S, src=src, o=o, qb=qb, acc=acc: e.activation(
                        S[:, o:o + w[qb]], src[:, o:o + w[qb]], ACT.Exp, bias=mn[:, qb:qb + 1], scale=-1.0, accum_out=acc),
                        toks_min, rS.free[h["bufs"][g]] if h["masks"][g] is None else None)
                    te.append(t)
                    o += w[qb]
                if h["masks"][g] is None:
                    banks.done(h["bank"], te)
            tot = sum(w)
            S0 = rS.tiles[h["bufs"][0]]
            if ng == 1 and h.get("sink") is not None:
                for qb in range(2):
                    te.append(act(lambda e, qb=qb: e.activation(st[:, col, 6 + qb:7 + qb], h["sink"], ACT.Exp,
                                                                bias=mn[:, qb:qb + 1], scale=-1.0), toks_min))
                t = dve(lambda e: e.tensor_tensor(l, l, st[:, col, 6:8], ALU.add), te)
            elif ng == 3:
                t = dve(lambda e: e.tensor_tensor(l, st[:, col, 6:8], st[:, col, 8:10], ALU.add), te)
                t = dve(lambda e: e.tensor_tensor(l, l, st[:, col, 10:12], ALU.add), t)
                S1, S2 = rS.tiles[h["bufs"][1]], rS.tiles[h["bufs"][2]]
                t2 = pool(lambda e: e.tensor_tensor(S0[:, 0:tot], S0[:, 0:tot], S1[:, 0:tot], ALU.add), te)
                t3 = dve(lambda e: e.tensor_tensor(S0[:, 0:tot], S0[:, 0:tot], S2[:, 0:tot], ALU.add), t2)
                rS.free[h["bufs"][1]] = t2
                rS.free[h["bufs"][2]] = t3
                t = [t, t3]
            else:
                t = te
            t = dve(lambda e: e.reciprocal(r, l), t, te)
            o = 0
            h["p"] = []
            for qb in range(2):
                h["p"].append(dve(lambda e, o=o, qb=qb: e.tensor_scalar(S0[:, o:o + w[qb]], S0[:, o:o + w[qb]], r[:, qb:qb + 1],
                                                                       None, ALU.mult), t))
                o += w[qb]
            small["free"][col] = h["p"]

        def turn(h):
            w = h["widths"]
            i = h["bufs"][0]
            S = rS.tiles[i]
            b = banks.get("att")
            h["pt"] = []
            o = 0
            first = [banks.free[b], h["p"]]
            for qb in range(2):
                for kb in range(w[qb] // P):
                    slot = len(h["pt"])
                    h["pt"].append((kb, qb))
                    out, src = banks.tiles[b][:, slot * P:slot * P + P], S[:, o + kb * P:o + kb * P + P]
                    tok = pr.op("pe", lambda e, out=out, src=src: e.transpose(out, src, ident), first, sig=True)
                    first = None
                o += w[qb]
            rS.free[i] = tok
            j = rT.get()
            h["T"] = j
            n_ = len(h["pt"]) * P
            dst, src = rT.tiles[j][:, 0:n_], banks.tiles[b][:, 0:n_]
            t = act(lambda e: e.activation(dst, src, ACT.Copy), tok, rT.free[j])
            banks.done(b, [t])
            h["tt"] = t

        pair = {}

        def values(h):
            d = h["d"]
            TT = rT.tiles[h["T"]]
            base = h["base"]
            if base == 0:
                pair["b"] = banks.get("att")
            b = pair["b"]
            first = [banks.free[b], h["tt"], h["vdeps"]]
            w = h["widths"]
            for qb in range(2):
                kbs = [kb for kb, q in h["pt"] if q == qb]
                out = banks.tiles[b][base:base + d, qb * P:qb * P + P]
                for x, kb in enumerate(kbs):
                    slot = h["pt"].index((kb, qb))
                    tok = mm(out, h["v"](kb), TT[:, slot * P:slot * P + P], x == 0, x == len(kbs) - 1, first, sig=(x == len(kbs) - 1))
                    first = None
            rT.free[h["T"]] = tok
            if base + d == P:
                src = banks.tiles[b][:, 0:T]
                hi, lo, sink_list = h["out"]
                t1 = act(lambda e: e.activation(hi, src, ACT.Copy), tok, h["odeps"])
                t2 = dve(lambda e: e.tensor_tensor(lo, src, hi.bitcast(F32), ALU.subtract), t1)
                banks.done(b, [t1, t2])
                sink_list.append([t1, t2])

        for i in range(n + 3):
            if i < n:
                scores(heads[i])
            if fine:
                yield
            if 0 <= i - lag["t"] < n:
                turn(heads[i - lag["t"]])
            if 0 <= i - lag["v"] < n:
                values(heads[i - lag["v"]])
            yield

    def mk_small(ctx):
        return {"tile": sb(ctx, [P, 6, 12]), "n": 0, "size": 6, "free": [None] * 6}

    ALL, SOME, ATT = list(range(7)), [0, 1, 2], [3, 4, 5, 6]

    def head(**kw):
        return dict(dict(deps=None, base=0, sink=None, odeps=None), **kw)

    def mixer1(l, sums_in):
        with ExitStack() as s1:
            cA = sb(s1, [P, sum(w for _, w in atA.values())])

            def CA(name):
                o, w = atA[name]
                return cA[:, o:o + w]

            y0, y1 = sb(s1, [P, 8, T], F32R), None
            ytok = [[], [], []]
            S_ring = Ring([sb(s1, [P, 512]) for _ in range(3)])
            T_ring = Ring([sb(s1, [P, 512]) for _ in range(2)])
            small = mk_small(s1)
            nsink = sb(s1, [P, 8])
            gq, gk, gv, kp = sb(s1, [P, 4, T]), sb(s1, [P, 4, T]), sb(s1, [P, 2, P]), sb(s1, [P, 2, T])
            cqn_h, cqn_l = sb(s1, [P, 3, T], F32R), sb(s1, [P, 3, T], F32R)
            ckn_h, ckn_l = sb(s1, [P, 2, T], F32R), sb(s1, [P, 2, T], F32R)
            pr.fence(["act", "dve", "pool"])
            t_cA = []
            turning = mk_turning(s1, CA("cos1"), CA("sin1"), CA("perm1"), t_cA)
            o_s = atP[0][f"sink{l}"]
            t_sink = pool(lambda e: e.tensor_scalar(nsink[:, :], par[:, o_s:o_s + 8], -1.0, None, ALU.mult))
            tz1 = pool(lambda e: e.memset(kp[:, :, :], 0.0))
            tz2 = pool(lambda e: e.memset(gk[:, :, :], 0.0))
            made = {}
            tkp, tgq, tgk, tgv = [], [], [], []

            with ExitStack() as s2:
                bias = sb(s2, [P, 8, 2, T])
                Q, K, V = sb(s2, [P, 4, T]), sb(s2, [P, 8, T]), sb(s2, [P, 2, 512])
                cq, ck = sb(s2, [P, 3, T]), sb(s2, [P, 2, T])
                t_z = pool(lambda e: e.memset(K[:, :, :], 0.0))
                tb = []
                nm = CA("namask").unsqueeze(1).broadcast_to([P, 64, 64])
                bv = bias[:, :, :, :].rearrange("p h q (r c) -> p (h q r) c", c=64)
                H = rms_split(X, 8, f"norm1_g{l}", sums_in, Hh, Hl)
                tq, tk, tv = [], [], []

                def evac_q(j, out, tok):
                    tq.append(act(lambda e: e.mul(Q[:, j, :], out, -0.125), tok))
                    return tq[-1:]

                def evac_k(j, out, tok):
                    t1 = dve(lambda e: e.tensor_copy(K[0:64, 2 * j, :], out[0:64, :]), tok, t_z)
                    t2 = act(lambda e: e.activation(K[64:128, 2 * j + 1, :], out[64:128, :], ACT.Copy), tok, t_z)
                    tk.extend([t1, t2])
                    return [t1, t2]

                run(project("w_in", l, range(8), pieces(0, 512), H, evac_q, together=True))
                t_cA.append(pr.op("act", lambda e: e.dma_start(cA[:, :], dram["cA"]), None, sem="ld_A", step=16))
                for rq in range(4):
                    src = dram["rpb"][l, :, :, 3 - rq:7 - rq, :].rearrange("p h r c -> p h (r c)")
                    r2, qb = rq % 2, rq // 2
                    dst = bias[64 * r2:64 * r2 + 64, :, qb, :]
                    tb.append(pr.op("act", lambda e, src=src, dst=dst: e.dma_start(dst, src), None, sem=f"ld_b{rq}", step=16))
                t_bias = pool(lambda e: e.tensor_tensor(bv, nm, bv, ALU.subtract), tb, t_cA)
                run(project("w_in", l, range(8), pieces(512, 1024), H, evac_k),
                    by_token("w_in", l, range(8), np.arange(1024, 1536), H, T, V, tv))

                def latent():
                    sums = Sums(3)

                    def evac(j, out, tok):
                        dst = cq[:, j, :] if j < 3 else ck[:, j - 3, :]
                        t = act(lambda e: e.activation(dst, out, ACT.Copy), tok)
                        made["s"].add(dst, t)
                        return [t]
                    made["s"] = sums
                    for n, _ in enumerate(project("w_in", l, range(8), pieces(1536, 2176), H, evac)):
                        if n == 2:
                            t = rms_root(3, sums)
                            made["s"] = Sums(2)
                        if n == 3:
                            made["cq"] = rms_apply(cq, 3, f"mla_qa_g{l}", t, cqn_h, cqn_l)
                        yield
                    t = rms_root(2, made["s"])
                    yield
                    made["ck"] = rms_apply(ck, 2, f"mla_kva_g{l}", t, ckn_h, ckn_l)

                kr = np.arange(2176, 2240)
                tiles = [np.concatenate([kr, kr])] + pieces(2240, 2752)
                for g in range(2):
                    k0 = np.arange(2752 + 64 * g, 2816 + 64 * g)
                    tiles.append(np.concatenate([k0, k0]))

                def place_g(j):
                    if j == 0:
                        return [(kp[0:64, 0, :], 0, 64), (kp[64:128, 1, :], 64, 128)], 1.0, tkp, tz1
                    if j < 5:
                        return [(gq[:, j - 1, :], 0, 128)], -0.125, tgq, None
                    g = j - 5
                    return [(gk[0:64, 2 * g, :], 0, 64), (gk[64:128, 2 * g + 1, :], 64, 128)], 1.0, tgk, tz2

                filler = chain(latent(), rotated("w_in", l, range(8), tiles, H, turning, place_g),
                               by_token("w_in", l, range(8), np.arange(2880, 3008), H, P, gv, tgv))
                heads = []
                for h in range(8):
                    def qk(ps, free, h=h):
                        for qb in range(2):
                            tok = mm(ps[:, qb * T:qb * T + T], Q[:, h // 2, qb * P:qb * P + P], K[:, h, :], True, True,
                                     [free, tq, tk] if qb == 0 else None, sig=True)
                        return tok
                    heads.append(head(qk=[qk], masks=[[bias[:, h, 0, :], bias[:, h, 1, :]]], widths=[T, T], deps=[t_bias], d=64,
                                      base=64 * (h % 2), v=lambda kb, h=h: V[:, kb, 64 * h:64 * h + 64], vdeps=tv,
                                      out=(y0[:, h // 2, :], y0[:, 4 + h // 2, :], ytok[0])))
                banks.assign(lin=SOME, att=ATT)
                weave(attention(heads, S_ring, T_ring, small), filler, 1)
                run(filler)
                banks.assign(lin=ALL, att=ALL)

            with ExitStack() as s2:
                pr.fence(["act", "dve", "pool"])
                y1, y2 = sb(s2, [P, 8, T], F32R), sb(s2, [P, 8, T], F32R)
                mg = sb(s2, [P, 8, T])
                qn, qp, kn, vm = sb(s2, [P, 4, T]), sb(s2, [P, 2, T]), sb(s2, [P, 4, T]), sb(s2, [P, 2, 512])
                sc = -(192.0 ** -0.5)
                tiles = [np.arange(192 * h, 192 * h + P) for h in range(4)]
                tiles += [np.concatenate([np.arange(192 * h + P, 192 * h + 192) for h in (2 * c, 2 * c + 1)]) for c in range(2)]
                tqn, tqp, tkn, tvm = [], [], [], []

                def evac_uq(j, out, tok):
                    tqn.append(act(lambda e: e.mul(qn[:, j, :], out, sc), tok))
                    return tqn[-1:]

                def evac_uk(j, out, tok):
                    tkn.append(dve(lambda e: e.tensor_copy(kn[:, j, :], out), tok))
                    return tkn[-1:]

                vc = np.concatenate([np.arange(256 * h + P, 256 * h + 256) for h in range(4)])
                run(rotated("mla_w_uq", l, range(3), tiles[4:6], made["cq"], turning, lambda j: ([(qp[:, j, :], 0, 128)], sc, tqp, None), per_unit=2),
                    project("mla_w_uq", l, range(3), tiles[0:4], made["cq"], evac_uq, per_unit=4),
                    project("mla_w_ukv", l, range(2), [np.arange(256 * h, 256 * h + P) for h in range(4)], made["ck"], evac_uk, per_unit=4),
                    by_token("mla_w_ukv", l, range(2), vc, made["ck"], T, vm, tvm))
                ys = [y0, y1, y2]
                mtok = [None] * 8
                last_pe = {}

                def branch(br):
                    name = ["w_br_na", "w_br_mla", "w_br_gqa"][br]
                    Y = Act2(ys[br][:, 0:4, :], ys[br][:, 4:8, :], ytok[br])
                    G = {}

                    def evac_gate(j, out, tok):
                        i = scr.get()
                        G[j] = i
                        bg = par_col(f"b_gate{l}", 8 * br + j)
                        t = act(lambda e: e.activation(scr.tiles[i][:, :], out, ACT.Sigmoid, bias=bg), tok, scr.free[i])
                        G[j] = (i, t)
                        return [t]

                    def evac_br(j, out, tok):
                        i, tg = G[j]
                        g, m = scr.tiles[i][:, :], mg[:, j, :]
                        if br == 0:
                            t = dve(lambda e: e.tensor_tensor(m, g, out, ALU.mult), tok, tg)
                            mtok[j] = t
                            scr.free[i] = t
                            return [t]
                        t = dve(lambda e: e.tensor_tensor(g, g, out, ALU.mult), tok, tg)
                        t2 = pool(lambda e: e.tensor_tensor(m, m, g, ALU.add), t, mtok[j])
                        scr.free[i] = t2
                        mtok[j] = t2
                        if br == 2:
                            mtok[j] = split_act(m, y0[:, j, :], y1[:, j, :], t2, last_pe["t"], eng="dve")
                        last_pe["t"] = tok
                        return [t]

                    gates = project("w_in", l, range(8), pieces(3008 + D * br, 3008 + D * br + D), H, evac_gate)
                    brs = project(name, l, range(4), pieces(0, D), Y, evac_br, per_unit=2)
                    for j in range(4):
                        for g in (gates, gates, brs, brs):
                            next(g)
                            yield
                    run(gates, brs)

                heads = []
                for h in range(4):
                    def qk(ps, free, h=h):
                        for qb in range(2):
                            mm(ps[:, qb * T:qb * T + T], qn[:, h, qb * P:qb * P + P], kn[:, h, :], True, False,
                               [free, tqn, tqp, tkn, tkp] if qb == 0 else None)
                            tok = mm(ps[:, qb * T:qb * T + T], qp[:, h // 2, qb * P:qb * P + P], kp[:, h % 2, :], False, True, sig=True)
                        return tok
                    heads.append(head(qk=[qk], masks=[None], widths=[T, T], d=P, v=lambda kb, h=h: vm[:, kb, P * h:P * h + P], vdeps=tvm,
                                      out=(y1[:, h, :], y1[:, 4 + h, :], ytok[1])))
                gm = CA("gmask")
                for h in range(8):
                    def qk(ps, free, h=h):
                        for qb in range(2):
                            tok = mm(ps[:, qb * T:qb * T + T], gq[:, h // 2, qb * P:qb * P + P], gk[:, 2 * (h // 4) + h % 2, :], True, True,
                                     [free, tgq, tgk] if qb == 0 else None, sig=True)
                        return tok
                    heads.append(head(qk=[qk], masks=[[gm[:, 0:T], gm[:, T:2 * T]]], widths=[T, T], deps=[t_cA, t_sink], d=64,
                                      base=64 * (h % 2), sink=nsink[:, h:h + 1], v=lambda kb, h=h: gv[:, kb, 64 * (h // 4):64 * (h // 4) + 64],
                                      vdeps=tgv, out=(y2[:, h // 2, :], y2[:, 4 + h // 2, :], ytok[2])))
                banks.assign(lin=SOME, att=ATT)
                filler = chain(branch(0), branch(1))
                weave(attention(heads, S_ring, T_ring, small, fine=True), filler, 1)
                run(filler)
                banks.assign(lin=ALL, att=ALL)
                run(branch(2))
                sums = Sums(8)
                run(residual("w_out", l, range(8), Act2(y0, y1, mtok), 1.0, sums))
                return sums

    def ffn1(l, sums_in):
        with ExitStack() as s1:
            pr.fence(["act", "dve", "pool"])
            fh, fl = sb(s1, [P, 22, T], F32R), sb(s1, [P, 22, T], F32R)
            H = rms_split(X, 8, f"norm2_g{l}", sums_in, Hh, Hl)
            ab = Ring([sb(s1, [P, 2, T]) for _ in range(4)])
            ft = [None] * 22
            tiles = []
            for m in range(22):
                tiles += [np.arange(P * m, P * m + P), np.arange(DFF + P * m, DFF + P * m + P)]
            cur = {}

            def second(m, i, tt):
                A = ab.tiles[i]
                t = act(lambda e: e.activation(A[:, 1, :], A[:, 1, :], ACT.Gelu_apprx_tanh), tt)
                t = dve(lambda e: e.tensor_tensor(A[:, 0, :], A[:, 0, :], A[:, 1, :], ALU.mult), t)
                ft[m] = split_act(A[:, 0, :], fh[:, m, :], fl[:, m, :], t, eng="pool")
                ab.free[i] = ft[m]

            def evac(j, out, tok):
                m, g = j // 2, j % 2
                f = 22 * g + m
                if g == 0:
                    if "pend" in cur:
                        cur["late"] = cur.pop("pend")
                    cur["i"], cur["tt"] = ab.get(), []
                i = cur["i"]
                A = ab.tiles[i][:, g, :]
                t = act(lambda e: e.activation(A, out, ACT.Identity, bias=par_col(f"conv_b{l}", f), scale=par_col(f"conv1_{l}", f)), tok, ab.free[i])
                t = dve(lambda e: e.scalar_tensor_tensor(A[:, 1:T], out[:, 0:T - 1], par_col(f"conv0_{l}", f), A[:, 1:T], ALU.mult, ALU.add), t)
                t = dve(lambda e: e.scalar_tensor_tensor(A[:, 0:T - 1], out[:, 1:T], par_col(f"conv2_{l}", f), A[:, 0:T - 1], ALU.mult, ALU.add), t)
                cur["tt"].append(t)
                if g:
                    if "late" in cur:
                        second(*cur.pop("late"))
                    cur["pend"] = (m, i, cur["tt"])
                return [t]

            run(project("w_up", l, range(8), tiles, H, evac, together=True))
            second(*cur["pend"])
            sums = Sums(8)
            run(residual("w_down", l, range(22), Act2(fh, fl, ft), 1.0, sums, kpart=11))
            return sums

    def mlp2(l, H):
        with ExitStack() as s1:
            pr.fence(["act", "dve", "pool"])
            fh, fl = sb(s1, [P, 32, T], F32R), sb(s1, [P, 32, T], F32R)
            ring = Ring([sb(s1, [P, T]) for _ in range(4)])
            ft = [None] * 32

            def evac(j, out, tok):
                i = ring.get()
                R = ring.tiles[i][:, :]
                t0 = dve(lambda e: e.tensor_scalar(R, out, 0.0, None, ALU.max), tok, ring.free[i])
                t = act(lambda e: e.activation(R, R, ACT.Square), t0)
                ft[j] = split_act(R, fh[:, j, :], fl[:, j, :], t, eng="pool")
                ring.free[i] = ft[j]
                return [t0]

            run(project("mlp_w1_2", l, range(8), pieces(0, 4096), H, evac, together=True))
            sums = Sums(8, True)
            run(residual("mlp_w2_2", l, range(32), Act2(fh, fl, ft), ALPHA, sums, kpart=16))
            return sums

    def turn_tokens(src, dst, dep):
        res = []
        for tb in range(2):
            b = banks.get()
            first = [dep, banks.free[b]]
            for c in range(4):
                o, s = banks.tiles[b][:, c * P:c * P + P], src[:, c, tb * P:tb * P + P]
                tok = pr.op("pe", lambda e, o=o, s=s: e.transpose(o, s, ident), first, sig=True)
                first = None
            t = act(lambda e, tb=tb, b=b: e.activation(dst[:, tb, :], banks.tiles[b][:, :], ACT.Copy), tok, dep)
            banks.done(b, [t])
            res.append(t)
        return res

    def rwkv_moba(H):
        with ExitStack() as s1:
            pr.fence(["act", "dve", "pool"])
            ym = sb(s1, [P, 8, T], F32R)
            ytok = []
            bonus, gate, KH, BH = (sb(s1, [P, 4, T]) for _ in range(4))
            AR = sb(s1, [P, 4, 4, 2, 64])
            Vt, FC = sb(s1, [P, 2, 512]), sb(s1, [P, 4, 4])

            half2 = half[:, 0:P:64]

            def head_sums(out, src, deps):
                for f in range(4):
                    tok = mm(out[:, 2 * f:2 * f + 2], src[:, f, :], half2, True, True, deps if f == 0 else None, sig=True)
                return tok

            def head_spread(out, r, deps):
                for h in range(8):
                    p = slice(64 * (h % 2), 64 * (h % 2) + 64)
                    tok = mm(out[p, h // 2 * P:h // 2 * P + P], r[:, h:h + 1].broadcast_to([P, 64]), ident, True, True,
                             deps if h == 0 else None, sig=True)
                return tok

            def prep(Z, tz, lora, t_l, small3, tp):
                mid, end, hst = small3
                kk, ex, aa, sig = (t[:, :, :] for t in (BH, KH, bonus, gate))
                cs = Vt[:, :, :].rearrange("p a (c t) -> p (a c) t", t=T)
                v4 = lambda t: t.rearrange("p c (k i) -> p c k i", i=64)
                fl2 = lambda t: t.rearrange("p c t -> p (c t)")
                cs4, sg4, ex4, kk4 = v4(cs), v4(sig), v4(ex), v4(kk)
                R, K, V = Z[:, 0:4, 1:T + 1], Z[:, 4:8, 1:T + 1], Z[:, 8:12, 1:T + 1]
                wd, ad, g1, g2 = Z[0:64, 12, 1:T + 1], Z[64:128, 12, 1:T + 1], Z[:, 13, 1:T + 1], Z[0:32, 14, 1:T + 1]
                t_w = act(lambda e: e.activation(wd, wd, ACT.Tanh), tz[12])
                t_g1 = act(lambda e: e.activation(g1, g1, ACT.Sigmoid), tz[13])
                t_g2 = act(lambda e: e.activation(g2, g2, ACT.Sigmoid), tz[14])
                t_one = pool(lambda e: e.memset(ex, 1.0))
                t_one = pool(lambda e: e.memset(ex4[:, :, :, 0:1], 0.0), t_one)
                tk = [pool(lambda e, c=c: e.tensor_scalar(kk[:, c, :], K[:, c, :], par_col("ab_k_k_2", c), None, ALU.mult), tz[4 + c])
                      for c in range(4)]
                yield
                ts, ta, tg = [], [], []
                for c in range(4):
                    cc = slice(P * c, P * c + P)
                    b = banks.get()
                    o1 = banks.tiles[b][:, 0:T]
                    t1 = mm(o1, lora[0:64, 0, cc], wd, True, True, [t_w, t_l, banks.free[b]], sig=True)
                    ts.append(act(lambda e, c=c, o1=o1: e.activation(sig[:, c, :], o1, ACT.Sigmoid, bias=par_col("ab_w0_2", c)), t1))
                    banks.done(b, ts[-1:])
                    if c % 2:
                        yield
                for c in range(4):
                    cc = slice(P * c, P * c + P)
                    b = banks.get()
                    o2 = banks.tiles[b][:, 0:T]
                    t2 = mm(o2, lora[64:128, 0, cc], ad, True, True, [t_l, tz[12], banks.free[b]], sig=True)
                    ta.append(act(lambda e, c=c, o2=o2: e.activation(aa[:, c, :], o2, ACT.Sigmoid, bias=par_col("ab_a0_2", c)), t2))
                    banks.done(b, ta[-1:])
                    if c % 2:
                        yield
                t_cs = dve(lambda e: e.tensor_tensor_scan(fl2(cs), fl2(ex), fl2(sig), 0.0, ALU.mult, ALU.add), t_one, ts)
                t_m = dve(lambda e: e.tensor_copy(mid[:, :, :], cs4[:, :, :, 31]), t_cs)
                t_c = []
                for c in range(4):
                    mb = mid[:, c, :].unsqueeze(2).broadcast_to([P, 4, 64])
                    t_c.append(dve(lambda e, c=c, mb=mb: e.tensor_tensor(cs4[:, c], cs4[:, c], mb, ALU.subtract), t_m))
                yield
                t_d = dve(lambda e: e.tensor_tensor(sig, cs, sig, ALU.subtract), t_c)
                t_e = pool(lambda e: e.tensor_tensor(end[:, :, 0:3], cs4[:, :, 0:3, 63], mid[:, :, 1:4], ALU.add), t_c)
                t_one = pool(lambda e: e.memset(FC[:, :, 3:4], 1.0))
                t_x = act(lambda e: e.activation(ex, cs, ACT.Exp, scale=-KAPPA), t_c, t_cs)
                t_xa = act(lambda e: e.activation(sig, sig, ACT.Exp, scale=-KAPPA), t_d)
                yield
                t_F = [act(lambda e: e.activation(FC[:, :, 0:3], end[:, :, 0:3], ACT.Exp, scale=-KAPPA), t_e), t_one]
                t_xk = act(lambda e: e.activation(cs, cs, ACT.Exp, scale=KAPPA), t_e, t_x, t_d)
                t_r = [dve(lambda e, c=c: e.tensor_tensor(AR[:, c, :, 1, :], v4(R)[:, c], ex4[:, c], ALU.mult), t_x, tz[c]) for c in range(4)]
                yield
                t_sq = act(lambda e: e.activation(ex, kk, ACT.Square), tk, t_r)
                yield
                b = banks.get()
                for tb in range(2):
                    tok = head_sums(banks.tiles[b][:, 8 * tb:8 * tb + 8], ex[:, :, tb * P:tb * P + P], [t_sq, banks.free[b]])
                hs = banks.tiles[b][:, 0:16]
                t = dve(lambda e: e.tensor_scalar(hst[:, :], hs, 1e-24, None, ALU.max), tok)
                banks.done(b, [t])
                t = act(lambda e: e.activation(hst[:, :], hst[:, :], ACT.Sqrt), t)
                t_h = dve(lambda e: e.reciprocal(hst[:, :], hst[:, :]), t)
                yield
                tn = []
                for tb in range(2):
                    b = banks.get()
                    tok = head_spread(banks.tiles[b], hst[:, 8 * tb:8 * tb + 8], [t_h, banks.free[b]])
                    k_, ps = kk[:, :, tb * P:tb * P + P], banks.tiles[b][:, :].rearrange("p (f t) -> p f t", f=4)
                    tn.append(dve(lambda e, k_=k_, ps=ps: e.tensor_tensor(k_, k_, ps, ALU.mult), tok))
                    banks.done(b, tn[-1:])
                yield
                t_a = [dve(lambda e, c=c: e.scalar_tensor_tensor(AR[:, c, :, 0, :], kk4[:, c], -1.0, sg4[:, c],
                                                                 ALU.mult, ALU.mult), tn, t_xa) for c in range(4)]
                t = dve(lambda e: e.tensor_tensor(kk, kk, aa, ALU.mult), t_a, ta, tn)
                t_b = dve(lambda e: e.tensor_tensor(kk, kk, cs, ALU.mult), t, t_xk)
                tk2 = []
                ta2 = [pool(lambda e, c=c: e.tensor_scalar(aa[:, c, :], aa[:, c, :], -1.0, par_col("ab_k_a_2", c), ALU.add, ALU.mult), t)
                       for c in range(4)]
                yield
                for c in range(4):
                    cc = slice(P * c, P * c + P)
                    b = banks.get()
                    o3 = banks.tiles[b][:, 0:T]
                    mm(o3, lora[:, 1, cc], g1, True, False, [t_g1, t_g2, t_l, banks.free[b]])
                    t3 = mm(o3, lora[0:32, 2, cc], g2, False, True, sig=True)
                    tg.append(act(lambda e, c=c, o3=o3: e.activation(gate[:, c, :], o3, ACT.Copy), t3, t_a))
                    banks.done(b, tg[-1:])
                    tk2.append(dve(lambda e, c=c: e.scalar_tensor_tensor(K[:, c, :], aa[:, c, :], 1.0, K[:, c, :], ALU.add, ALU.mult), ta2[c], tk))
                    if c % 2:
                        yield
                tb_ = [dve(lambda e, c=c: e.scalar_tensor_tensor(ex[:, c, :], R[:, c, :], par_col("ab_r_k_2", c), K[:, c, :],
                                                                 ALU.mult, ALU.mult), tk2[c], tn, tz[c]) for c in range(4)]
                yield
                t_bon, tok_b = [], []
                for c2 in range(2):
                    b = banks.get()
                    for c in range(2):
                        tok = mm(banks.tiles[b][:, c * T:c * T + T], half, ex[:, 2 * c2 + c, :], True, True, [tb_, banks.free[b]], sig=True)
                    tok_b.append(tok)
                    t = dve(lambda e, c2=c2, b=b: e.tensor_tensor(
                        bonus[:, 2 * c2:2 * c2 + 2, :], banks.tiles[b][:, :].rearrange("p (c t) -> p c t", c=2),
                        V[:, 2 * c2:2 * c2 + 2, :], ALU.mult), tok, tz[8:12], tk2)
                    banks.done(b, [t])
                    for f in (2 * c2, 2 * c2 + 1):
                        t_bon.append(pool(lambda e, f=f: e.tensor_scalar(bonus[:, f, :], bonus[:, f, :], par_col("ab_lnx_b_2", f), None, ALU.add), t))
                    yield
                t_k = dve(lambda e: e.tensor_tensor(ex, K, cs, ALU.mult), tk2, t_xk, tok_b)
                yield
                t_vt = turn_tokens(V, Vt, [tz[8:12], t_k, t_b])
                tp.update(a=t_a, r=t_r, b=t_b, k=t_k, F=t_F, bonus=t_bon, gate=tg, v=t_vt)

            def scan(tp, Yh, Yl, t_y, filler):
                with ExitStack() as s3:
                    cW = sb(s3, [P, sum(w for _, w in atW.values())])
                    Bt, Kt = sb(s3, [P, 2, 512]), sb(s3, [P, 2, 512])
                    NT, RB, AK, RK, XX, XT, YY = (sb(s3, [P, 8, 2, 64]) for _ in range(7))
                    ET = [sb(s3, [P, 8, 2, 64]) for _ in range(2)]
                    SZ, SF, gst = sb(s3, [P, 8, 64]), sb(s3, [P, 4, 64]), sb(s3, [P, 2, 8])
                    pr.fence(["act", "dve", "pool"])
                    t_cW = pr.op("act", lambda e: e.dma_start(cW[:, :], dram["cW"]), None, sem="ld_W", step=16)

                    def CW(name):
                        o, w = atW[name]
                        return cW[:, o:o + w]

                    strict, incl, id64 = CW("strict"), CW("incl"), CW("id64")
                    flat = lambda t: t[:, :, :, :].rearrange("p h b i -> p (h b) i")
                    chunks = lambda t: t[:, :, :, :].rearrange("p (f a) b i -> p f (a b) i", f=4)
                    t_s0 = pool(lambda e: e.memset(SZ[:, :, :], 0.0))
                    t_by = []
                    for src, buf, dst, dep in ((BH, XX, Bt, tp["b"]), (KH, YY, Kt, tp["k"])):
                        tt = []
                        for f in range(4):
                            s_ = src[:, f, :].rearrange("p (k i) -> p k i", i=64)
                            fb = FC[:, f, :].unsqueeze(2).broadcast_to([P, 4, 64])
                            o = chunks(buf)[:, f, :, :]
                            tt.append(pool(lambda e, o=o, s_=s_, fb=fb: e.tensor_tensor(o, s_, fb, ALU.mult), dep, tp["F"]))
                        t_by.append((buf, dst, tt))
                    tsc = {}
                    for n, L, dst, dep in ((0, BH, (NT, RB), tp["b"]), (1, KH, (AK, RK), tp["k"])):
                        tsc[n] = []
                        for tbk in range(2):
                            bb = [banks.get(), banks.get()]
                            tok = [None, None]
                            for f in range(4):
                                for c2, par2 in ((0, 0), (1, 1), (1, 0), (0, 1)):
                                    c, r0, p0 = 2 * tbk + c2, 64 * par2, 64 * c2
                                    tok[par2] = mm(banks.tiles[bb[par2]][p0:p0 + 64, f * P:f * P + P], L[r0:r0 + 64, f, 64 * c:64 * c + 64],
                                                   AR[r0:r0 + 64, f, c, :, :].rearrange("p a i -> p (a i)"), True, True,
                                                   [dep, tp["a"], tp["r"], banks.free[bb[0]], banks.free[bb[1]]] if f == 0 else None, sig=(f == 3))
                            for par2 in range(2):
                                src = banks.tiles[bb[par2]][:, :].rearrange("p (f a i) -> p f a i", f=4, a=2)
                                ts2 = []
                                for a2, m in ((0, strict), (1, incl)):
                                    mk = m.unsqueeze(1).broadcast_to([P, 4, 64])
                                    o = dst[a2][:, par2:8:2, tbk, :]
                                    ts2.append(dve(lambda e, o=o, a2=a2, mk=mk, src=src: e.tensor_tensor(o, src[:, :, a2, :], mk, ALU.mult),
                                                   tok[par2], t_cW))
                                banks.done(bb[par2], ts2)
                                tsc[n] += ts2

                    def products(lhs, rhs, deps):
                        res = []
                        for tbk in range(2):
                            b = banks.get()
                            for h in range(8):
                                for c2 in range(2):
                                    p = slice(64 * c2, 64 * c2 + 64)
                                    r = id64[p, :] if rhs is None else rhs[p, h, tbk, :]
                                    tok = mm(banks.tiles[b][p, 64 * h:64 * h + 64], lhs[p, h, tbk, :], r, True, True,
                                             [deps[tbk], banks.free[b]] if h + c2 == 0 else None, sig=(h == 7 and c2 == 1))
                            res.append((tbk, b, tok, banks.tiles[b][:, :].rearrange("p (h i) -> p h i", h=8)))
                        return res

                    idb = id64.unsqueeze(1).broadcast_to([P, 8, 64])
                    t_E = {}

                    def level(n, dep):
                        m = CW(f"lev{n}").unsqueeze(1).broadcast_to([P, 16, 64])
                        t_E[n] = pool(lambda e: e.tensor_tensor(flat(ET[n % 2]), flat(NT), m, ALU.mult), dep, tsc[0], t_cW)

                    level(0, None)
                    level(1, None)
                    t_X, t_XT = [None] * 2, [None] * 2
                    for tbk in range(2):
                        t_XT[tbk] = dve(lambda e, tbk=tbk: e.tensor_tensor(XT[:, :, tbk, :], ET[0][:, :, tbk, :], idb, ALU.add), t_E[0])
                    t_turned = [turn_tokens(buf[:, :, :, :].rearrange("p (f a) b i -> p f (a b i)", f=4), dst, tt) for buf, dst, tt in t_by]
                    for tbk, b, tok, ps in products(ET[0], None, [t_E[0]] * 2):
                        t_X[tbk] = dve(lambda e, ps=ps, tbk=tbk: e.tensor_tensor(XX[:, :, tbk, :], ps, idb, ALU.add), tok, t_turned)
                        banks.done(b, [t_X[tbk]])
                    for n in range(1, 6):
                        if n < 5:
                            level(n + 1, [pr.last("pe"), t_XT])
                        t_Y = [None] * 2
                        for tbk, b, tok, ps in products(ET[n % 2], XX, [[t_E[n], t_X[i]] for i in range(2)]):
                            t_Y[tbk] = dve(lambda e, ps=ps, tbk=tbk: e.tensor_tensor(YY[:, :, tbk, :], ps, idb, ALU.add), tok, t_turned)
                            banks.done(b, [t_Y[tbk]])
                        if n in (1, 2, 3, 4, 5):
                            next(filler, None)
                        ry = [[t_Y[i], t_XT[i]] for i in range(2)]
                        rx = products(XT, YY, ry) if n < 5 else []
                        rt = products(YY, XT, ry)
                        for tbk, b, tok, ps in rx:
                            t_X[tbk] = act(lambda e, ps=ps, tbk=tbk: e.activation(XX[:, :, tbk, :], ps, ACT.Copy), tok)
                            banks.done(b, [t_X[tbk]])
                        for tbk, b, tok, ps in rt:
                            t_XT[tbk] = dve(lambda e, ps=ps, tbk=tbk: e.tensor_copy(XT[:, :, tbk, :], ps), tok)
                            banks.done(b, [t_XT[tbk]])
                    spare = ET[0][:, :, :, :].rearrange("p h b i -> p (h b i)")
                    Gs, Us = spare[:, 0:512], spare[:, 512:1024]
                    Yo = KH
                    sq = YY[:, :, :, :].rearrange("p (f a) b i -> p f (a b i)", f=4)
                    hd = lambda h: slice(64 * h, 64 * h + 64)

                    def norm(tb, t_yo):
                        tt = slice(P * tb, P * tb + P)
                        yv, sv = Yo[:, :, tt], sq[:, :, tt]
                        b = banks.get()
                        tok = mm(banks.tiles[b][:, :], half, yv, True, True, [t_yo, banks.free[b]], sig=True)
                        ps = banks.tiles[b][:, :].rearrange("p (f t) -> p f t", f=4)
                        t = dve(lambda e: e.scalar_tensor_tensor(yv, ps, -1.0 / 64, yv, ALU.mult, ALU.add), tok)
                        banks.done(b, [t])
                        yield
                        t2 = act(lambda e: e.activation(sv, yv, ACT.Square), t)
                        b2 = banks.get()
                        hs, g8 = banks.tiles[b2][:, 0:8], gst[:, tb, :]
                        tok = head_sums(hs, sv, [t2, banks.free[b2]])
                        t3 = act(lambda e: e.activation(g8, hs, ACT.Sqrt, bias=eps_gn, scale=1.0 / 64), tok)
                        banks.done(b2, [t3])
                        t3 = dve(lambda e: e.reciprocal(g8, g8), t3)
                        yield
                        b3 = banks.get()
                        tok = head_spread(banks.tiles[b3], g8, [t3, banks.free[b3]])
                        ps3 = banks.tiles[b3][:, :].rearrange("p (f t) -> p f t", f=4)
                        t3 = dve(lambda e: e.tensor_tensor(yv, yv, ps3, ALU.mult), tok)
                        banks.done(b3, [t3])
                        yield
                        for f in range(4):
                            y1 = yv[:, f, :]
                            t4 = dve(lambda e, y1=y1, f=f: e.scalar_tensor_tensor(y1, y1, par_col("ab_lnx_g_2", f), bonus[:, f, tt], ALU.mult, ALU.add),
                                     t3, tp["bonus"])
                            t4 = dve(lambda e, y1=y1, f=f: e.tensor_tensor(y1, y1, gate[:, f, tt], ALU.mult), t4, tp["gate"])
                            t_y[f].append(split_act(y1, Yh[:, f, tt], Yl[:, f, tt], t4, eng="pool"))
                            yield

                    def source(c, bank):
                        rows, tbk = slice(64 * (c % 2), 64 * (c % 2) + 64), c // 2
                        for h in range(8):
                            tok = mm(banks.tiles[bank][rows, hd(h)], AK[rows, h, tbk, :], Vt[rows, tbk, hd(h)], h == 0, c == 0 and h == 7,
                                     [tp["v"], tsc[1], banks.free[bank]] if h == 0 else None, sig=True)
                        return tok

                    t_s, t_sf = [t_s0], [None, None]
                    t_yo = []
                    after = iter(())
                    bg = banks.get()
                    tok = source(0, bg)
                    for c in range(4):
                        rows, tbk = slice(64 * (c % 2), 64 * (c % 2) + 64), c // 2
                        if c:
                            for h in range(8):
                                tok = mm(banks.tiles[bg][rows, hd(h)], AR[:, h // 2, c, 0, :], SZ[:, h, :], False, h == 7,
                                         t_s if h == 0 else None, sig=(h == 7))
                        g = banks.tiles[bg]
                        t_g = act(lambda e, g=g, rows=rows: e.activation(Gs[rows, :], g[rows, :], ACT.Copy), tok, pr.last("pe"))
                        banks.done(bg, [t_g])
                        bs = banks.get() if c < 3 else None
                        by = banks.get()
                        half_of = lambda bank, h: banks.tiles[bank][64 * (h % 2):64 * (h % 2) + 64, 64 * (h // 2):64 * (h // 2) + 64]
                        for h in range(8):
                            if c < 3:
                                mm(half_of(bs, h), Kt[rows, tbk, hd(h)], Vt[rows, tbk, hd(h)], h < 2, False,
                                   [t_turned, banks.free[bs]] if h == 0 else None)
                            mm(half_of(by, h), Vt[rows, tbk, hd(h)], RK[rows, h, tbk, :], h < 2, False, [banks.free[by]] if h == 0 else None)
                            if c:
                                mm(half_of(by, h), SZ[:, h, :], AR[:, h // 2, c, 1, :], False, False)
                        bu = banks.get()
                        for h in range(8):
                            tok = mm(banks.tiles[bu][rows, hd(h)], XT[rows, h, tbk, :], Gs[rows, hd(h)], True, True,
                                     [t_g, t_XT, banks.free[bu]] if h == 0 else None, sig=(h == 7))
                        u = banks.tiles[bu]
                        t_u = dve(lambda e, u=u, rows=rows: e.tensor_copy(Us[rows, :], u[rows, :]), tok)
                        banks.done(bu, [t_u])
                        if c < 3:
                            bg = banks.get()
                            tok = source(c + 1, bg)
                        if c in (0, 1):
                            next(filler, None)
                        for _ in range(4 if c > 1 else 0):
                            next(after, None)
                        if c < 3:
                            for h in range(8):
                                tok_s = mm(half_of(bs, h), Bt[rows, tbk, hd(h)], Us[rows, hd(h)], False, h > 5, t_u if h == 0 else None, sig=(h == 7))
                            new, ts_old = [], t_s
                            for par2 in range(2):
                                r = slice(64 * par2, 64 * par2 + 64)
                                z_, f_ = SZ[r, par2:8:2, :], SF[r, :, :]
                                ps = banks.tiles[bs][r, 0:T].rearrange("p (f i) -> p f i", f=4)
                                if c == 0:
                                    t = dve(lambda e, z_=z_, ps=ps: e.tensor_copy(z_, ps), tok_s, ts_old)
                                else:
                                    t = dve(lambda e, z_=z_, ps=ps, f_=f_: e.tensor_tensor(z_, f_, ps, ALU.add), tok_s, ts_old, t_sf[par2])
                                new.append(t)
                                if c < 2:
                                    fb = FC[r, :, c + 1:c + 2].broadcast_to([64, 4, 64])
                                    t_sf[par2] = dve(lambda e, z_=z_, f_=f_, fb=fb: e.tensor_tensor(f_, z_, fb, ALU.mult), t, tp["F"])
                            t_s = new + [t_s0]
                            banks.done(bs, new)
                        for h in range(8):
                            tok = mm(half_of(by, h), Us[rows, hd(h)], RB[rows, h, tbk, :], False, h > 5, [t_u, tsc[0]] if h == 0 else None, sig=(h == 7))
                        y_ = banks.tiles[by]
                        t = act(lambda e, y_=y_, c=c: e.activation(Yo[:, :, 64 * c:64 * c + 64], y_[:, 0:T].rearrange("p (f i) -> p f i", f=4), ACT.Copy), tok)
                        banks.done(by, [t])
                        t_yo.append(t)
                        if c % 2:
                            run(after)
                            after = norm(c // 2, t_yo)
                    weave(after, filler, 1)
                    run(filler)

            with ExitStack() as s2:
                Z = sb(s2, [P, 15, T + 1])
                t_z0 = pool(lambda e: e.memset(Z[:, :, 0:1], 0.0))
                tz = [None] * 15
                gcol = np.concatenate([np.arange(1792, 1824), np.full(96, -1)])
                order = [12, 13, 14] + list(range(4, 8)) + list(range(0, 4)) + list(range(8, 12))
                zcols = (pieces(0, 1792) + [gcol])

                def evac_z(n, out, tok):
                    j = order[n]
                    zj, zp = Z[:, j, 1:T + 1], Z[:, j, 0:T]
                    t0 = act(lambda e: e.activation(zj, out, ACT.Copy), tok)
                    i = scr.get()
                    d = scr.tiles[i][:, :]
                    t = pool(lambda e: e.tensor_tensor(d, zp, zj, ALU.subtract), t0, t_z0, scr.free[i])
                    tz[j] = dve(lambda e: e.scalar_tensor_tensor(zj, d, par_col("ab_shift_mix_2", j), zj, ALU.mult, ALU.add), t)
                    scr.free[i] = tz[j]
                    return [t0]

                lora = sb(s2, [P, 3, 512])
                small3 = sb(s2, [P, 4, 4]), sb(s2, [P, 4, 4]), sb(s2, [P, 16])
                cM = sb(s2, [P, sum(w for _, w in atM.values())])
                t_l = pr.op("act", lambda e: e.dma_start(lora[:, :, :], dram["lora"]), None, sem="ld_l", step=16)
                t_cM = pr.op("act", lambda e: e.dma_start(cM[:, :], dram["cM"]), None, sem="ld_M", step=16)

                def CM(name):
                    o, w = atM[name]
                    return cM[:, o:o + w]

                S_ring = Ring([sb(s2, [P, 384]) for _ in range(3)])
                T_ring = Ring([sb(s2, [P, 384]) for _ in range(2)])
                small = mk_small(s2)
                Q, K, V = sb(s2, [P, 4, T]), sb(s2, [P, 4, T]), sb(s2, [P, 2, 512])
                turning = mk_turning(s2, CM("cos2"), CM("sin2"), CM("perm2"), t_cM)
                tqk, tv = [], []

                def place_qk(j):
                    return [(Q[:, j, :] if j < 4 else K[:, j - 4, :], 0, P)], -(128.0 ** -0.5) if j < 4 else 1.0, tqk, None

                cz = CM("causal")
                heads = []
                for h in range(4):
                    def qk(ps, free, h=h):
                        mm(ps[:, 0:P], Q[:, h, 0:P], K[:, h, 0:P], True, True, [free, tqk])
                        return mm(ps[:, P:P + T], Q[:, h, P:T], K[:, h, :], True, True, sig=True)
                    heads.append(head(qk=[qk], masks=[[cz[:, 0:P], cz[:, T:2 * T]]], widths=[P, T], deps=[t_cM], d=P,
                                      v=lambda kb, h=h: V[:, kb, P * h:P * h + P], vdeps=tv,
                                      out=(ym[:, h, :], ym[:, 4 + h, :], ytok)))

                zs = project("ab_w_in_2", 0, range(8), [zcols[j] for j in order], H, evac_z, together=True)
                for _ in range(7):
                    next(zs)
                filler = chain(zs, rotated("ab_w_in_2", 0, range(8), pieces(1824, 2848), H, turning, place_qk),
                               by_token("ab_w_in_2", 0, range(8), np.arange(2848, 3360), H, T, V, tv),
                               attention(heads, S_ring, T_ring, small))
                banks.assign(lin=[0, 1, 2, 3], att=[4, 5, 6])
                tp = {}
                weave(prep(Z, tz, lora, t_l, small3, tp), filler, 1)
                run(filler)
                banks.assign(lin=ALL, att=ALL)
            t_y = [[] for _ in range(4)]
            filler = residual("ab_w_out_2", 0, range(4, 8), Act2(ym[:, 0:4, :], ym[:, 4:8, :], ytok), ALPHA, per_unit=4)
            scan(tp, Hh, Hl, t_y, filler)
            sums = Sums(8, True)
            run(residual("ab_w_out_2", 0, range(4), Act2(Hh, Hl, t_y), 1.0, sums, per_unit=4))
            return sums

    def dilated(H):
        with ExitStack() as s1:
            cD = sb(s1, [P, sum(w for _, w in atD.values())])
            pr.fence(["act", "dve", "pool"])
            n_t = atD["dil0"][0]
            t_cDt = pr.op("act", lambda e: e.dma_start(cD[:, 0:n_t], dram["cD"][:, 0:n_t]), None, sem="ld_Dt", step=16)
            t_cD = pr.op("act", lambda e: e.dma_start(cD[:, n_t:], dram["cD"][:, n_t:]), None, sem="ld_D", step=16)

            def CD(name):
                o, w = atD[name]
                return cD[:, o:o + w]

            yh, yl = sb(s1, [P, 8, T], F32R), sb(s1, [P, 8, T], F32R)
            ytok = [[], []]
            S_ring = Ring([sb(s1, [P, 384]) for _ in range(9)])
            T_ring = Ring([sb(s1, [P, 384]) for _ in range(2)])
            small = mk_small(s1)
            turning = mk_turning(s1, CD("cos2"), CD("sin2"), CD("perm2"), t_cDt)
            sets = [(sb(s1, [P, 12, T]), sb(s1, [P, 4, T]), sb(s1, [P, 2, 512])) for _ in range(2)]

            tq, tv = [[] for _ in range(8)], [[], []]

            def qk_of(hg):
                Q, K, _ = sets[hg]
                tiles = [np.arange(D * g + P * h, D * g + P * h + P) for h in range(4 * hg, 4 * hg + 4) for g in range(4)]

                def place(j):
                    h, g = j // 4, j % 4
                    return [(Q[:, 3 * h + g, :] if g < 3 else K[:, h, :], 0, P)], -(128.0 ** -0.5) if g < 3 else 1.0, tq[4 * hg + h], None

                return rotated("c_w_in_2", 0, range(8), tiles, H, turning, place, together=(hg == 0))

            def v_of(hg):
                v0 = 4 * D + 512 * hg
                return by_token("c_w_in_2", 0, range(8), np.arange(v0, v0 + 512), H, T, sets[hg][2], tv[hg])

            heads = []
            for h8 in range(8):
                hg, h = h8 // 4, h8 % 4
                Q, K, V = sets[hg]

                def qk(ps, fr, g, Q=Q, K=K, h=h, t=tq[h8]):
                    mm(ps[:, 0:P], Q[:, 3 * h + g, 0:P], K[:, h, 0:P], True, True, [fr, t])
                    return mm(ps[:, P:P + T], Q[:, 3 * h + g, P:T], K[:, h, :], True, True, sig=True)
                heads.append(head(qk=[lambda ps, fr, g=g, qk=qk: qk(ps, fr, g) for g in range(3)],
                                  masks=[[CD(f"dil{g}")[:, 0:P], CD(f"dil{g}")[:, T:2 * T]] for g in range(3)], widths=[P, T],
                                  deps=[t_cD], d=P, v=lambda kb, h=h, V=V: V[:, kb, P * h:P * h + P], vdeps=tv[hg],
                                  out=(yh[:, h8, :], yl[:, h8, :], ytok[hg])))

            filler = chain(qk_of(0), v_of(0), v_of(1), qk_of(1))
            due = [7, 11, 15, 20, 27, 31, 35, 37]
            made = [0]

            def up_to(n):
                while made[0] < n:
                    next(filler, None)
                    made[0] += 1

            banks.assign(lin=SOME, att=ATT)
            up_to(due[0])
            Y = Act2(yh, yl, None)
            half_out = None
            for step, _ in enumerate(attention(heads, S_ring, T_ring, small, fine=True)):
                i, late = step // 2, step % 2
                if i < 7:
                    up_to(due[i + 1] if late else (due[i] + due[i + 1]) // 2)
                elif late:
                    if half_out is None:
                        Y.toks = ytok[0] + [None] * 4
                        half_out = residual("c_w_out_2", 0, range(4), Y, ALPHA, per_unit=4)
                    next(half_out, None)
                    next(half_out, None)
            run(half_out)
            banks.assign(lin=ALL, att=ALL)
            Y2 = Act2(yh, yl, [None] * 4 + ytok[1])
            sums = Sums(8, True)
            run(residual("c_w_out_2", 0, range(4, 8), Y2, 1.0, sums, per_unit=4, xk=[4, 5, 6, 7]))
            return sums

    with top:
        sums = Sums(8)
        for k in range(8):
            sums.add(X[:, k, :], t_x)
        W.first()
        for l in range(2):
            sums = mixer1(l, sums)
            sums = ffn1(l, sums)
        H = rms_split(X, 8, "final_g", sums, Hh, Hl, keep=X)
        sums = rwkv_moba(H)
        H = layer_norm(sums, "ln1_g_20", "ln1_b_20")
        sums = mlp2(0, H)
        H = layer_norm(sums, "ln2_g_20", "ln2_b_20")
        sums = dilated(H)
        H = layer_norm(sums, "ln1_g_21", "ln1_b_21")
        sums = mlp2(1, H)
        xt = layer_norm(sums, "ln2_g_21", "ln2_b_21", split=False)
        t_out = [pr.op("sp", lambda e, k=k: e.dma_start(dram["out"][:, k:k + 2, :], X[:, k:k + 2, :]), xt[k:k + 2], sem=f"st{k}", step=16)
                 for k in range(0, 8, 2)]
        pr.op("sp", None, t_out, sig=False)

        if specs is not None:
            assert W.specs == specs
            sems = {s: top.enter_context(nc.semaphore(f"s_{s}")) for s in sorted(pr.count)}
            block = top.enter_context(nc.Block())

            def play(e, name):
                for waits, fn, s, step in pr.q[name]:
                    for ws, wv in waits:
                        e.wait_ge(sems[ws], wv)
                    if fn is not None:
                        ins = fn(e)
                        if s is not None:
                            ins.then_inc(sems[s], step)

            block.sync(lambda e: play(e, "sp"))
            block.tensor(lambda e: play(e, "pe"))
            block.vector(lambda e: play(e, "dve"))
            block.scalar(lambda e: play(e, "act"))
            block.gpsimd(lambda e: play(e, "pool"))
    return W.specs


def lay_unit(inputs, spec):
    name, layer, rows, cols = spec
    a = inputs[name][layer]
    cols = np.array(cols)
    parts = []
    for k in rows:
        block = np.zeros((P, len(cols)), a.dtype)
        block[:, cols >= 0] = a[k * P:(k + 1) * P, cols[cols >= 0]]
        parts.append(block)
    return np.concatenate(parts, axis=1).reshape(-1)


def lay_params(inputs):
    cols = []
    for key, name, idx in param_list():
        v = inputs[name][idx].reshape(-1)
        w = -(-v.size // P)
        pad = np.zeros(w * P, v.dtype)
        pad[:v.size] = v
        cols.append(pad.reshape(w, P).T)
    for l in range(2):
        cols.append(np.broadcast_to(inputs["gqa_sink"][l][None, :], (P, 8)))
    return np.ascontiguousarray(np.concatenate(cols, axis=1))


def lay_bias(rpb):
    out = np.zeros((2, 64, 8, 7, 64), rpb.dtype)
    for c in range(64):
        k = np.arange(max(0, c - 15), min(64, c + 16))
        out[:, c, :, :, k] = np.moveaxis(rpb[:, :, 4:11, k - c + 15], 3, 0)
    return out


def kernel(**inputs):
    import concourse.bacc as bacc
    from concourse.bass_utils import run_bass_kernel_spmd as run

    inputs = {k: np.asarray(v) for k, v in inputs.items()}
    c = shape_constants()
    packs = [pack(n, c) for n in (CONST1, CONST_A, CONST_M, CONST_W, CONST_D)]
    atP = param_places()
    places = [p[0] for p in packs] + [atP]

    scratch = bacc.Bacc("TRN2", target_bir_lowering=False, num_devices=1)

    def tensors(nc, total):
        shapes = {"x": (P, 8, T), "c1": packs[0][1].shape, "cA": packs[1][1].shape, "cM": packs[2][1].shape,
                  "cW": packs[3][1].shape, "cD": packs[4][1].shape, "par": (P, atP[1]), "w": (total,),
                  "rpb": (2, 64, 8, 7, 64), "lora": (P, 3, 512)}
        d = {k: nc.dram_tensor(f"in_{k}", s, F32, kind="ExternalInput").ap() for k, s in shapes.items()}
        d["out"] = nc.dram_tensor("out_0", (P, 8, T), F32, kind="ExternalOutput").ap()
        return d

    specs = program(scratch, tensors(scratch, P), places, None, [])
    offsets, total = [], 0
    for _, _, rows, cols in specs:
        offsets.append(total)
        total += P * len(rows) * len(cols)
    nc = bacc.Bacc("TRN2", target_bir_lowering=False, num_devices=1)
    program(nc, tensors(nc, total), places, specs, offsets)

    lora = np.zeros((P, 3, 512), np.float32)
    lora[0:64, 0] = inputs["ab_w_up_2"][0]
    lora[64:128, 0] = inputs["ab_a_up_2"][0]
    lora[:, 1] = inputs["ab_g_up_2"][0][0:128]
    lora[0:32, 2] = inputs["ab_g_up_2"][0][128:160]
    feed = {"in_x": np.ascontiguousarray(inputs["x"][0].T.reshape(8, P, T).transpose(1, 0, 2)),
            "in_c1": packs[0][1], "in_cA": packs[1][1], "in_cM": packs[2][1], "in_cW": packs[3][1], "in_cD": packs[4][1],
            "in_par": lay_params(inputs), "in_rpb": lay_bias(inputs["na_rpb"]), "in_lora": lora,
            "in_w": np.concatenate([lay_unit(inputs, s) for s in specs])}
    got = run(nc, [feed], core_ids=[0]).results[0]["out_0"]
    return np.ascontiguousarray(got.transpose(1, 0, 2).reshape(D, T).T)[None]
```
